# Optimizing a Trainium2 kernel written in Bass

```python
import math
import jax, jax.numpy as jnp
from jax import lax
import numpy as np

D_MODEL = 1024
BATCH = 1
SEQ = 512
DEPTH = 1
DEC_BATCH = 8
DEC_SEQ = 1
PAST_LEN = 4096
PAGE_SIZE = 128

HG_HEADS = 8
HG_FDIM = 64
HG_IDIM = 64
HG_W = HG_HEADS * HG_FDIM
HG_IW = HG_HEADS * HG_IDIM
RET_HEADS = 4
RET_DK = 128
RET_DV = 128
RET_QW = RET_HEADS * RET_DK
RET_VW = RET_HEADS * RET_DV
D_FF = 2816
CONV_W = 3
PLE_DIM = 256
CHUNK = 64
ROPE_BASE = 10000.0
EPS = 1e-6
IN_SPLITS = (HG_W, HG_W, HG_IW, HG_IW, RET_QW, RET_QW, RET_VW, RET_VW, D_MODEL, D_MODEL)
IN_COLS = 2 * HG_W + 2 * HG_IW + 2 * RET_QW + 2 * RET_VW + 2 * D_MODEL

kernel_name = 'hybrid_hgrn2_retention_convffn_step'

def _rmsnorm(x, g):
    xf = x.astype(jnp.float32)
    xf = xf * lax.rsqrt(jnp.mean(xf * xf, axis=-1, keepdims=True) + EPS)
    return (xf * g.astype(jnp.float32)).astype(x.dtype)

def _head_rmsnorm(o, n_heads, g):
    b, l, w = o.shape
    oh = o.reshape(b, l, n_heads, w // n_heads)
    oh = oh * lax.rsqrt(jnp.mean(oh * oh, axis=-1, keepdims=True) + EPS)
    return oh.reshape(b, l, w) * g.astype(jnp.float32)

def _split_heads(t, n_heads):
    b, l, w = t.shape
    return t.reshape(b, l, n_heads, w // n_heads).transpose(0, 2, 1, 3)

def _merge_heads(t):
    b, h, l, d = t.shape
    return t.transpose(0, 2, 1, 3).reshape(b, l, h * d)

def _to_chunks(t, c):
    b, h, l, d = t.shape
    return t.reshape(b, h, l // c, c, d).transpose(2, 0, 1, 3, 4)

def _from_chunks(t):
    n, b, h, c, d = t.shape
    return t.transpose(1, 2, 0, 3, 4).reshape(b, h, n * c, d)

def _rotary(x, pos0):
    d = x.shape[-1]
    l = x.shape[-2]
    inv_freq = ROPE_BASE ** (-jnp.arange(0, d, 2, dtype=jnp.float32) / d)
    pos = pos0 + jnp.arange(l, dtype=jnp.float32)
    ang = pos[:, None] * inv_freq[None, :]
    cos, sin = jnp.cos(ang), jnp.sin(ang)
    x1, x2 = x[..., : d // 2], x[..., d // 2:]
    return jnp.concatenate([x1 * cos - x2 * sin, x1 * sin + x2 * cos], axis=-1)

def _hgrn2_chunked(q, k, log_f, v, s0):
    l = q.shape[2]
    c = math.gcd(l, CHUNK)
    causal = jnp.tril(jnp.ones((c, c), dtype=bool))[:, :, None]

    def step(s, xs):
        qc, kc, lfc, vc = xs
        cum = jnp.cumsum(lfc, axis=-2)
        o_inter = jnp.einsum('bhtk,bhkv->bhtv', qc * jnp.exp(cum), s)
        diff = cum[:, :, :, None, :] - cum[:, :, None, :, :]
        decay = jnp.where(causal, jnp.exp(jnp.minimum(diff, 0.0)), 0.0)
        scores = jnp.einsum('bhtsk,bhsk->bhts', qc[:, :, :, None, :] * decay, kc)
        o = o_inter + jnp.einsum('bhts,bhsv->bhtv', scores, vc)
        last = cum[:, :, -1:, :]
        s_new = (jnp.exp(last[:, :, 0, :])[..., None] * s
                 + jnp.einsum('bhsk,bhsv->bhkv', kc * jnp.exp(last - cum), vc))
        return s_new, o

    s_fin, o = lax.scan(step, s0, (_to_chunks(q, c), _to_chunks(k, c),
                                   _to_chunks(log_f, c), _to_chunks(v, c)))
    return _from_chunks(o), s_fin

def _retention_chunked(q, k, v, log_gamma, r0):
    l = q.shape[2]
    c = math.gcd(l, CHUNK)
    t = jnp.arange(c, dtype=jnp.float32)
    delta = t[:, None] - t[None, :]
    decay = jnp.where(delta >= 0, jnp.exp(jnp.maximum(delta, 0.0) * log_gamma[:, None, None]), 0.0)
    q_decay = jnp.exp((t + 1.0)[None, :] * log_gamma[:, None])[:, :, None]
    k_decay = jnp.exp((c - 1.0 - t)[None, :] * log_gamma[:, None])[:, :, None]
    chunk_decay = jnp.exp(c * log_gamma)[:, None, None]

    def step(r, xs):
        qc, kc, vc = xs
        scores = jnp.einsum('bhtd,bhsd->bhts', qc, kc) * decay
        o = (jnp.einsum('bhts,bhsv->bhtv', scores, vc)
             + jnp.einsum('bhtd,bhdv->bhtv', qc * q_decay, r))
        r_new = chunk_decay * r + jnp.einsum('bhsd,bhsv->bhdv', kc * k_decay, vc)
        return r_new, o

    r_fin, o = lax.scan(step, r0, (_to_chunks(q, c), _to_chunks(k, c), _to_chunks(v, c)))
    return _from_chunks(o), r_fin

def _layer(h, p, s_hg0, s_ret0, conv0, pos0, log_gamma, lb,
           w_in, g_mix, g_hg_out, g_ret_out, w_br_hg, w_br_ret, w_out,
           g_ffn, w_up, conv_w, conv_b, w_down, g_ple, w_ple, w_ple_gate):
    f32 = jnp.float32
    l = h.shape[1]
    xn = _rmsnorm(h, g_mix)
    u = xn @ w_in
    split_idx = np.cumsum(IN_SPLITS)[:-1].tolist()
    hq, hf, hi, hg, rq, rk, rv, rg, ga, gb = jnp.split(u, split_idx, axis=-1)

    f = lb + (1.0 - lb) * jax.nn.sigmoid(hf.astype(f32))
    o_hg, s_hg = _hgrn2_chunked(
        _split_heads(jax.nn.silu(hq.astype(f32)), HG_HEADS),
        _split_heads(1.0 - f, HG_HEADS),
        _split_heads(jnp.log(f), HG_HEADS),
        _split_heads(hi.astype(f32), HG_HEADS),
        s_hg0.astype(f32))
    a_hg = _head_rmsnorm(_merge_heads(o_hg), HG_HEADS, g_hg_out) * jax.nn.silu(hg.astype(f32))
    y_hg = a_hg.astype(h.dtype) @ w_br_hg

    q_r = _rotary(_split_heads(rq.astype(f32), RET_HEADS), pos0)
    k_r = _rotary(_split_heads(rk.astype(f32), RET_HEADS), pos0) * (RET_DK ** -0.5)
    o_r, s_ret = _retention_chunked(q_r, k_r, _split_heads(rv.astype(f32), RET_HEADS),
                                    log_gamma, s_ret0.astype(f32))
    a_r = _head_rmsnorm(_merge_heads(o_r), RET_HEADS, g_ret_out) * jax.nn.silu(rg.astype(f32))
    y_ret = a_r.astype(h.dtype) @ w_br_ret

    mixed = jax.nn.sigmoid(ga) * y_hg + jax.nn.sigmoid(gb) * y_ret
    h = h + mixed @ w_out

    xn = _rmsnorm(h, g_ffn)
    a, g = jnp.split(xn @ w_up, 2, axis=-1)
    padded = jnp.concatenate([conv0.astype(a.dtype), a], axis=1)
    ac = conv_b + sum(padded[:, j:j + l, :] * conv_w[j] for j in range(CONV_W))
    conv_new = padded[:, -(CONV_W - 1):, :]
    h = h + (jax.nn.gelu(ac) * g) @ w_down

    gate = jax.nn.sigmoid(_rmsnorm(h, g_ple) @ w_ple_gate)
    h = h + gate * (p @ w_ple)
    return h, s_hg, s_ret, conv_new

def setup_inputs(seed: int = 0) -> dict:
    key = jax.random.key(seed)
    ks = jax.random.split(key, 24)

    def nrm(k, shape, scale):
        return jax.random.normal(k, shape, jnp.float32) * scale

    def gain(k, shape):
        return 1.0 + 0.05 * jax.random.normal(k, shape, jnp.float32)

    return {
        'x_prompt': nrm(ks[0], (BATCH, SEQ, D_MODEL), 1.0),
        'x_sample': nrm(ks[1], (DEC_BATCH, DEC_SEQ, D_MODEL), 1.0),
        'state_hgrn': nrm(ks[2], (DEPTH, DEC_BATCH, HG_HEADS, HG_FDIM, HG_IDIM), 0.5),
        'state_ret': nrm(ks[3], (DEPTH, DEC_BATCH, RET_HEADS, RET_DK, RET_DV), 1.0),
        'state_conv': nrm(ks[4], (DEPTH, DEC_BATCH, CONV_W - 1, D_FF), 1.0),
        'p_prompt': nrm(ks[5], (DEPTH, BATCH, SEQ, PLE_DIM), 1.0),
        'p_sample': nrm(ks[6], (DEPTH, DEC_BATCH, DEC_SEQ, PLE_DIM), 1.0),
        'lb_logits': nrm(ks[7], (DEPTH + 1, HG_W), 0.5),
        'w_in': nrm(ks[8], (DEPTH, D_MODEL, IN_COLS), D_MODEL ** -0.5),
        'g_mix': gain(ks[9], (DEPTH, D_MODEL)),
        'g_hg_out': gain(ks[10], (DEPTH, HG_IW)),
        'g_ret_out': gain(ks[11], (DEPTH, RET_VW)),
        'w_br_hg': nrm(ks[12], (DEPTH, HG_IW, D_MODEL), HG_IW ** -0.5),
        'w_br_ret': nrm(ks[13], (DEPTH, RET_VW, D_MODEL), RET_VW ** -0.5),
        'w_out': nrm(ks[14], (DEPTH, D_MODEL, D_MODEL), D_MODEL ** -0.5),
        'g_ffn': gain(ks[15], (DEPTH, D_MODEL)),
        'w_up': nrm(ks[16], (DEPTH, D_MODEL, 2 * D_FF), D_MODEL ** -0.5),
        'conv_w': nrm(ks[17], (DEPTH, CONV_W, D_FF), CONV_W ** -0.5),
        'conv_b': nrm(ks[18], (DEPTH, D_FF), 0.01),
        'w_down': nrm(ks[19], (DEPTH, D_FF, D_MODEL), D_FF ** -0.5),
        'g_ple': gain(ks[20], (DEPTH, D_MODEL)),
        'w_ple': nrm(ks[21], (DEPTH, PLE_DIM, D_MODEL), PLE_DIM ** -0.5),
        'w_ple_gate': nrm(ks[22], (DEPTH, D_MODEL, D_MODEL), D_MODEL ** -0.5),
        'g_final': gain(ks[23], (D_MODEL,)),
    }

def reference(x_prompt, x_sample, state_hgrn, state_ret, state_conv, p_prompt, p_sample,
              lb_logits, w_in, g_mix, g_hg_out, g_ret_out, w_br_hg, w_br_ret, w_out,
              g_ffn, w_up, conv_w, conv_b, w_down, g_ple, w_ple, w_ple_gate, g_final):
    f32 = jnp.float32
    log_gamma = jnp.log1p(-jnp.exp2(-5.0 - jnp.arange(RET_HEADS, dtype=f32)))
    lb_all = jnp.cumsum(jax.nn.softmax(lb_logits.astype(f32), axis=0), axis=0)

    hp, hs = x_prompt, x_sample
    bp = x_prompt.shape[0]
    hg_p, ret_p, cv_p, hg_s, ret_s, cv_s = [], [], [], [], [], []
    for i in range(DEPTH):
        lw = (log_gamma, lb_all[i], w_in[i], g_mix[i], g_hg_out[i], g_ret_out[i],
              w_br_hg[i], w_br_ret[i], w_out[i], g_ffn[i], w_up[i], conv_w[i], conv_b[i],
              w_down[i], g_ple[i], w_ple[i], w_ple_gate[i])
        hp, s1, s2, s3 = _layer(
            hp, p_prompt[i],
            jnp.zeros((bp, HG_HEADS, HG_FDIM, HG_IDIM), f32),
            jnp.zeros((bp, RET_HEADS, RET_DK, RET_DV), f32),
            jnp.zeros((bp, CONV_W - 1, D_FF), hp.dtype),
            0, *lw)
        hg_p.append(s1); ret_p.append(s2); cv_p.append(s3)
        hs, s1, s2, s3 = _layer(
            hs, p_sample[i], state_hgrn[i], state_ret[i], state_conv[i],
            PAST_LEN, *lw)
        hg_s.append(s1); ret_s.append(s2); cv_s.append(s3)

    y_prompt = _rmsnorm(hp, g_final)
    y_sample = _rmsnorm(hs, g_final)
    return (y_prompt, y_sample,
            jnp.stack(hg_p, axis=0), jnp.stack(ret_p, axis=0), jnp.stack(cv_p, axis=0),
            jnp.stack(hg_s, axis=0), jnp.stack(ret_s, axis=0), jnp.stack(cv_s, axis=0))


_drawn_inputs = setup_inputs


def setup_inputs(seed=0):
    import zlib

    import numpy as np

    out = dict(_drawn_inputs(seed))
    spreads = {}
    factors = {'g_hg_out': 3.11, 'g_ret_out': 3.579, 'conv_b': 8.0, 'g_ple': 26.488}
    for name, (base, spread) in spreads.items():
        noise = np.random.default_rng([zlib.crc32(name.encode()), seed]).standard_normal(out[name].shape)
        drawn = base * np.exp(spread * noise) if base else spread * noise
        out[name] = __import__('jax').numpy.asarray(drawn.astype(out[name].dtype))
    for name, factor in factors.items():
        out[name] = (out[name] * factor).astype(out[name].dtype)
    return out
```

```python
import concourse.bass as bass
from concourse import mybir
from contextlib import ExitStack

NT = 512
NS = 8
TT = NT + NS
HT = TT // 2
DM = 1024
DC = DM // 128
CH = 128
NCH = NT // CH
LV = 7
FF = 2816
FC = FF // 128
PD = 256
EPS = 1e-6
WMAX = FC // 2 * 128

SEC = dict(A=(0, 0, 2), B=(16, 16, 18), C=(32, 32, 34), D=(48, 48, 50), E=(56, 64, 66),
           F=(64, 72, 74), G=(108, 116, 118), H=(124, 132, 126))
SIZE = dict(A=1024, B=1024, C=1024, D=1024, E=1024, F=1024, G=WMAX, H=1280)
M_A, M_B, M_S, M_C, M_R, M_F, M_G = 3, 11, 43, 44, 60, 61, 62
L_C, L_F = 16, 32
L_TOTAL = L_F
MERGES = 15


class Steps:

    def __init__(self, eng, sem, after=None):
        self.eng, self.sem, self.base, self.k, self.it, self.per = eng, sem, 0, 0, 0, 0
        self.after = after

    def loop(self, it, per):
        self.base, self.k, self.it, self.per = self.base + self.k, 0, it, per

    def end(self, rounds):
        assert self.k == self.per, (self.k, self.per)
        self.base, self.k, self.it, self.per = self.base + rounds * self.per, 0, 0, 0

    def __call__(self, ins):
        ins.then_inc(self.sem, 1)
        self.k += 1
        self.eng.wait_ge(self.sem, self.it * self.per + (self.base + self.k))
        if self.after:
            self.after()


def hybrid_layer(nc, x_prompt, x_sample, state_hgrn, state_ret, state_conv, p_prompt, p_sample,
                 lb_logits, w_in, g_mix, g_hg_out, g_ret_out, w_br_hg, w_br_ret, w_out, g_ffn, w_up,
                 conv_w, conv_b, w_down, g_ple, w_ple, w_ple_gate, g_final, consts, masks,
                 y_prompt, y_sample, hg_prompt, ret_prompt, conv_prompt, hg_sample, ret_sample,
                 conv_sample, offs):
    fp, fr, u32 = mybir.dt.float32, mybir.dt.float32r, mybir.dt.uint32
    ALU, ACT = mybir.AluOpType, mybir.ActivationFunctionType
    MUL, ADD, SUB = ALU.mult, ALU.add, ALU.subtract
    KSCALE = float(128 ** -0.5)

    def tiles(w):
        return w[0].rearrange("(c p) (t n) -> p c t n", p=128, n=128)

    win_v, wbh_v, wbr_v, wout_v = tiles(w_in), tiles(w_br_hg), tiles(w_br_ret), tiles(w_out)
    wup_v, wdn_v, wpl_v, wpg_v = tiles(w_up), tiles(w_down), tiles(w_ple), tiles(w_ple_gate)
    COL = {n: i for n, i in zip(("hq", "hf", "hi", "hg", "rq", "rk", "rv", "rg"), range(0, 32, 4))}
    COL.update(ga=32, gb=40)
    xt_dram = nc.dram_tensor("x_transposed", [128, DC, TT], fp).ap()

    base = (nc.sbuf_base + 31) // 32 * 32

    def at(name, shape, off, dt=fp):
        size = 4
        for n in shape[1:]:
            size *= n
        assert off + size <= 212832, (name, off + size)
        return nc.alloc_sbuf_tensor_at(name, shape, dt, offset=base + off)

    class Region:
        def __init__(self, start, stop):
            self.at, self.stop = start, stop

        def __call__(self, name, shape, dt=fp):
            size = 4
            for n in shape[1:]:
                size *= n
            t = at(name, shape, self.at, dt)
            self.at += (size + 31) // 32 * 32
            assert self.at <= self.stop, (name, self.at, self.stop)
            return t

    r = Region(0, 33792)
    raw = [r(f"raw{i}", [128, WMAX]) for i in range(2)]
    whi = [r(f"whi{i}", [128, WMAX], fr) for i in range(2)]
    wlo = [r(f"wlo{i}", [128, WMAX], fr) for i in range(2)]
    r = Region(33792, 49152)
    NCST = consts.shape[1]
    cst = r("cst", [128, NCST])
    msk = r("msk", [128, LV * 64], u32)
    ones128 = r("ones128", [128, 128])
    ones1024 = r("ones1024", [128, 128])
    vc = r("vc", [128, 136])
    lbt = r("lbt", [128, 6, 4])
    eps = r("eps", [128, 1])
    ssx = r("ssx", [128, 8])
    ot = r("ot", [128, 512])
    ident = cst[:, offs["ident"]:offs["ident"] + 128]
    blk64 = cst[:, offs["blk64"]:offs["blk64"] + 128]
    headsel = cst[:, offs["headsel"]:offs["headsel"] + 2]
    cosT = cst[:, offs["cos"]:offs["cos"] + TT]
    sinT = cst[:, offs["sin"]:offs["sin"] + TT]
    decay = cst[:, offs["decay"]:offs["decay"] + 512]
    qdec = cst[:, offs["qdec"]:offs["qdec"] + 512]
    kdec = cst[:, offs["kdec"]:offs["kdec"] + 4]
    g128 = cst[:, offs["g128"]:offs["g128"] + 4]
    gam = cst[:, offs["gam"]:offs["gam"] + 4]
    r = Region(49152, 49152 + 33280)
    xah = r("xah", [128, DC, TT], fr)
    xal = r("xal", [128, DC, TT], fr)
    XA_END = 82432
    r = Region(XA_END, 212832)
    G0 = r.at
    fT = r("fT", [128, 4, TT])
    lq = [r(f"lq{i}", [128, 4, CH]) for i in range(4)]
    lk = [r(f"lk{i}", [128, 4, CH]) for i in range(4)]
    qk = r("qk", [128, 4, CH])
    sfull = r("sfull", [128, 8, CH])
    khat = r("khat", [128, 512])
    r.at = G1 = G0 + 2 * DC * TT * 4
    qT = r("qT", [128, 4, TT])
    qr = r("qr", [128, 4, TT])
    AH0 = r.at
    vhg = r("vhg", [128, NCH, 512])
    v8h = r("v8h", [NS, 512])
    ghg = r("ghg", [128, 4, TT])
    AR0 = r.at
    kr = r("kr", [128, 4, TT])
    vr = r("vr", [128, NCH, 512])
    v8r = r("v8r", [NS, 512])
    grt = r("grt", [128, 4, TT])
    vst = r("vst", [128, 512])
    tl = [r(f"tl{i}", [128, 4, CH >> i]) for i in range(LV + 1)]
    sst = r("sst", [128, 4, 64])
    sq = r("sq", [128, 512])
    rs = r("rs", [128, 512])
    vblk = r("vblk", [NS, 1024])
    k8 = r("k8", [NS, 128])
    fs8 = r("fs8", [128, 8])
    ks8 = r("ks8", [128, 8])
    qs8 = r("qs8", [128, 8])
    sqs = r("sqs", [128, 32])
    rss = r("rss", [128, 32])
    T0 = r.at
    xs = [r(f"xs{i}", [128, TT]) for i in range(2)]
    hiT = r("hiT", [128, TT])
    sg = [r(f"sg{i}", [128, TT]) for i in range(2)]
    r = Region(T0, r.at)
    kst = r("kst", [128, 4, CH])
    qst = r("qst", [128, 4, CH])
    qd = r("qd", [128, 4, CH])
    prb = r("prb", [128, 4, CH])
    r = Region(T0 + 10400, 212832)
    ktk = at("ktk", [128, 512], r.at)
    sgf = r("sgf", [128, TT])
    rst = r("rst", [128, 4, 128])
    ss = at("ss", [128, 8, 64], r.at)
    rsm = r("rsm", [128, 8, 128])
    r = Region(G0, 212832)
    xtok = r("xtok", [128, 5, DM])
    xsc = r("xsc", [128, 5, DM])
    vrow = r("vrow", [128, 2, 128])
    xstg = at("xstg", [128, DC, TT], AR0)
    xsm = at("xsm", [128, DC, NS], AR0 + 16640 + 2048)
    gab = at("gab", [128, 2 * DC, TT], G0)
    assert G0 + 16 * TT * 4 <= G1
    r = Region(AH0, AR0)
    ahh = r("ahh", [128, 4, TT], fr)
    ahl = r("ahl", [128, 4, TT], fr)
    r = Region(AR0, AR0 + 16640)
    arh = r("arh", [128, 4, TT], fr)
    arl = r("arl", [128, 4, TT], fr)
    A0, B0, H0 = 49152, 49152 + 91520, 49152 + 91520 + 33280
    r = Region(A0, B0)
    ach = r("ach", [128, FC, TT], fr)
    acl = r("acl", [128, FC, TT], fr)
    r = Region(B0, H0)
    xbh = r("xbh", [128, DC, TT], fr)
    xbl = r("xbl", [128, DC, TT], fr)
    r = Region(H0, 212832)
    hT = r("hT", [128, DC, TT])
    m1 = r("m1", [128, TT])
    m2 = r("m2", [128, TT])
    sqt = r("sqt", [128, TT])
    ssq = r("ssq", [128, TT])
    rstd = r("rstd", [128, TT])
    F0 = r.at
    ab = [r(f"ab{i}", [128, TT + 2]) for i in range(2)]
    cv = r("cv", [128, TT])
    gg = r("gg", [128, TT])
    part = r("part", [128, FC, NS])
    cs = at("cs", [128, FC, 10], H0 + 16640)
    stT = at("stT", [128, FC, 16], A0 + 40000)
    strow = at("strow", [16, FF], A0 + 48000)
    csr = at("csr", [10, FF], F0)
    r = Region(A0, B0)
    ptok = at("ptok", [128, 5, PD], F0)
    pxh = r("pxh", [128, 2, TT], fr)
    pxl = r("pxl", [128, 2, TT], fr)
    tg = r("tg", [128, TT])
    sgg = r("sgg", [128, TT])
    tp = r("tp", [128, TT])
    yT = r("yT", [128, DC, TT])
    ytok = r("ytok", [128, 5, DM])
    rt = r("rt", [128, 5])

    ctx = ExitStack()
    with ctx:
        def sem(name):
            return ctx.enter_context(nc.semaphore(name))

        acc = [ctx.enter_context(nc.psum_tensor(f"acc{i}", [128, 2, 512], fp)) for i in range(2)]
        lvb = ctx.enter_context(nc.psum_tensor("lvb", [128, 2, 512], fp))
        ob = ctx.enter_context(nc.psum_tensor("ob", [128, 512], fp))
        mb = ctx.enter_context(nc.psum_tensor("mb", [128, 512], fp))

        raw_loaded = [sem(f"raw_loaded{i}") for i in range(2)]
        hi_ready = sem("hi_ready")
        lo_ready = sem("lo_ready")
        part_done = sem("part_done")
        acc_free = [sem(f"acc_free{i}") for i in range(2)]
        lv_full = sem("lv_full")
        sc_full = sem("sc_full")
        merged = sem("merged")
        lv_free = [sem(f"lv_free{i}") for i in range(2)]
        misc_full = sem("misc_full")
        misc_free = sem("misc_free")
        const_loaded = sem("const_loaded")
        vec_loaded = sem("vec_loaded")
        x_loaded = sem("x_loaded")
        set_up = sem("set_up")
        x_sq = sem("x_sq")
        x_scaled = sem("x_scaled")
        xa_hi = sem("xa_hi")
        xa_lo = sem("xa_lo")
        vec_ready = sem("vec_ready")
        lb_exp = sem("lb_exp")
        xt_copied = sem("xt_copied")
        xt_stored = sem("xt_stored")
        sig_ready = sem("sig_ready")
        f_done = sem("f_done")
        swapped = sem("swapped")
        rot_done = sem("rot_done")
        prep = sem("prep")
        o_ready = sem("o_ready")
        staged = sem("staged")
        vst_ready = sem("vst_ready")
        sq_ready = sem("sq_ready")
        o_free = sem("o_free")
        a_done = sem("a_done")
        ss_loaded = sem("ss_loaded")
        ss_stored = sem("ss_stored")
        rsm_loaded = sem("rsm_loaded")
        rsm_stored = sem("rsm_stored")
        ret_o = sem("ret_o")
        smp_sq = sem("smp_sq")
        smp_done = sem("smp_done")
        ah_hi = sem("ah_hi")
        ah_lo = sem("ah_lo")
        h_loaded = sem("h_loaded")
        mix_sum = sem("mix_sum")
        mix_hi = sem("mix_hi")
        mix_lo = sem("mix_lo")
        h_new = sem("h_new")
        xb_hi = sem("xb_hi")
        xb_lo = sem("xb_lo")
        ssq_ready = sem("ssq_ready")
        rstd_ready = sem("rstd_ready")
        st_loaded = sem("st_loaded")
        c_first = sem("c_first")
        c_ready = sem("c_ready")
        gelu_ready = sem("gelu_ready")
        act_ready = sem("act_ready")
        ac_hi = sem("ac_hi")
        ac_lo = sem("ac_lo")
        cs_ready = sem("cs_ready")
        p_loaded = sem("p_loaded")
        p_hi = sem("p_hi")
        y_ready = sem("y_ready")
        rt_ready = sem("rt_ready")
        stored = sem("stored")
        pe_s, act_s, dve_s, pool_s = (sem(n) for n in ("pe_step", "act_step", "dve_step", "pool_step"))
        pe_passed, act_passed, dve_passed, pool_passed = (
            sem(n) for n in ("pe_passed", "act_passed", "dve_passed", "pool_passed"))

        def unit(sec, k, it):
            return it * 4 + (SEC[sec][0] + k)

        def parts(sec, k, it, per=4):
            return it * per + (SEC[sec][1] + k)

        def tidx(sec, k, it, per=4):
            return it * (per // 2) + (SEC[sec][2] + k) // 2

        def two(ap):
            return ap.rearrange("p (a b) -> p a b", a=2)

        def ps2(t, lo=0, hi=128):
            return acc[t % 2][lo:hi, :, 0:HT]

        def m4(ap):
            return ap.rearrange("p (a b) -> p a b", a=4)

        block = ctx.enter_context(nc.Block())


        @block.sync
        def _(sp):
            xp = x_prompt[0].rearrange("(i p) n -> p i n", p=128)
            for i in range(NCH):
                sp.dma_start(xtok[:, i, :], xp[:, i, :]).then_inc(x_loaded, 16)
            sp.dma_start(xtok[0:NS, 4, :], x_sample[:, 0, :]).then_inc(x_loaded, 16)

            def load(sec, k, it, srcs):
                u = unit(sec, k, it)
                sp.wait_ge(lo_ready, u + 1)
                if len(srcs) == 1:
                    n = (srcs[0].shape[1] + 1) // 2
                    srcs = [srcs[0][:, 0:n], srcs[0][:, n:]]
                at0 = 0
                for src in srcs:
                    n = src.shape[1]
                    dst = raw[k % 2][:, at0 * 128:(at0 + n) * 128].rearrange("p (c n) -> p c n", n=128)
                    sp.dma_start(dst, src).then_inc(raw_loaded[k % 2], 16)
                    at0 += n

            with sp.Fori(0, 4) as it:
                for k, n in enumerate(("hq", "hf", "hi", "hg")):
                    load("A", k, it, [win_v[:, :, it + COL[n], :]])
            sp.wait_ge(xt_copied, 9)
            sp.dma_start(xt_dram, xstg[:]).then_inc(xt_stored, 16)
            with sp.Fori(0, 4) as it:
                for k, n in enumerate(("rq", "rk", "rv", "rg")):
                    load("B", k, it, [win_v[:, :, it + COL[n], :]])
            with sp.Fori(0, 4) as it:
                for k in range(4):
                    load("C", k, it, [win_v[:, :, it * 2 + (COL["ga" if k % 2 == 0 else "gb"] + k // 2), :]])
            with sp.Fori(0, 2) as it:
                for k in range(4):
                    load("D", k, it, [wbh_v[:, :, it * 4 + k, :], wbr_v[:, :, it * 4 + k, :]])
            with sp.Fori(0, 2) as it:
                for k in range(4):
                    load("E", k, it, [wout_v[:, :, it * 4 + k, :]])
            with sp.Fori(0, 11) as it:
                for k in range(4):
                    load("F", k, it, [wup_v[:, :, it * 2 + (k // 2 + (0 if k % 2 == 0 else FC)), :]])
            with sp.Fori(0, 4) as it:
                for k in range(4):
                    load("G", k, it, [wdn_v[:, FC // 2 * (k % 2):FC // 2 * (k % 2 + 1), it * 2 + k // 2, :]])
            sp.wait_ge(misc_free, M_G + 6)
            sp.dma_start(conv_prompt[0, 0], csr[0:2, :]).then_inc(stored, 16)
            sp.dma_start(conv_sample[0, :, 1, :], csr[2:10, :]).then_inc(stored, 16)
            sp.dma_start(conv_sample[0, :, 0, :], state_conv[0, :, 1, :]).then_inc(stored, 16)
            sp.wait_ge(stored, 96)
            sp.dma_start(ptok[:, 0:NCH, :], p_prompt[0, 0].rearrange("(i p) n -> p i n", p=128)).then_inc(p_loaded, 16)
            sp.dma_start(ptok[0:NS, 4, :], p_sample[0, :, 0, :]).then_inc(p_loaded, 16)
            with sp.Fori(0, 2) as it:
                for k in range(4):
                    load("H", k, it, [wpg_v[:, :, it * 4 + k, :], wpl_v[:, :, it * 4 + k, :]])
            yp = y_prompt[0].rearrange("(i p) n -> p i n", p=128)
            for i in range(NCH):
                for b in range(2):
                    sp.wait_ge(lv_free[b], L_F // 2 + 3 + i)
                sp.dma_start(yp[:, i, :], ytok[:, i, :]).then_inc(stored, 16)
            for b in range(2):
                sp.wait_ge(lv_free[b], L_F // 2 + 7)
            sp.dma_start(y_sample[:, 0, :], ytok[0:NS, 4, :]).then_inc(stored, 16)
            sp.wait_ge(xt_stored, 16)
            sp.wait_ge(ss_stored, 80)
            sp.wait_ge(rsm_stored, 80)
            sp.wait_ge(stored, 16 * 11)

        @block.tensor
        def _(pe):
            def taken():
                pe.sem_inc(pe_passed, 1)

            step = Steps(pe, pe_s, taken)

            def level(n):
                return lvb[:, n % 2, :]

            def wait_level(base, k, it, per):
                pe.wait_ge(lv_free[k % 2], it * (per // 2) + (base + k) // 2)

            def wait_misc(base, k, it, per):
                pe.wait_ge(misc_free, it * per + (base + k))

            def product(sec, k, it, slot, tile, chunks, w0, xh, xl, first=True, last=True, tper=4,
                        wait_unit=True, chunk_wait=None):
                if wait_unit:
                    pe.wait_ge(hi_ready, unit(sec, k, it) + 1)
                    pe.wait_ge(lo_ready, unit(sec, k, it) + 3)
                if first:
                    pe.wait_ge(acc_free[tile % 2], tidx(sec, tile, it, tper))
                n = len(chunks)
                for i, c in enumerate(chunks):
                    if chunk_wait:
                        chunk_wait(c)
                    w = slice((w0 + i) * 128, (w0 + i + 1) * 128)
                    for q, (wt, xx) in enumerate(((whi, xh), (whi, xl), (wlo, xh))):
                        for b in range(2):
                            mm = pe.matmul(acc[tile % 2][:, b, 0:HT], wt[slot][:, w],
                                           xx[:, c, b * HT:(b + 1) * HT],
                                           start=first and i == 0 and q == 0,
                                           stop=last and i == n - 1 and q == 2)
                if last or len(chunks) > 4:
                    mm.then_inc(part_done, 1)

            C8 = range(DC)
            pe.wait_ge(const_loaded, 32)
            pe.wait_ge(vec_loaded, 16 * 12)
            pe.transpose(mb[:, 0:48], vrow[0:48, 0, :], ident[0:48, 0:48])
            pe.transpose(mb[:, 48:136], vrow[0:88, 1, :], ident[0:88, 0:88]).then_inc(misc_full, 1)
            pe.wait_ge(x_loaded, 80)
            pe.wait_ge(misc_free, 1)
            for j in range(DC):
                mm = pe.transpose(mb[:, j * 8:j * 8 + 8], xtok[0:NS, 4, j * 128:(j + 1) * 128],
                                  ident[0:NS, 0:NS])
            mm.then_inc(misc_full, 1)
            pe.wait_ge(x_scaled, 5)
            pe.wait_ge(misc_free, 2)
            for j in range(DC):
                mm = pe.transpose(mb[:, j * 8:j * 8 + 8], xsc[0:NS, 4, j * 128:(j + 1) * 128],
                                  ident[0:NS, 0:NS])
            mm.then_inc(misc_full, 1)
            for n in range(2 * DC):
                j, src = n % DC, xsc if n < DC else xtok
                pe.wait_ge(lv_free[n % 2], n // 2)
                for i in range(NCH):
                    mm = pe.transpose(level(n)[:, i * 128:(i + 1) * 128],
                                      src[:, i, j * 128:(j + 1) * 128], ident)
                mm.then_inc(lv_full, 1)
            pe.wait_ge(xa_lo, 1)

            def v_transposes(base, k, it, per):
                wait_misc(base, k, it, per)
                for i in range(NCH):
                    mm = pe.transpose(mb[:, i * 128:(i + 1) * 128], hiT[:, i * 128:(i + 1) * 128], ident)
                mm.then_inc(misc_full, 1)
                wait_misc(base, k + 1, it, per)
                pe.transpose(mb[0:NS, 0:128], hiT[:, NT:TT], ident).then_inc(misc_full, 1)

            with pe.Fori(0, 4) as it:
                for k in range(4):
                    product("A", k, it, k % 2, k, C8, 0, xah, xal)
                pe.wait_ge(acc_free[0], it * 2 + (SEC["A"][2] + 2) // 2 + 1)
                v_transposes(M_A, 0, it, 2)

            def head(t, h, cols=slice(None)):
                return t[64 * (h % 2):64 * (h % 2) + 64, h // 2, cols]

            def scores(use, it):
                levels = [l for l in (2 * use, 2 * use + 1) if l < LV]
                pe.wait_ge(prep, it * 8 + levels[-1] + 1)
                pe.wait_ge(merged, it * MERGES + (4 * use + 1))
                taken()
                if use == 3:
                    for c in range(4):
                        pe.matmul(lvb[:, 0, 256 + 2 * c:258 + 2 * c], qk[:, c, :], headsel,
                                  start=True, stop=True)
                for l in levels:
                    hb = 1 << l
                    for h in range(8):
                        q2 = head(lq[l % 4], h).rearrange("k (b two h) -> k b two h", two=2, h=hb)[:, :, 1, :]
                        c0 = 256 * (l % 2) + 64 * (h // 2)
                        out = lvb[:, h % 2, c0:c0 + 64].rearrange("s (b h) -> s b h", h=hb)
                        mm = pe.matmul(out, head(lk[l % 4], h), q2, start=True, stop=True)
                mm.then_inc(sc_full, 1)

            def halves(k, it, between):
                product("B", k, it, k % 2, k, range(4), 0, xah, xal, last=False)
                between()
                product("B", k, it, k % 2, k, range(4, 8), 4, xah, xal, first=False, wait_unit=False)

            with pe.Fori(0, 4) as it:
                step.loop(it, 1)
                halves(0, it, lambda: scores(0, it))
                scores(1, it)
                pe.wait_ge(staged, it + 1)
                wait_misc(M_B, 0, it, 8)
                pe.transpose(mb[0:NS, 0:128], ks8[:], ident).then_inc(misc_full, 1)

                halves(1, it, lambda: scores(2, it))
                scores(3, it)
                pe.wait_ge(prep, it * 8 + 8)
                wait_misc(M_B, 1, it, 8)
                for c in range(4):
                    mm = pe.transpose(mb[:, c * 128:(c + 1) * 128], lk[3][:, c, :], ident)
                mm.then_inc(misc_full, 1)

                def sample_outer():
                    wait_misc(M_B, 2, it, 8)
                    taken()
                    for h2 in range(2):
                        mm = pe.matmul(mb[64 * h2:64 * h2 + 64, :], k8[:, 64 * h2:64 * h2 + 64],
                                       vblk[:, 512 * h2:512 * h2 + 512], start=True, stop=True)
                    mm.then_inc(misc_full, 1)

                halves(2, it, sample_outer)
                pe.wait_ge(merged, it * MERGES + (MERGES + 1))
                pe.wait_ge(vst_ready, it + 1)
                pe.wait_ge(o_free, it + 1)
                wait_misc(M_B, 3, it, 8)
                for h in range(8):
                    out = ob[64 * (h % 2):64 * (h % 2) + 64, (h // 2) * 128:(h // 2 + 1) * 128]
                    pe.matmul(out, vst[:, h * 64:(h + 1) * 64], sfull[:, h, :], start=True, stop=False)
                    mm = pe.matmul(out, head(sst, h), head(lq[3], h), start=False, stop=True)
                mm.then_inc(o_ready, 1)
                for h in range(8):
                    mm = pe.matmul(mb[64 * (h % 2):64 * (h % 2) + 64, (h // 2) * 64:(h // 2 + 1) * 64],
                                   khat[:, h * 64:(h + 1) * 64], vst[:, h * 64:(h + 1) * 64],
                                   start=True, stop=True)
                mm.then_inc(misc_full, 1)

                def sample_outputs():
                    wait_misc(M_B, 4, it, 8)
                    taken()
                    for h2 in range(2):
                        for b in range(NS):
                            mm = pe.matmul(mb[64 * h2:64 * h2 + 64, b:b + 1], ss[64 * h2:64 * h2 + 64, b, :],
                                           qs8[64 * h2:64 * h2 + 64, b:b + 1], start=True, stop=True)
                        if h2 == 0:
                            step(mm)
                    mm.then_inc(misc_full, 1)

                halves(3, it, sample_outputs)
                pe.wait_ge(sq_ready, it + 1)
                wait_misc(M_B, 5, it, 8)
                pe.matmul(mb[:], blk64, sq[:], start=True, stop=True).then_inc(misc_full, 1)
                pe.wait_ge(acc_free[0], it * 2 + (SEC["B"][2] + 2) // 2 + 1)
                v_transposes(M_B, 6, it, 8)
            step.end(4)

            pe.wait_ge(smp_sq, 1)
            wait_misc(M_S, 0, 0, 0)
            pe.matmul(mb[:, 0:32], blk64, sqs[:], start=True, stop=True).then_inc(misc_full, 1)

            with pe.Fori(0, 4) as it:
                product("C", 0, it, 0, 0, C8, 0, xah, xal)
                pe.wait_ge(staged, it + 5)
                wait_level(L_C, 0, it, 4)
                for h in range(4):
                    mm = pe.matmul(level(0)[:, h * 128:(h + 1) * 128], kst[:, h, :], qst[:, h, :],
                                   start=True, stop=True)
                mm.then_inc(lv_full, 1)
                wait_level(L_C, 1, it, 4)
                for h in range(4):
                    mm = pe.transpose(level(1)[:, h * 128:(h + 1) * 128], kst[:, h, :], ident)
                mm.then_inc(lv_full, 1)
                wait_misc(M_C, 0, it, 4)
                pe.transpose(mb[0:NS, 0:128], ks8[:], ident).then_inc(misc_full, 1)

                product("C", 1, it, 1, 1, C8, 0, xah, xal)
                for b in range(2):
                    pe.wait_ge(lv_free[b], it * 2 + L_C // 2 + 1)
                pe.wait_ge(o_free, it + 5)
                for h in range(4):
                    out = ob[:, h * 128:(h + 1) * 128]
                    pe.matmul(out, vst[:, h * 128:(h + 1) * 128], prb[:, h, :], start=True, stop=False)
                    mm = pe.matmul(out, rst[:, h, :], qd[:, h, :], start=False, stop=True)
                mm.then_inc(ret_o, 1)
                wait_misc(M_C, 1, it, 4)
                for h in range(4):
                    mm = pe.matmul(mb[:, h * 128:(h + 1) * 128], ktk[:, h * 128:(h + 1) * 128],
                                   vst[:, h * 128:(h + 1) * 128], start=True, stop=True)
                mm.then_inc(misc_full, 1)
                for b in range(2):
                    wait_level(L_C, 2 + b, it, 4)
                    pe.matmul(level(b), k8[:], vblk[:, 512 * b:512 * b + 512],
                              start=True, stop=True).then_inc(lv_full, 1)

                product("C", 2, it, 0, 2, C8, 0, xah, xal)
                pe.wait_ge(sq_ready, it + 5)
                wait_misc(M_C, 2, it, 4)
                pe.matmul(mb[:], ones128[:], sq[:], start=True, stop=True).then_inc(misc_full, 1)
                wait_misc(M_C, 3, it, 4)
                for b in range(2):
                    pe.wait_ge(lv_free[b], it * 2 + L_C // 2 + 2)
                for b in range(NS):
                    mm = pe.matmul(mb[:, b:b + 1], rsm[:, b, :], qs8[:, b:b + 1], start=True, stop=True)
                mm.then_inc(misc_full, 1)

                product("C", 3, it, 1, 3, C8, 0, xah, xal)

            pe.wait_ge(smp_sq, 2)
            wait_misc(M_R, 0, 0, 0)
            pe.matmul(mb[:, 0:32], ones128[:], sqs[:], start=True, stop=True).then_inc(misc_full, 1)
            pe.wait_ge(ah_lo, 1)
            with pe.Fori(0, 2) as it:
                for k in range(4):
                    product("D", k, it, k % 2, 2 * k, range(4), 0, ahh, ahl, tper=8)
                    pe.wait_ge(ah_lo, 2)
                    product("D", k, it, k % 2, 2 * k + 1, range(4), 4, arh, arl, tper=8, wait_unit=False)

            with pe.Fori(0, 2) as it:
                for k in range(4):
                    product("E", k, it, k % 2, k, C8, 0, xah, xal,
                            chunk_wait=(lambda c: pe.wait_ge(mix_lo, c + 2)) if k == 0 else None)

            def mean_square(n):
                pe.wait_ge(ssq_ready, 8 * (n + 1) + 1)
                for b in range(2):
                    pe.wait_ge(lv_free[b], L_F // 2 + n)
                    pe.matmul(lvb[:, b, 0:HT], ones1024[:], ssq[:, b * HT:(b + 1) * HT],
                              start=True, stop=True).then_inc(lv_full, 1)

            pe.wait_ge(st_loaded, 16)
            wait_misc(M_F, 0, 0, 0)
            for j in range(FC):
                mm = pe.transpose(mb[:, j * 16:(j + 1) * 16], strow[:, j * 128:(j + 1) * 128],
                                  ident[0:16, 0:16])
            mm.then_inc(misc_full, 1)
            mean_square(0)
            pe.wait_ge(xb_lo, 8)
            with pe.Fori(0, 11) as it:
                for k in range(4):
                    product("F", k, it, k % 2, k, C8, 0, xbh, xbl)

            pe.wait_ge(cs_ready, FC)
            for n in range(6):
                wait_misc(M_G, n, 0, 0)
                for j in range(4 * n, min(4 * n + 4, FC)):
                    mm = pe.transpose(mb[0:10, (j % 4) * 128:(j % 4 + 1) * 128], cs[:, j, :], ident)
                mm.then_inc(misc_full, 1)
            pe.wait_ge(ac_lo, FC + 1)
            with pe.Fori(0, 4) as it:
                for k in range(4):
                    product("G", k, it, k % 2, k // 2, range(11 * (k % 2), 11 * (k % 2) + 11), 0, ach, acl,
                            first=k % 2 == 0, last=k % 2 == 1, tper=2)
            pe.wait_ge(p_loaded, 32)
            for j in range(2):
                wait_misc(M_G + 6, 2 * j, 0, 0)
                for i in range(NCH):
                    mm = pe.transpose(mb[:, i * 128:(i + 1) * 128], ptok[:, i, j * 128:(j + 1) * 128], ident)
                mm.then_inc(misc_full, 1)
                wait_misc(M_G + 6, 2 * j + 1, 0, 0)
                pe.transpose(mb[:, 0:NS], ptok[0:NS, 4, j * 128:(j + 1) * 128],
                             ident[0:NS, 0:NS]).then_inc(misc_full, 1)
            mean_square(1)
            pe.wait_ge(xb_lo, 16)
            pe.wait_ge(misc_free, M_G + 10)
            with pe.Fori(0, 2) as it:
                for k in range(4):
                    product("H", k, it, k % 2, 2 * k, C8, 0, xbh, xbl, tper=8)
                    product("H", k, it, k % 2, 2 * k + 1, range(2), 8, pxh, pxl, tper=8, wait_unit=False)

            pe.wait_ge(ssq_ready, 25)
            wait_misc(M_G + 10, 0, 0, 0)
            for i in range(5):
                n = 128 if i < 4 else NS
                mm = pe.matmul(mb[0:n, i:i + 1], ssq[:, i * 128:i * 128 + n], ones1024[:, 0:1],
                               start=True, stop=True)
            mm.then_inc(misc_full, 1)
            pe.wait_ge(y_ready, 8)
            for i in range(5):
                n = 128 if i < 4 else NS
                for half in range(2):
                    u = 2 * i + half
                    pe.wait_ge(lv_free[u % 2], L_F // 2 + 2 + u // 2)
                    for j in range(4 * half, 4 * half + 4):
                        mm = pe.transpose(lvb[0:n, u % 2, (j % 4) * 128:(j % 4 + 1) * 128],
                                          yT[:, j, i * 128:i * 128 + n], ident)
                    mm.then_inc(lv_full, 1)

        @block.scalar
        def _(act):
            step = Steps(act, act_s)
            act.sem_inc(ss_stored, 16)
            act.sem_inc(rsm_stored, 16)

            def taken():
                act.sem_inc(act_passed, 1)

            def hi(sec, k, it, size=None):
                act.wait_ge(raw_loaded[k % 2], it * 64 + 32 * ((SEC[sec][0] + k) // 2 + 1))
                n = size or SIZE[sec]
                act.activation(whi[k % 2][:, 0:n], raw[k % 2][:, 0:n], ACT.Copy).then_inc(hi_ready, 1)

            def done(sec, k, it, per=4):
                act.wait_ge(part_done, parts(sec, k, it, per) + 1)

            def ahead(sec, k, it, nxt=None):
                if k < 2:
                    hi(sec, k + 2, it)
                elif nxt is None:
                    hi(sec, k - 2, it + 1)
                else:
                    hi(nxt, k - 2, 0)

            for src, row in ((lb_logits[0], 0), (lb_logits[1], 4)):
                act.dma_start(vrow[row:row + 4, 0, :], src.rearrange("(c p) -> c p", p=128)).then_inc(vec_loaded, 16)
            for src, row in ((g_mix[0], 8), (g_ffn[0], 16), (g_ple[0], 24), (g_final, 32),
                             (g_hg_out[0], 40), (g_ret_out[0], 44)):
                n = src.shape[0] // 128
                act.dma_start(vrow[row:row + n, 0, :], src.rearrange("(c p) -> c p", p=128)).then_inc(vec_loaded, 16)
            act.dma_start(cst[:], consts).then_inc(const_loaded, 16)
            for i in range(3):
                act.dma_start(vrow[22 * i:22 * i + 22, 1, :],
                              conv_w[0, i].rearrange("(c p) -> c p", p=128)).then_inc(vec_loaded, 16)
            act.dma_start(vrow[66:88, 1, :], conv_b[0].rearrange("(c p) -> c p", p=128)).then_inc(vec_loaded, 16)
            act.dma_start(msk[:], masks).then_inc(const_loaded, 16)
            act.wait_ge(x_loaded, 80)
            act.wait_ge(set_up, 6)
            for i in range(5):
                n = 128 if i < 4 else NS
                act.activation(xsc[0:n, i, :], xtok[0:n, i, :], ACT.Square,
                               accum_out=ssx[0:n, i:i + 1]).then_inc(x_sq, 1)
            act.wait_ge(x_sq, 5)
            step(act.activation(ssx[:, 0:5], ssx[:, 0:5], ACT.Sqrt, bias=eps[:], scale=1.0 / DM))
            hi("A", 0, 0)
            hi("A", 1, 0)
            act.wait_ge(vec_ready, 1)
            act.activation(lbt[:, 1:3, :], lbt[:, 1:3, :], ACT.Exp).then_inc(lb_exp, 1)
            act.wait_ge(misc_full, 2)
            act.activation(xstg[:, :, NT:TT], mb[:, 0:64].rearrange("p (a b) -> p a b", b=NS),
                           ACT.Copy).then_inc(misc_free, 1)
            act.wait_ge(misc_free, 2)
            act.sem_inc(xt_copied, 1)
            for j in range(DC):
                act.wait_ge(lv_full, j + 1)
                act.activation(xah[:, j, 0:NT], lvb[:, j % 2, :], ACT.Copy,
                               scale=vc[:, 8 + j:9 + j]).then_inc(xa_hi, 1)
            act.wait_ge(misc_free, 3)
            act.activation(xah[:, :, NT:TT], xsm[:], ACT.Copy).then_inc(xa_hi, 1)
            for j in range(DC):
                act.wait_ge(lv_full, DC + j + 1)
                act.activation(xstg[:, j, 0:NT], lvb[:, j % 2, :], ACT.Copy).then_inc(lv_free[j % 2], 1)
            act.wait_ge(lv_free[0], 8)
            act.wait_ge(lv_free[1], 8)
            act.sem_inc(xt_copied, 8)

            with act.Fori(0, 4) as it:
                done("A", 0, it)
                ahead("A", 0, it)
                act.activation(two(sg[0][:]), ps2(0), ACT.Sigmoid).then_inc(sig_ready, 1)
                done("A", 1, it)
                ahead("A", 1, it)
                act.wait_ge(f_done, it + 1)
                act.activation(two(sgf[:]), ps2(1), ACT.Sigmoid).then_inc(acc_free[1], 1)
                done("A", 2, it)
                ahead("A", 2, it)
                act.wait_ge(misc_full, it * 2 + M_A)
                act.activation(two(hiT[:]), ps2(2), ACT.Copy).then_inc(acc_free[0], 1)
                done("A", 3, it)
                ahead("A", 3, it)
                act.activation(two(sg[1][:]), ps2(3), ACT.Sigmoid).then_inc(sig_ready, 1)
                act.wait_ge(misc_full, it * 2 + (M_A + 1))
                taken()
                act.activation(vhg[:, :, bass.ds(it * 128, 128)], m4(mb[:]), ACT.Copy).then_inc(misc_free, 1)
                act.wait_ge(misc_full, it * 2 + (M_A + 2))
                taken()
                act.activation(v8h[:, bass.ds(it * 128, 128)], mb[0:NS, 0:128], ACT.Copy).then_inc(misc_free, 1)

            with act.Fori(0, 4) as it:
                act.wait_ge(ss_stored, it * 16 + 16)
                act.wait_ge(misc_full, it * 8 + (M_B - 3))
                taken()
                act.dma_start(ss[:], state_hgrn[0].rearrange("b (c two) k v -> (two k) c b v", two=2)[:, it])\
                    .then_inc(ss_loaded, 16)
                for k, scale in ((0, 1.0), (1, KSCALE)):
                    done("B", k, it)
                    ahead("B", k, it)
                    act.wait_ge(rot_done, it * 2 + (k + 1))
                    for a, b in ((0, 64), (64, 0)):
                        act.activation(two(xs[k][a:a + 64, :]), ps2(k, b, b + 64), ACT.Copy,
                                       scale=scale).then_inc(swapped, 1)
                    if k == 0:
                        act.wait_ge(misc_full, it * 8 + (M_B + 1))
                        act.activation(k8[:], mb[0:NS, 0:128], ACT.Copy).then_inc(misc_free, 1)
                    else:
                        act.wait_ge(misc_full, it * 8 + (M_B + 2))
                        act.activation(khat[:], mb[:], ACT.Copy).then_inc(misc_free, 1)
                done("B", 2, it)
                ahead("B", 2, it)
                act.wait_ge(misc_full, it * 8 + M_B)
                act.activation(two(hiT[:]), ps2(2), ACT.Copy).then_inc(acc_free[0], 1)
                act.wait_ge(misc_free, it * 8 + (M_B + 3))
                taken()
                act.dma_start(hg_sample[0].rearrange("b (c two) k v -> (two k) c b v", two=2)[:, it], ss[:])\
                    .then_inc(ss_stored, 16)
                act.wait_ge(o_ready, it + 1)
                act.activation(sq[:], ob[:], ACT.Square).then_inc(sq_ready, 1)
                done("B", 3, it)
                ahead("B", 3, it)
                act.activation(two(sg[1][:]), ps2(3), ACT.Sigmoid).then_inc(sig_ready, 1)
                act.wait_ge(misc_full, it * 8 + (M_B + 6))
                act.activation(rs[:], mb[:], ACT.Sqrt, bias=eps[:]).then_inc(misc_free, 1)
                act.wait_ge(misc_full, it * 8 + (M_B + 7))
                taken()
                act.activation(vr[:, :, bass.ds(it * 128, 128)], m4(mb[:]), ACT.Copy).then_inc(misc_free, 1)
                act.wait_ge(misc_full, it * 8 + (M_B + 8))
                taken()
                act.activation(v8r[:, bass.ds(it * 128, 128)], mb[0:NS, 0:128], ACT.Copy).then_inc(misc_free, 1)

            act.wait_ge(misc_full, M_S + 1)
            act.activation(rss[:], mb[:, 0:32], ACT.Sqrt, bias=eps[:]).then_inc(misc_free, 1)
            act.wait_ge(smp_done, 1)
            act.wait_ge(a_done, 5)
            act.activation(ahh[:], qT[:], ACT.Copy).then_inc(ah_hi, 1)

            with act.Fori(0, 4) as it:
                act.wait_ge(rsm_stored, it * 16 + 16)
                act.wait_ge(misc_full, it * 4 + M_C)
                taken()
                act.dma_start(rsm[:], state_ret[0].rearrange("b h d v -> h d b v")[it]).then_inc(rsm_loaded, 16)
                for k in range(4):
                    done("C", k, it)
                    ahead("C", k, it)
                    act.activation(two(gab[:, it * 2 + (k // 2 + DC * (k % 2)), :]), ps2(k),
                                   ACT.Sigmoid).then_inc(acc_free[k % 2], 1)
                    if k == 0:
                        act.wait_ge(misc_full, it * 4 + (M_C + 1))
                        act.activation(k8[:], mb[0:NS, 0:128], ACT.Copy).then_inc(misc_free, 1)
                    if k == 1:
                        act.wait_ge(ret_o, it + 1)
                        act.activation(sq[:], ob[:], ACT.Square).then_inc(sq_ready, 1)
                    if k == 2:
                        act.wait_ge(misc_full, it * 4 + (M_C + 3))
                        act.activation(rs[:], mb[:], ACT.Sqrt, bias=eps[:]).then_inc(misc_free, 1)
                        act.wait_ge(lv_free[1], it * 2 + (L_C // 2 + 2))
                        taken()
                        act.dma_start(ret_sample[0].rearrange("b h d v -> h d b v")[it], rsm[:])\
                            .then_inc(rsm_stored, 16)

            act.wait_ge(misc_full, M_R + 1)
            act.activation(rss[:], mb[:, 0:32], ACT.Sqrt, bias=eps[:]).then_inc(misc_free, 1)
            act.wait_ge(smp_done, 2)
            act.wait_ge(a_done, 9)
            act.activation(arh[:], qr[:], ACT.Copy).then_inc(ah_hi, 1)
            for h2 in range(2):
                act.dma_start(hg_prompt[0, 0].rearrange("(c two) k v -> two k c v", two=2)[h2],
                              sst[64 * h2:64 * h2 + 64]).then_inc(stored, 16)
            act.dma_start(ret_prompt[0, 0].rearrange("h d v -> d h v"), rst[:]).then_inc(stored, 16)
            act.wait_ge(stored, 48)
            act.wait_ge(rsm_stored, 80)
            act.wait_ge(xt_stored, 16)
            act.wait_ge(ah_lo, 2)
            act.dma_start(hT[:], xt_dram).then_inc(h_loaded, 16)

            with act.Fori(0, 2) as it:
                for k in range(4):
                    done("D", 2 * k + 1, it, 8)
                    ahead("D", k, it)
                    act.wait_ge(mix_sum, it * 4 + (k + 1))
                    taken()
                    act.activation(xah[:, it * 4 + k, :], m1[:], ACT.Copy).then_inc(mix_hi, 1)

            act.dma_start(strow[:], state_conv[0].rearrange("b w n -> (b w) n")).then_inc(st_loaded, 16)

            def residual(sec, tile, it, per, gain):
                j = it * per + tile
                act.wait_ge(acc_free[tile % 2], tidx(sec, tile, it, per) + 1)
                taken()
                act.activation(xbh[:, j, :], hT[:, j, :], ACT.Copy,
                               scale=vc[:, bass.ds(j + gain, 1)]).then_inc(xb_hi, 1)

            def inverse_rms(n):
                act.wait_ge(lv_full, L_TOTAL + 2 * n + 2)
                for b in range(2):
                    act.activation(rstd[:, b * HT:(b + 1) * HT], lvb[:, b, 0:HT], ACT.Sqrt,
                                   bias=eps[:]).then_inc(lv_free[b], 1)

            with act.Fori(0, 2) as it:
                for k in range(4):
                    done("E", k, it)
                    ahead("E", k, it)
                    residual("E", k, it, 4, 16)

            act.wait_ge(misc_full, M_F + 1)
            act.activation(stT[:].rearrange("p a b -> p (a b)"), mb[:, 0:FC * 16], ACT.Copy).then_inc(misc_free, 1)
            inverse_rms(0)

            def ffn(it, nxt=None):
                for k in range(4):
                    done("F", k, it)
                    ahead("F", k, it, nxt)
                    if k % 2 == 0:
                        act.wait_ge(acc_free[0], tidx("F", k, it) + 1)
                        act.wait_ge(act_ready, it * 2 + (k // 2 + 1))
                        taken()
                        act.activation(cv[:, 0:NT], ab[k // 2][:, 0:NT], ACT.Identity,
                                       scale=vc[:, bass.ds(it * 2 + (48 + k // 2), 1)],
                                       bias=vc[:, bass.ds(it * 2 + (48 + 3 * FC + k // 2), 1)]).then_inc(c_first, 1)
                        act.wait_ge(c_ready, it * 2 + (k // 2 + 1))
                        act.activation(cv[:], cv[:], ACT.Gelu_apprx_tanh).then_inc(gelu_ready, 1)
                    else:
                        act.wait_ge(act_ready, it * 2 + (k // 2 + 2))
                        taken()
                        act.activation(ach[:, it * 2 + k // 2, :], gg[:], ACT.Copy).then_inc(ac_hi, 1)

            with act.Fori(0, 10) as it:
                ffn(it)
            ffn(10, "G")
            act.wait_ge(ac_lo, FC + 1)
            for n in range(6):
                w = 512 if n < 5 else 256
                act.wait_ge(misc_full, M_G + n + 1)
                act.activation(csr[:, n * 512:n * 512 + w], mb[0:10, 0:w], ACT.Copy).then_inc(misc_free, 1)

            def down(it, nxt=None):
                for k in range(4):
                    done("G", k, it)
                    ahead("G", k, it, nxt)
                    if k % 2:
                        residual("G", k // 2, it, 2, 24)

            with act.Fori(0, 3) as it:
                down(it)
            down(3, "H")
            for j in range(2):
                act.wait_ge(misc_full, M_G + 6 + 2 * j + 1)
                act.activation(pxh[:, j, 0:NT], mb[:], ACT.Copy).then_inc(p_hi, 1)
                act.wait_ge(misc_full, M_G + 6 + 2 * j + 2)
                act.activation(pxh[:, j, NT:TT], mb[:, 0:NS], ACT.Copy).then_inc(p_hi, 1)
            inverse_rms(1)

            def embed(it, last=False):
                for k in range(4):
                    done("H", 2 * k, it, 8)
                    act.wait_ge(acc_free[0], tidx("H", 2 * k, it, 8) + 1)
                    act.activation(sgg[:], tg[:], ACT.Sigmoid).then_inc(sig_ready, 1)
                    done("H", 2 * k + 1, it, 8)
                    if k < 2 or not last:
                        ahead("H", k, it)
                    act.wait_ge(h_new, it * 4 + (k + 2))
                    taken()
                    act.activation(yT[:, it * 4 + k, :], hT[:, it * 4 + k, :], ACT.Copy,
                                   scale=vc[:, bass.ds(it * 4 + (32 + k), 1)]).then_inc(y_ready, 1)

            embed(0)
            embed(1, last=True)
            act.wait_ge(misc_full, M_G + 11)
            act.activation(rt[:, 0:4], mb[:, 0:4], ACT.Sqrt, bias=eps[:])
            act.activation(rt[0:NS, 4:5], mb[0:NS, 4:5], ACT.Sqrt, bias=eps[0:NS]).then_inc(misc_free, 1)
            act.wait_ge(rt_ready, 1)
            for u in range(0, 10, 2):
                n = 128 if u < 8 else NS
                act.wait_ge(lv_full, L_TOTAL + 4 + u + 1)
                act.activation(ytok[0:n, u // 2, 0:512], lvb[0:n, 0, :], ACT.Copy,
                               scale=rt[0:n, u // 2:u // 2 + 1]).then_inc(lv_free[0], 1)

        @block.vector
        def _(dve):
            def taken():
                dve.sem_inc(dve_passed, 1)

            step = Steps(dve, dve_s)
            dve.sem_inc(lo_ready, 2)
            for first in (*acc_free, rot_done, f_done, merged, o_free, mix_lo, ac_lo, h_new):
                dve.sem_inc(first, 1)

            def lo(sec, k, it):
                dve.wait_ge(hi_ready, unit(sec, k, it) + 1)
                n = SIZE[sec]
                dve.tensor_tensor(wlo[k % 2][:, 0:n], raw[k % 2][:, 0:n], whi[k % 2][:, 0:n].bitcast(fp),
                                  SUB).then_inc(lo_ready, 1)

            def done(sec, k, it, per=4):
                dve.wait_ge(part_done, parts(sec, k, it, per) + 1)

            def ahead(sec, k, it, nxt=None):
                if k < 2:
                    lo(sec, k + 2, it)
                elif nxt is None:
                    lo(sec, k - 2, it + 1)
                else:
                    lo(nxt, k - 2, 0)

            dve.wait_ge(misc_full, 1)
            dve.tensor_copy(vc[:], mb[:, 0:136]).then_inc(misc_free, 1)
            dve.wait_ge(misc_free, 1)
            step(dve.tensor_tensor(lbt[:, 0, :], vc[:, 0:4], vc[:, 4:8], ALU.max))
            step(dve.tensor_tensor(lbt[:, 1, :], vc[:, 0:4], lbt[:, 0, :], SUB))
            dve.tensor_tensor(lbt[:, 2, :], vc[:, 4:8], lbt[:, 0, :], SUB).then_inc(vec_ready, 1)
            dve.wait_ge(act_s, 1)
            step(dve.reciprocal(ssx[:, 0:5], ssx[:, 0:5]))
            for i in range(5):
                n = 128 if i < 4 else NS
                dve.tensor_scalar(xsc[0:n, i, :], xtok[0:n, i, :], ssx[0:n, i:i + 1], None,
                                  MUL).then_inc(x_scaled, 1)
            lo("A", 0, 0)
            lo("A", 1, 0)
            dve.wait_ge(lb_exp, 1)
            step(dve.tensor_tensor(lbt[:, 5, :], lbt[:, 1, :], lbt[:, 2, :], ADD))
            step(dve.reciprocal(lbt[:, 5, :], lbt[:, 5, :]))
            step(dve.tensor_tensor(lbt[:, 3, :], lbt[:, 1, :], lbt[:, 5, :], MUL))
            step(dve.tensor_scalar(lbt[:, 4, :], lbt[:, 3, :], -1.0, 1.0, MUL, ADD))
            dve.wait_ge(misc_full, 3)
            dve.tensor_tensor(xsm[:], mb[:, 0:64].rearrange("p (a b) -> p a b", b=NS),
                              vc[:, 8:16].unsqueeze(2).broadcast_to([128, DC, NS]), MUL).then_inc(misc_free, 1)
            for j in range(DC):
                dve.wait_ge(xa_hi, j + 1)
                dve.scalar_tensor_tensor(xal[:, j, 0:NT], lvb[:, j % 2, :], vc[:, 8 + j:9 + j],
                                         xah[:, j, 0:NT].bitcast(fp), MUL, SUB).then_inc(lv_free[j % 2], 1)
            dve.wait_ge(xa_hi, 9)
            dve.tensor_tensor(xal[:, :, NT:TT], xsm[:], xah[:, :, NT:TT].bitcast(fp), SUB).then_inc(xa_lo, 1)

            with dve.Fori(0, 4) as it:
                done("A", 0, it)
                ahead("A", 0, it)
                dve.wait_ge(sig_ready, it * 2 + 1)
                dve.tensor_tensor(two(qT[:, it, :]), ps2(0), two(sg[0][:]), MUL).then_inc(acc_free[0], 1)
                done("A", 1, it)
                ahead("A", 1, it)
                dve.wait_ge(acc_free[1], tidx("A", 1, it) + 1)
                dve.tensor_scalar(fT[:, it, :], sgf[:], lbt[:, 4, bass.ds(it, 1)], lbt[:, 3, bass.ds(it, 1)],
                                  MUL, ADD).then_inc(f_done, 1)
                done("A", 2, it)
                ahead("A", 2, it)
                done("A", 3, it)
                ahead("A", 3, it)
                dve.wait_ge(sig_ready, it * 2 + 2)
                dve.scalar_tensor_tensor(two(ghg[:, it, :]), ps2(3), vc[:, bass.ds(it + 40, 1)],
                                         two(sg[1][:]), MUL, MUL).then_inc(acc_free[1], 1)

            dve.wait_ge(xt_stored, 16)
            dve.wait_ge(set_up, 7)

            def merge(use, it):
                dve.wait_ge(sc_full, it * 4 + (use + 1))
                n = 4 * use
                for l in (2 * use, 2 * use + 1):
                    for b in range(2):
                        dve.wait_ge(merged, it * MERGES + (n + 1))
                        taken()
                        n += 1
                        if l == LV:
                            if b == 0:
                                dve.copy_predicated(
                                    sfull[:], ident.bitcast(u32).unsqueeze(1).broadcast_to([128, 8, CH]),
                                    lvb[:, 0, 256:264].unsqueeze(2).broadcast_to([128, 8, CH])).then_inc(merged, 1)
                            continue
                        hb = 1 << l
                        dst = sfull[:].rearrange("s (e par) (b two h) -> s par e b two h", par=2, two=2, h=hb)
                        on = msk[:, l * 64:(l + 1) * 64].rearrange("s (b h) -> s b h", h=hb).unsqueeze(1)\
                            .broadcast_to([128, 4, 64 // hb, hb])
                        c0 = 256 * (l % 2)
                        src = lvb[:, b, c0:c0 + 256].rearrange("s (e b h) -> s e b h", e=4, h=hb)
                        dve.copy_predicated(dst[:, b, :, :, 1, :], on, src).then_inc(merged, 1)

            def rotate(dst, k, it):
                step(dve.tensor_tensor(xs[k][:], xs[k][:], sinT, MUL))
                dve.wait_ge(acc_free[k], tidx("B", k, it) + 1)
                dve.tensor_tensor(dst, dst, xs[k][:], ADD).then_inc(rot_done, 1)

            with dve.Fori(0, 4) as it:
                step.loop(it, 5)
                done("B", 0, it)
                dve.wait_ge(swapped, it * 4 + 2)
                dve.tensor_tensor(two(qr[:, it, :]), ps2(0), two(cosT), MUL).then_inc(acc_free[0], 1)
                merge(0, it)
                ahead("B", 0, it)
                merge(1, it)
                rotate(qr[:, it, :], 0, it)

                done("B", 1, it)
                dve.wait_ge(swapped, it * 4 + 4)
                dve.scalar_tensor_tensor(two(kr[:, it, :]), ps2(1), KSCALE, two(cosT), MUL,
                                         MUL).then_inc(acc_free[1], 1)
                merge(2, it)
                ahead("B", 1, it)
                merge(3, it)
                dve.wait_ge(ss_loaded, it * 16 + 16)
                dve.wait_ge(staged, it + 1)
                step(dve.tensor_tensor(ss[:], ss[:], fs8[:].unsqueeze(2).broadcast_to([128, NS, 64]), MUL))
                dve.wait_ge(misc_full, it * 8 + (M_B + 3))
                dve.tensor_tensor(ss[:], ss[:], mb[:].rearrange("p (b v) -> p b v", b=NS),
                                  ADD).then_inc(misc_free, 1)
                rotate(kr[:, it, :], 1, it)

                done("B", 2, it)
                ahead("B", 2, it)
                dve.wait_ge(o_ready, it + 1)
                dve.wait_ge(prep, it * 8 + 8)
                step(dve.tensor_tensor(sst[:], sst[:], tl[LV][:].broadcast_to([128, 4, 64]), MUL))
                dve.wait_ge(misc_full, it * 8 + (M_B + 4))
                dve.tensor_tensor(sst[:], sst[:], mb[:, 0:256].rearrange("p (c v) -> p c v", c=4),
                                  ADD).then_inc(misc_free, 1)
                dve.wait_ge(misc_full, it * 8 + (M_B + 5))
                dve.tensor_copy(qT[:, it, NT:TT], mb[:, 0:NS]).then_inc(misc_free, 1)

                done("B", 3, it)
                ahead("B", 3, it)
                dve.wait_ge(sig_ready, it + 9)
                dve.scalar_tensor_tensor(two(grt[:, it, :]), ps2(3), vc[:, bass.ds(it + 44, 1)],
                                         two(sg[1][:]), MUL, MUL).then_inc(acc_free[1], 1)
                dve.wait_ge(misc_free, it * 8 + (M_B + 6))
                step(dve.reciprocal(rs[:], rs[:]))
                dve.wait_ge(a_done, it + 1)
                dve.tensor_tensor(ot[:], ob[:], rs[:], MUL).then_inc(o_free, 1)
            step.end(4)

            def norm_samples(t, gate, n, m):
                cols = t[:, :, NT:TT]
                dve.wait_ge(misc_free, m)
                dve.tensor_tensor(sqs[:].rearrange("p (a b) -> p a b", a=4), cols, cols, MUL).then_inc(smp_sq, 1)
                dve.wait_ge(misc_free, m + 1)
                step(dve.reciprocal(rss[:], rss[:]))
                step(dve.tensor_tensor(cols, cols, rss[:].rearrange("p (a b) -> p a b", a=4), MUL))
                dve.tensor_tensor(cols, cols, gate[:, :, NT:TT], MUL).then_inc(smp_done, 1)

            norm_samples(qT, ghg, 1, M_S)
            dve.wait_ge(ah_hi, 1)
            dve.tensor_tensor(ahl[:], qT[:], ahh[:].bitcast(fp), SUB).then_inc(ah_lo, 1)

            with dve.Fori(0, 4) as it:
                step.loop(it, 2)
                done("C", 0, it)
                dve.wait_ge(lv_full, it * 4 + (L_C + 1))
                dve.tensor_tensor(prb[:].rearrange("s h t -> s (h t)"), lvb[:, 0, :], decay,
                                  MUL).then_inc(lv_free[0], 1)
                dve.wait_ge(lv_full, it * 4 + (L_C + 2))
                dve.tensor_tensor(m4(ktk[:]), m4(lvb[:, 1, :]), kdec.unsqueeze(2).broadcast_to([128, 4, 128]),
                                  MUL).then_inc(lv_free[1], 1)
                ahead("C", 0, it)
                done("C", 1, it)
                ahead("C", 1, it)
                dve.wait_ge(ret_o, it + 1)
                step(dve.tensor_tensor(rst[:], rst[:], g128.unsqueeze(2).broadcast_to([128, 4, 128]), MUL))
                dve.wait_ge(misc_full, it * 4 + (M_C + 2))
                dve.tensor_tensor(rst[:], rst[:], m4(mb[:]), ADD).then_inc(misc_free, 1)
                dve.wait_ge(rsm_loaded, it * 16 + 16)
                for b in range(2):
                    dve.wait_ge(lv_full, it * 4 + (L_C + 3 + b))
                    part4 = rsm[:, 4 * b:4 * b + 4, :].rearrange("p b v -> p (b v)")
                    dve.scalar_tensor_tensor(part4, part4, gam[:, bass.ds(it, 1)], lvb[:, b, :], MUL,
                                             ADD).then_inc(lv_free[b], 1)
                done("C", 2, it)
                ahead("C", 2, it)
                dve.wait_ge(misc_free, it * 4 + (M_C + 3))
                step(dve.reciprocal(rs[:], rs[:]))
                dve.wait_ge(a_done, it + 5)
                dve.tensor_tensor(ot[:], ob[:], rs[:], MUL).then_inc(o_free, 1)
                dve.wait_ge(misc_full, it * 4 + (M_C + 4))
                dve.tensor_copy(qr[:, it, NT:TT], mb[:, 0:NS]).then_inc(misc_free, 1)
                done("C", 3, it)
                ahead("C", 3, it)
            step.end(4)

            norm_samples(qr, grt, 2, M_R)
            dve.wait_ge(ah_hi, 2)
            dve.tensor_tensor(arl[:], qr[:], arh[:].bitcast(fp), SUB).then_inc(ah_lo, 1)

            with dve.Fori(0, 2) as it:
                for k in range(4):
                    done("D", 2 * k, it, 8)
                    dve.wait_ge(mix_lo, it * 4 + (k + 1))
                    dve.tensor_tensor(two(m1[:]), ps2(0), two(gab[:, it * 4 + k, :]), MUL).then_inc(acc_free[0], 1)
                    done("D", 2 * k + 1, it, 8)
                    dve.tensor_tensor(two(m2[:]), ps2(1), two(gab[:, it * 4 + (DC + k), :]),
                                      MUL).then_inc(acc_free[1], 1)
                    for b in range(2):
                        dve.wait_ge(acc_free[b], tidx("D", 2 * k + b, it, 8) + 1)
                    dve.tensor_tensor(m1[:], m1[:], m2[:], ADD).then_inc(mix_sum, 1)
                    ahead("D", k, it)
                    dve.wait_ge(mix_hi, it * 4 + (k + 1))
                    dve.tensor_tensor(xal[:, it * 4 + k, :], m1[:], xah[:, it * 4 + k, :].bitcast(fp),
                                      SUB).then_inc(mix_lo, 1)

            def residual(sec, tile, it, per, gain, n):
                j = it * per + tile
                dve.tensor_tensor(two(hT[:, j, :]), ps2(tile), two(hT[:, j, :]), ADD).then_inc(acc_free[tile % 2], 1)

                def low():
                    dve.wait_ge(xb_hi, it * per + (n + tile + 1))
                    dve.scalar_tensor_tensor(xbl[:, j, :], hT[:, j, :], vc[:, bass.ds(j + gain, 1)],
                                             xbh[:, j, :].bitcast(fp), MUL, SUB).then_inc(xb_lo, 1)
                return low

            dve.wait_ge(h_loaded, 16)
            with dve.Fori(0, 2) as it:
                for k in range(4):
                    done("E", k, it)
                    low = residual("E", k, it, 4, 16, 0)
                    ahead("E", k, it)
                    low()

            def inverse_rms(n):
                for b in range(2):
                    dve.wait_ge(lv_free[b], L_F // 2 + n + 1)
                step(dve.reciprocal(rstd[:], rstd[:]))

            dve.wait_ge(misc_free, M_F + 1)
            old = stT[:].rearrange("p j (b w) -> p j b w", w=2)

            def tap(i):
                return vc[:, 48 + FC * i:48 + FC * (i + 1)].unsqueeze(2).broadcast_to([128, FC, NS])

            tmp = gg[:, 0:FC * NS].rearrange("p (j b) -> p j b", b=NS)
            step(dve.tensor_tensor(part[:], old[:, :, :, 0], tap(0), MUL))
            step(dve.tensor_tensor(tmp, old[:, :, :, 1], tap(1), MUL))
            step(dve.tensor_tensor(part[:], part[:], tmp, ADD))
            step(dve.tensor_tensor(part[:], part[:], tap(3), ADD))
            for b in range(2):
                step(dve.memset(ab[b][:, 0:2], 0.0))
            inverse_rms(0)

            def ffn(it, nxt=None):
                for k in range(4):
                    done("F", k, it)
                    j = it * 2 + k // 2
                    if k % 2 == 0:
                        a = ab[k // 2]
                        dve.tensor_tensor(two(a[:, 2:TT + 2]), ps2(k), two(rstd[:]), MUL).then_inc(acc_free[0], 1)
                        ahead("F", k, it, nxt)
                        dve.wait_ge(c_first, it * 2 + (k // 2 + 1))
                        w1 = vc[:, bass.ds(it * 2 + (48 + FC + k // 2), 1)]
                        w2 = vc[:, bass.ds(it * 2 + (48 + 2 * FC + k // 2), 1)]
                        step(dve.scalar_tensor_tensor(cv[:, NT:TT], a[:, TT - 6:TT + 2], w2, part[:, j, :], MUL, ADD))
                        step(dve.scalar_tensor_tensor(cv[:, 0:NT], a[:, 1:NT + 1], w1, cv[:, 0:NT], MUL, ADD))
                        dve.scalar_tensor_tensor(cv[:, 0:NT], a[:, 2:NT + 2], w2, cv[:, 0:NT], MUL,
                                                 ADD).then_inc(c_ready, 1)
                    else:
                        dve.wait_ge(ac_lo, it * 2 + (k // 2 + 1))
                        dve.tensor_tensor(two(gg[:]), ps2(k), two(rstd[:]), MUL).then_inc(acc_free[1], 1)
                        ahead("F", k, it, nxt)
                        dve.wait_ge(ac_hi, it * 2 + (k // 2 + 1))
                        dve.tensor_tensor(acl[:, j, :], gg[:], ach[:, j, :].bitcast(fp), SUB).then_inc(ac_lo, 1)

            with dve.Fori(0, 10) as it:
                step.loop(it, 4)
                ffn(it)
            step.end(10)
            ffn(10, "G")

            def down(it, nxt=None):
                for k in range(4):
                    done("G", k, it)
                    if k % 2:
                        low = residual("G", k // 2, it, 2, 24, 8)
                    ahead("G", k, it, nxt)
                    if k % 2:
                        low()

            with dve.Fori(0, 3) as it:
                down(it)
            down(3, "H")
            for j in range(2):
                dve.wait_ge(p_hi, 2 * j + 1)
                dve.tensor_tensor(pxl[:, j, 0:NT], mb[:], pxh[:, j, 0:NT].bitcast(fp), SUB).then_inc(misc_free, 1)
                dve.wait_ge(p_hi, 2 * j + 2)
                dve.tensor_tensor(pxl[:, j, NT:TT], mb[:, 0:NS], pxh[:, j, NT:TT].bitcast(fp),
                                  SUB).then_inc(misc_free, 1)
            inverse_rms(1)

            def embed(it, last=False):
                for k in range(4):
                    done("H", 2 * k, it, 8)
                    dve.tensor_tensor(two(tg[:]), ps2(0), two(rstd[:]), MUL).then_inc(acc_free[0], 1)
                    done("H", 2 * k + 1, it, 8)
                    dve.wait_ge(sig_ready, it * 4 + (12 + k + 1))
                    dve.wait_ge(h_new, it * 4 + (k + 1))
                    dve.tensor_tensor(two(tp[:]), ps2(1), two(sgg[:]), MUL).then_inc(acc_free[1], 1)
                    dve.wait_ge(acc_free[1], tidx("H", 2 * k + 1, it, 8) + 1)
                    dve.tensor_tensor(hT[:, it * 4 + k, :], hT[:, it * 4 + k, :], tp[:], ADD).then_inc(h_new, 1)
                    if k < 2 or not last:
                        ahead("H", k, it)

            embed(0)
            embed(1, last=True)
            dve.wait_ge(misc_free, M_G + 11)
            dve.reciprocal(rt[:, 0:4], rt[:, 0:4])
            dve.reciprocal(rt[0:NS, 4:5], rt[0:NS, 4:5]).then_inc(rt_ready, 1)
            dve.wait_ge(rt_ready, 1)
            for u in range(1, 10, 2):
                n = 128 if u < 8 else NS
                dve.wait_ge(lv_full, L_TOTAL + 4 + u + 1)
                dve.tensor_scalar(ytok[0:n, u // 2, 512:1024], lvb[0:n, 1, :], rt[0:n, u // 2:u // 2 + 1], None,
                                  MUL).then_inc(lv_free[1], 1)

        @block.gpsimd
        def _(pool):
            def taken():
                pool.sem_inc(pool_passed, 1)

            step = Steps(pool, pool_s, taken)
            for first in (a_done, act_ready, ssq_ready):
                pool.sem_inc(first, 1)
            for t, v in ((ones128, 1.0 / 128), (ones1024, 1.0 / DM), (eps, EPS), (ssx, 1.0), (sst, 0.0), (rst, 0.0)):
                pool.memset(t[:], v).then_inc(set_up, 1)
            pool.wait_ge(const_loaded, 32)

            def chunk(t, c):
                return t[:, :, bass.ds(c * CH, CH)]

            def first_level(c):
                step(pool.tensor_copy(tl[0][:], chunk(fT, c)))
                step(pool.tensor_scalar(lk[0][:], tl[0][:], -1.0, 1.0, MUL, ADD))
                step(pool.tensor_tensor(lq[0][:], chunk(qT, c), tl[0][:], MUL))
                pool.tensor_tensor(qk[:], chunk(qT, c), lk[0][:], MUL).then_inc(prep, 1)

            def next_level(l):
                hb = 1 << (l - 1)

                def halves(t):
                    return t[:].rearrange("p c (b two h) -> p (c b) two h", two=2, h=hb)
                q0, q1, k0, k1 = (halves(t[i % 4]) for t in (lq, lk) for i in (l - 1, l))
                t0 = tl[l - 1][:].rearrange("p c (b two) -> p (c b) two", two=2)
                shape = [128, 4 * (CH // (2 * hb)), hb]
                pool.tensor_copy(q1[:, :, 0, :], q0[:, :, 0, :])
                pool.tensor_copy(k1[:, :, 1, :], k0[:, :, 1, :])
                pool.tensor_tensor(q1[:, :, 1, :], q0[:, :, 1, :], t0[:, :, 0:1].broadcast_to(shape), MUL)
                pool.tensor_tensor(k1[:, :, 0, :], k0[:, :, 0, :], t0[:, :, 1:2].broadcast_to(shape), MUL)
                pool.tensor_tensor(tl[l][:].rearrange("p c b -> p (c b)"), t0[:, :, 0], t0[:, :, 1],
                                   MUL).then_inc(prep, 1)

            def outer_values(src, it, groups):
                g, w = groups, 128 // groups
                out = vblk[:].rearrange("p (g b v) -> p g b v", g=g, b=NS)
                v = src[:, bass.ds(it * 128, 128)].rearrange("p (g v) -> p g v", g=g).unsqueeze(2)\
                    .broadcast_to([NS, g, NS, w])
                d = ident[0:NS, 0:NS].unsqueeze(1).unsqueeze(3).broadcast_to([NS, g, NS, w])
                return pool.tensor_tensor(out, v, d, MUL)

            pool.wait_ge(acc_free[0], 9)
            pool.wait_ge(acc_free[1], 9)
            pool.wait_ge(f_done, 5)
            pool.wait_ge(misc_free, M_B)
            pool.memset(sfull[:], 0.0).then_inc(set_up, 1)
            first_level(0)
            for l in range(1, 4):
                pool.wait_ge(prep, l)
                next_level(l)

            def hgrn(it, last=False):
                pool.wait_ge(misc_free, it * 8 + (M_B - 3))
                taken()
                step(pool.tensor_copy(fs8[:], fT[:, it, NT:TT]))
                pool.tensor_copy(qs8[:], qT[:, it, NT:TT])
                outer_values(v8h, it, 2)
                pool.tensor_scalar(ks8[:], fs8[:], -1.0, 1.0, MUL, ADD).then_inc(staged, 1)
                pool.tensor_copy(vst[:], vhg[:, it, :]).then_inc(vst_ready, 1)
                for l in range(4, LV + 1):
                    pool.wait_ge(prep, it * 8 + l)
                    pool.wait_ge(sc_full, it * 4 + ((l - 4) // 2 + 1))
                    taken()
                    next_level(l)
                if not last:
                    pool.wait_ge(sc_full, it * 4 + 4)
                    taken()
                    first_level(it + 1)
                    for l in range(1, 4):
                        pool.wait_ge(prep, it * 8 + (8 + l))
                        if l == 3:
                            pool.wait_ge(o_ready, it + 1)
                        taken()
                        next_level(l)
                pool.wait_ge(o_free, it + 2)
                taken()
                pool.tensor_tensor(chunk(qT, it), m4(ot[:]), chunk(ghg, it), MUL).then_inc(a_done, 1)

            with pool.Fori(0, 3) as it:
                step.loop(it, 4)
                hgrn(it)
            step.end(3)
            hgrn(3, last=True)

            pool.wait_ge(rot_done, 9)
            with pool.Fori(0, 4) as it:
                step.loop(it, 1)
                pool.wait_ge(misc_free, it * 4 + M_C)
                taken()
                pool.tensor_copy(kst[:], chunk(kr, it))
                step(pool.tensor_copy(qst[:], chunk(qr, it)))
                pool.tensor_copy(vst[:], vr[:, it, :])
                pool.tensor_copy(ks8[:], kr[:, it, NT:TT])
                pool.tensor_copy(qs8[:], qr[:, it, NT:TT])
                outer_values(v8r, it, 1)
                pool.tensor_tensor(qd[:], qst[:], m4(qdec), MUL).then_inc(staged, 1)
                pool.wait_ge(o_free, it + 6)
                taken()
                pool.tensor_tensor(chunk(qr, it), m4(ot[:]), chunk(grt, it), MUL).then_inc(a_done, 1)
            step.end(4)

            def squares(j, n):
                pool.wait_ge(ssq_ready, j + (n + 1))
                taken()
                step(pool.tensor_tensor(sqt[:], hT[:, j, :], hT[:, j, :], MUL))
                pool.tensor_tensor(ssq[:], ssq[:], sqt[:], ADD).then_inc(ssq_ready, 1)

            pool.wait_ge(acc_free[0], tidx("E", 0, 0) + 1)
            step(pool.memset(ssq[:], 0.0))
            with pool.Fori(0, 2) as it:
                step.loop(it, 4)
                for k in range(4):
                    pool.wait_ge(acc_free[k % 2], tidx("E", k, it) + 1)
                    taken()
                    squares(it * 4 + k, 0)
            step.end(2)

            with pool.Fori(0, 11) as it:
                for k in range(2):
                    pool.wait_ge(acc_free[0], tidx("F", 2 * k, it) + 1)
                    taken()
                    pool.tensor_copy(cs[:, it * 2 + k, :], ab[k][:, NT:TT + 2]).then_inc(cs_ready, 1)
                    pool.wait_ge(acc_free[1], tidx("F", 2 * k + 1, it) + 1)
                    pool.wait_ge(gelu_ready, it * 2 + (k + 1))
                    pool.tensor_tensor(gg[:], gg[:], cv[:], MUL).then_inc(act_ready, 1)

            pool.wait_ge(acc_free[0], tidx("G", 0, 0, 2) + 1)
            step(pool.memset(ssq[:], 0.0))
            with pool.Fori(0, 4) as it:
                step.loop(it, 2)
                for k in range(2):
                    pool.wait_ge(acc_free[k], tidx("G", k, it, 2) + 1)
                    taken()
                    squares(it * 2 + k, 8)
            step.end(4)
            pool.wait_ge(h_new, 2)
            step(pool.memset(ssq[:], 0.0))
            with pool.Fori(0, 2) as it:
                step.loop(it, 4)
                for k in range(4):
                    pool.wait_ge(h_new, it * 4 + (k + 2))
                    taken()
                    squares(it * 4 + k, 16)
            step.end(2)


def shape_tables():
    import numpy as np
    f32 = np.float32
    gamma = 1.0 - 2.0 ** (-5.0 - np.arange(4))
    inv = (f32(10000.0) ** (-np.arange(0, 128, 2, dtype=f32) / f32(128))).astype(f32)
    pos = np.concatenate([np.arange(512, dtype=f32), np.full(8, 4096.0, f32)])
    ang = (pos[None, :] * inv[:, None]).astype(f32).astype(np.float64)
    t = np.arange(128)
    s_, t_ = t[:, None], t[None, :]
    tables = {
        "ident": np.eye(128),
        "blk64": (s_ // 64 == t_ // 64) / 64.0,
        "headsel": (s_ // 64 == np.arange(2)[None, :]) * 1.0,
        "cos": np.concatenate([np.cos(ang), np.cos(ang)]),
        "sin": np.concatenate([-np.sin(ang), np.sin(ang)]),
        "decay": np.concatenate([np.where(t_ >= s_, g ** np.maximum(t_ - s_, 0), 0.0) for g in gamma], 1),
        "qdec": np.concatenate([np.broadcast_to(g ** (t_ + 1.0), (128, 128)) for g in gamma], 1),
        "kdec": gamma[None, :] ** (127.0 - s_),
        "g128": np.broadcast_to(gamma ** 128.0, (128, 4)),
        "gam": np.broadcast_to(gamma, (128, 4)),
    }
    offs, at = {}, 0
    for n, a in tables.items():
        offs[n] = at
        at += a.shape[1]
    masks = []
    for l in range(7):
        h = 1 << l
        second = t[(t // h) % 2 == 1]
        masks.append(((s_ // (2 * h) == second[None, :] // (2 * h)) & ((s_ // h) % 2 == 0)).astype(np.uint32))
    return (np.ascontiguousarray(np.concatenate(list(tables.values()), 1), dtype=f32), offs,
            np.ascontiguousarray(np.concatenate(masks, 1)))


_INS = ["x_prompt", "x_sample", "state_hgrn", "state_ret", "state_conv", "p_prompt", "p_sample", "lb_logits",
        "w_in", "g_mix", "g_hg_out", "g_ret_out", "w_br_hg", "w_br_ret", "w_out", "g_ffn", "w_up", "conv_w",
        "conv_b", "w_down", "g_ple", "w_ple", "w_ple_gate", "g_final"]
_OUTS = [(1, 512, 1024), (8, 1, 1024), (1, 1, 8, 64, 64), (1, 1, 4, 128, 128), (1, 1, 2, 2816),
         (1, 8, 8, 64, 64), (1, 8, 4, 128, 128), (1, 8, 2, 2816)]


def kernel(**inputs):
    import numpy as _np
    import concourse.bacc as _bacc
    from concourse import mybir as _mybir
    from concourse.bass_utils import run_bass_kernel_spmd as _run

    nc = _bacc.Bacc("TRN2", target_bir_lowering=False, num_devices=1)
    consts, offs, masks = shape_tables()
    arrays, args = {}, []
    for name in _INS:
        arrays[f"in_{name}"] = _np.ascontiguousarray(inputs[name])
    arrays["consts"], arrays["masks"] = consts, masks
    for name, a in arrays.items():
        args.append(nc.dram_tensor(name, a.shape, _mybir.dt.from_np(a.dtype), kind="ExternalInput").ap())
    for i, shape in enumerate(_OUTS):
        args.append(nc.dram_tensor(f"out_{i}", shape, _mybir.dt.float32, kind="ExternalOutput").ap())
    hybrid_layer(nc, *args, offs=offs)
    r = _run(nc, [arrays], core_ids=[0])
    return tuple(r.results[0][f"out_{i}"] for i in range(len(_OUTS)))
```

```python
import concourse.bass as bass
from concourse import mybir
from contextlib import ExitStack

NT = 512
NS = 8
TT = NT + NS
HT = TT // 2
DM = 1024
DC = DM // 128
CH = 128
NCH = NT // CH
LV = 7
FF = 2816
FC = FF // 128
PD = 256
EPS = 1e-6
WMAX = FC // 2 * 128

SEC = dict(A=(0, 0, 2), V=(8, 8, 10), B=(16, 16, 18), C=(32, 32, 34), D=(48, 48, 50), E=(56, 64, 66),
           F=(64, 72, 74), G=(108, 116, 118), H=(124, 132, 126))
SIZE = dict(A=1024, V=1024, B=1024, C=1024, D=1024, E=1024, F=1024, G=WMAX, H=1280)
M_A, M_B, M_C, M_R, M_F, M_G = 3, 11, 35, 51, 52, 53
L_C, L_F = 16, 32
L_TOTAL = L_F
MERGES = 15


class Steps:

    def __init__(self, eng, sem, after=None):
        self.eng, self.sem, self.base, self.k, self.it, self.per = eng, sem, 0, 0, 0, 0
        self.after = after

    def loop(self, it, per):
        self.base, self.k, self.it, self.per = self.base + self.k, 0, it, per

    def end(self, rounds):
        assert self.k == self.per, (self.k, self.per)
        self.base, self.k, self.it, self.per = self.base + rounds * self.per, 0, 0, 0

    def __call__(self, ins):
        ins.then_inc(self.sem, 1)
        self.k += 1
        self.eng.wait_ge(self.sem, self.it * self.per + (self.base + self.k))
        if self.after:
            self.after()


def hybrid_layer(nc, x_prompt, x_sample, state_hgrn, state_ret, state_conv, p_prompt, p_sample,
                 lb_logits, w_in, g_mix, g_hg_out, g_ret_out, w_br_hg, w_br_ret, w_out, g_ffn, w_up,
                 conv_w, conv_b, w_down, g_ple, w_ple, w_ple_gate, g_final, consts, masks,
                 y_prompt, y_sample, hg_prompt, ret_prompt, conv_prompt, hg_sample, ret_sample,
                 conv_sample, offs):
    fp, fr, u32 = mybir.dt.float32, mybir.dt.float32r, mybir.dt.uint32
    ALU, ACT = mybir.AluOpType, mybir.ActivationFunctionType
    MUL, ADD, SUB = ALU.mult, ALU.add, ALU.subtract
    KSCALE = float(128 ** -0.5)

    def tiles(w):
        return w[0].rearrange("(c p) (t n) -> p c t n", p=128, n=128)

    win_v, wbh_v, wbr_v, wout_v = tiles(w_in), tiles(w_br_hg), tiles(w_br_ret), tiles(w_out)
    wup_v, wdn_v, wpl_v, wpg_v = tiles(w_up), tiles(w_down), tiles(w_ple), tiles(w_ple_gate)
    COL = {n: i for n, i in zip(("hq", "hf", "hi", "hg", "rq", "rk", "rv", "rg"), range(0, 32, 4))}
    COL.update(ga=32, gb=40)
    xt_dram = nc.dram_tensor("x_transposed", [128, DC, TT], fp).ap()

    base = (nc.sbuf_base + 31) // 32 * 32

    def at(name, shape, off, dt=fp):
        size = 4
        for n in shape[1:]:
            size *= n
        assert off + size <= 212832, (name, off + size)
        return nc.alloc_sbuf_tensor_at(name, shape, dt, offset=base + off)

    class Region:
        def __init__(self, start, stop):
            self.at, self.stop = start, stop

        def __call__(self, name, shape, dt=fp):
            size = 4
            for n in shape[1:]:
                size *= n
            t = at(name, shape, self.at, dt)
            self.at += (size + 31) // 32 * 32
            assert self.at <= self.stop, (name, self.at, self.stop)
            return t

    r = Region(0, 33792)
    raw = [r(f"raw{i}", [128, WMAX]) for i in range(2)]
    whi = [r(f"whi{i}", [128, WMAX], fr) for i in range(2)]
    wlo = [r(f"wlo{i}", [128, WMAX], fr) for i in range(2)]
    r = Region(33792, 49152)
    NCST = consts.shape[1]
    cst = r("cst", [128, NCST])
    msk = r("msk", [128, LV * 64], u32)
    ones128 = r("ones128", [128, 128])
    ones1024 = r("ones1024", [128, 128])
    vc = r("vc", [128, 136])
    lbt = r("lbt", [128, 6, 4])
    eps = r("eps", [128, 1])
    ssx = r("ssx", [128, 8])
    ot = r("ot", [128, 512])
    ident = cst[:, offs["ident"]:offs["ident"] + 128]
    blk64 = cst[:, offs["blk64"]:offs["blk64"] + 128]
    headsel = cst[:, offs["headsel"]:offs["headsel"] + 2]
    cosT = cst[:, offs["cos"]:offs["cos"] + TT]
    sinT = cst[:, offs["sin"]:offs["sin"] + TT]
    decay = cst[:, offs["decay"]:offs["decay"] + 512]
    qdec = cst[:, offs["qdec"]:offs["qdec"] + 512]
    kdec = cst[:, offs["kdec"]:offs["kdec"] + 4]
    g128 = cst[:, offs["g128"]:offs["g128"] + 4]
    gam = cst[:, offs["gam"]:offs["gam"] + 4]
    r = Region(49152, 49152 + 33280)
    xah = r("xah", [128, DC, TT], fr)
    xal = r("xal", [128, DC, TT], fr)
    XA_END = 82432
    r = Region(XA_END, 212832)
    G0 = r.at
    fT = r("fT", [128, 4, TT])
    qT = r("qT", [128, 4, TT])
    qr = r("qr", [128, 4, TT])
    G1 = r.at
    lq = [r(f"lq{i}", [128, 4, CH]) for i in range(4)]
    lk = [r(f"lk{i}", [128, 4, CH]) for i in range(4)]
    qk = r("qk", [128, 4, CH])
    sfull = r("sfull", [128, 8, CH])
    khat = r("khat", [128, 512])
    vhg = r("vhg", [128, NCH, 512])
    v8h = r("v8h", [NS, 512])
    AG0 = r.at
    ghg = r("ghg", [128, 4, TT])
    AR0 = r.at
    kr = r("kr", [128, 4, TT])
    vr = r("vr", [128, NCH, 512])
    v8r = r("v8r", [NS, 512])
    grt = r("grt", [128, 4, TT])
    vst = r("vst", [128, 512])
    tl = [None] + [r(f"tl{i}", [128, 4, CH >> i]) for i in range(1, LV + 1)]
    sst = r("sst", [128, 4, 64])
    sq = r("sq", [128, 512])
    rs = r("rs", [128, 512])
    vblk = r("vblk", [NS, 1024])
    k8 = r("k8", [NS, 128])
    fs8 = r("fs8", [128, 8])
    ks8 = r("ks8", [128, 8])
    qs8 = r("qs8", [128, 8])
    sqs = r("sqs", [128, 64])
    rss = r("rss", [128, 64])
    smp = r("smp", [128, 2, 4, NS])
    one = r("one", [128, 1])
    T0 = r.at
    xs = [r(f"xs{i}", [128, TT]) for i in range(2)]
    hiT = r("hiT", [128, TT])
    sg = [r(f"sg{i}", [128, TT]) for i in range(2)]
    r = Region(T0, r.at)
    kst = r("kst", [128, 4, CH])
    qst = r("qst", [128, 4, CH])
    qd = r("qd", [128, 4, CH])
    prb = r("prb", [128, 4, CH])
    r = Region(T0 + 10400, 212832)
    ktk = at("ktk", [128, 512], r.at)
    sgf = r("sgf", [128, TT])
    rst = r("rst", [128, 4, 128])
    ss = at("ss", [128, 8, 64], r.at)
    rsm = r("rsm", [128, 8, 128])
    r = Region(G0, 212832)
    xtok = r("xtok", [128, 5, DM])
    xsc = r("xsc", [128, 5, DM])
    vrow = r("vrow", [128, 2, 128])
    xstg = at("xstg", [128, DC, TT], AR0)
    xsm = at("xsm", [128, DC, NS], AR0 + 16640 + 2048)
    gab = at("gab", [128, 2 * DC, TT], G1)
    assert G1 + 16 * TT * 4 <= AG0
    ahh = at("ahh", [128, 4, TT], G0 + 4 * TT * 4, fr)
    ahl = at("ahl", [128, 4, TT], G0, fr)
    arh = at("arh", [128, 4, TT], G0 + 8 * TT * 4, fr)
    arl = at("arl", [128, 4, TT], AG0, fr)
    A0, B0, H0 = 49152, 49152 + 91520, 49152 + 91520 + 33280
    r = Region(A0, B0)
    ach = r("ach", [128, FC, TT], fr)
    acl = r("acl", [128, FC, TT], fr)
    r = Region(B0, H0)
    xbh = r("xbh", [128, DC, TT], fr)
    xbl = r("xbl", [128, DC, TT], fr)
    r = Region(H0, 212832)
    hT = r("hT", [128, DC, TT])
    m1 = r("m1", [128, TT])
    m2 = r("m2", [128, TT])
    sqt = r("sqt", [128, TT])
    ssq = r("ssq", [128, TT])
    rstd = r("rstd", [128, TT])
    F0 = r.at
    ab = [r(f"ab{i}", [128, TT + 2]) for i in range(2)]
    cv = r("cv", [128, TT])
    gg = r("gg", [128, TT])
    part = r("part", [128, FC, NS])
    cs = at("cs", [128, FC, 10], H0 + 16640)
    stT = at("stT", [128, FC, 16], A0 + 40000)
    strow = at("strow", [16, FF], A0 + 48000)
    csr = at("csr", [10, FF], F0)
    r = Region(A0, B0)
    ptok = at("ptok", [128, 5, PD], F0)
    pxh = r("pxh", [128, 2, TT], fr)
    pxl = r("pxl", [128, 2, TT], fr)
    tg = r("tg", [128, TT])
    sgg = r("sgg", [128, TT])
    tp = r("tp", [128, TT])
    yT = r("yT", [128, DC, TT])
    ytok = r("ytok", [128, 5, DM])
    rt = r("rt", [128, 5])

    ctx = ExitStack()
    with ctx:
        def sem(name):
            return ctx.enter_context(nc.semaphore(name))

        acc = [ctx.enter_context(nc.psum_tensor(f"acc{i}", [128, 2, 512], fp)) for i in range(2)]
        lvb = ctx.enter_context(nc.psum_tensor("lvb", [128, 2, 512], fp))
        ob = ctx.enter_context(nc.psum_tensor("ob", [128, 512], fp))
        mb = ctx.enter_context(nc.psum_tensor("mb", [128, 512], fp))

        raw_loaded = [sem(f"raw_loaded{i}") for i in range(2)]
        hi_ready = sem("hi_ready")
        lo_ready = sem("lo_ready")
        part_done = sem("part_done")
        acc_free = [sem(f"acc_free{i}") for i in range(2)]
        lv_full = sem("lv_full")
        sc_full = sem("sc_full")
        merged = sem("merged")
        lv_free = [sem(f"lv_free{i}") for i in range(2)]
        misc_full = sem("misc_full")
        misc_free = sem("misc_free")
        const_loaded = sem("const_loaded")
        vec_loaded = sem("vec_loaded")
        x_loaded = sem("x_loaded")
        set_up = sem("set_up")
        x_sq = sem("x_sq")
        x_scaled = sem("x_scaled")
        xa_hi = sem("xa_hi")
        xa_lo = sem("xa_lo")
        vec_ready = sem("vec_ready")
        lb_exp = sem("lb_exp")
        xt_copied = sem("xt_copied")
        xt_stored = sem("xt_stored")
        sig_ready = sem("sig_ready")
        f_done = sem("f_done")
        swapped = sem("swapped")
        rot_done = sem("rot_done")
        prep = sem("prep")
        o_ready = sem("o_ready")
        v_full = sem("v_full")
        v_taken = sem("v_taken")
        smp_staged = sem("smp_staged")
        staged = sem("staged")
        outer_ready = sem("outer_ready")
        vst_ready = sem("vst_ready")
        sq_ready = sem("sq_ready")
        o_free = sem("o_free")
        a_done = sem("a_done")
        ss_loaded = sem("ss_loaded")
        ss_stored = sem("ss_stored")
        rsm_loaded = sem("rsm_loaded")
        rsm_stored = sem("rsm_stored")
        ret_o = sem("ret_o")
        smp_sq = sem("smp_sq")
        smp_done = sem("smp_done")
        ah_hi = sem("ah_hi")
        ah_lo = sem("ah_lo")
        h_loaded = sem("h_loaded")
        mix_sum = sem("mix_sum")
        mix_hi = sem("mix_hi")
        mix_lo = sem("mix_lo")
        h_new = sem("h_new")
        xb_hi = sem("xb_hi")
        xb_lo = sem("xb_lo")
        ssq_ready = sem("ssq_ready")
        rstd_ready = sem("rstd_ready")
        st_loaded = sem("st_loaded")
        c_first = sem("c_first")
        c_ready = sem("c_ready")
        gelu_ready = sem("gelu_ready")
        act_ready = sem("act_ready")
        ac_hi = sem("ac_hi")
        ac_lo = sem("ac_lo")
        cs_ready = sem("cs_ready")
        p_loaded = sem("p_loaded")
        p_hi = sem("p_hi")
        y_ready = sem("y_ready")
        rt_ready = sem("rt_ready")
        stored = sem("stored")
        pe_s, act_s, dve_s, pool_s = (sem(n) for n in ("pe_step", "act_step", "dve_step", "pool_step"))
        pe_passed, act_passed, dve_passed, pool_passed = (
            sem(n) for n in ("pe_passed", "act_passed", "dve_passed", "pool_passed"))

        def unit(sec, k, it):
            return it * 4 + (SEC[sec][0] + k)

        def parts(sec, k, it, per=4):
            return it * per + (SEC[sec][1] + k)

        def tidx(sec, k, it, per=4):
            return it * (per // 2) + (SEC[sec][2] + k) // 2

        def two(ap):
            return ap.rearrange("p (a b) -> p a b", a=2)

        def ps2(t, lo=0, hi=128):
            return acc[t % 2][lo:hi, :, 0:HT]

        def m4(ap):
            return ap.rearrange("p (a b) -> p a b", a=4)

        block = ctx.enter_context(nc.Block())


        @block.sync
        def _(sp):
            xp = x_prompt[0].rearrange("(i p) n -> p i n", p=128)
            for i in range(NCH):
                sp.dma_start(xtok[:, i, :], xp[:, i, :]).then_inc(x_loaded, 16)
            sp.dma_start(xtok[0:NS, 4, :], x_sample[:, 0, :]).then_inc(x_loaded, 16)

            def load(sec, k, it, srcs):
                u = unit(sec, k, it)
                sp.wait_ge(lo_ready, u + 1)
                if len(srcs) == 1:
                    n = (srcs[0].shape[1] + 1) // 2
                    srcs = [srcs[0][:, 0:n], srcs[0][:, n:]]
                at0 = 0
                for src in srcs:
                    n = src.shape[1]
                    dst = raw[k % 2][:, at0 * 128:(at0 + n) * 128].rearrange("p (c n) -> p c n", n=128)
                    sp.dma_start(dst, src).then_inc(raw_loaded[k % 2], 16)
                    at0 += n

            for sec, names in (("A", ("hq", "hf")), ("V", ("hi", "hg"))):
                with sp.Fori(0, 2) as it:
                    for k in range(4):
                        load(sec, k, it, [win_v[:, :, it * 2 + (COL[names[k % 2]] + k // 2), :]])
            sp.wait_ge(xt_copied, 9)
            sp.dma_start(xt_dram, xstg[:]).then_inc(xt_stored, 16)
            with sp.Fori(0, 4) as it:
                for k, n in enumerate(("rq", "rk", "rv", "rg")):
                    load("B", k, it, [win_v[:, :, it + COL[n], :]])
            with sp.Fori(0, 4) as it:
                for k in range(4):
                    load("C", k, it, [win_v[:, :, it * 2 + (COL["ga" if k % 2 == 0 else "gb"] + k // 2), :]])
            with sp.Fori(0, 2) as it:
                for k in range(4):
                    load("D", k, it, [wbh_v[:, :, it * 4 + k, :], wbr_v[:, :, it * 4 + k, :]])
            with sp.Fori(0, 2) as it:
                for k in range(4):
                    load("E", k, it, [wout_v[:, :, it * 4 + k, :]])
            with sp.Fori(0, 11) as it:
                for k in range(4):
                    load("F", k, it, [wup_v[:, :, it * 2 + (k // 2 + (0 if k % 2 == 0 else FC)), :]])
            with sp.Fori(0, 4) as it:
                for k in range(4):
                    load("G", k, it, [wdn_v[:, FC // 2 * (k % 2):FC // 2 * (k % 2 + 1), it * 2 + k // 2, :]])
            sp.wait_ge(misc_free, M_G + 6)
            sp.dma_start(conv_prompt[0, 0], csr[0:2, :]).then_inc(stored, 16)
            sp.dma_start(conv_sample[0, :, 1, :], csr[2:10, :]).then_inc(stored, 16)
            sp.dma_start(conv_sample[0, :, 0, :], state_conv[0, :, 1, :]).then_inc(stored, 16)
            sp.wait_ge(stored, 96)
            sp.dma_start(ptok[:, 0:NCH, :], p_prompt[0, 0].rearrange("(i p) n -> p i n", p=128)).then_inc(p_loaded, 16)
            sp.dma_start(ptok[0:NS, 4, :], p_sample[0, :, 0, :]).then_inc(p_loaded, 16)
            with sp.Fori(0, 2) as it:
                for k in range(4):
                    load("H", k, it, [wpg_v[:, :, it * 4 + k, :], wpl_v[:, :, it * 4 + k, :]])
            yp = y_prompt[0].rearrange("(i p) n -> p i n", p=128)
            for i in range(NCH):
                for b in range(2):
                    sp.wait_ge(lv_free[b], L_F // 2 + 3 + i)
                sp.dma_start(yp[:, i, :], ytok[:, i, :]).then_inc(stored, 16)
            for b in range(2):
                sp.wait_ge(lv_free[b], L_F // 2 + 7)
            sp.dma_start(y_sample[:, 0, :], ytok[0:NS, 4, :]).then_inc(stored, 16)
            sp.wait_ge(xt_stored, 16)
            sp.wait_ge(ss_stored, 80)
            sp.wait_ge(rsm_stored, 80)
            sp.wait_ge(stored, 16 * 11)

        @block.tensor
        def _(pe):
            def taken():
                pe.sem_inc(pe_passed, 1)

            step = Steps(pe, pe_s, taken)

            def level(n):
                return lvb[:, n % 2, :]

            def wait_level(base, k, it, per):
                pe.wait_ge(lv_free[k % 2], it * (per // 2) + (base + k) // 2)

            def wait_misc(base, k, it, per):
                pe.wait_ge(misc_free, it * per + (base + k))

            def product(sec, k, it, slot, tile, chunks, w0, xh, xl, first=True, last=True, tper=4,
                        wait_unit=True, chunk_wait=None):
                if wait_unit:
                    pe.wait_ge(hi_ready, unit(sec, k, it) + 1)
                    pe.wait_ge(lo_ready, unit(sec, k, it) + 3)
                if first:
                    pe.wait_ge(acc_free[tile % 2], tidx(sec, tile, it, tper))
                n = len(chunks)
                for i, c in enumerate(chunks):
                    if chunk_wait:
                        chunk_wait(c)
                    w = slice((w0 + i) * 128, (w0 + i + 1) * 128)
                    for q, (wt, xx) in enumerate(((whi, xh), (whi, xl), (wlo, xh))):
                        for b in range(2):
                            mm = pe.matmul(acc[tile % 2][:, b, 0:HT], wt[slot][:, w],
                                           xx[:, c, b * HT:(b + 1) * HT],
                                           start=first and i == 0 and q == 0,
                                           stop=last and i == n - 1 and q == 2)
                if last or len(chunks) > 4:
                    mm.then_inc(part_done, 1)

            C8 = range(DC)
            pe.wait_ge(const_loaded, 32)
            pe.wait_ge(vec_loaded, 16 * 12)
            pe.transpose(mb[:, 0:48], vrow[0:48, 0, :], ident[0:48, 0:48])
            pe.transpose(mb[:, 48:136], vrow[0:88, 1, :], ident[0:88, 0:88]).then_inc(misc_full, 1)
            pe.wait_ge(x_loaded, 80)
            pe.wait_ge(misc_free, 1)
            for j in range(DC):
                mm = pe.transpose(mb[:, j * 8:j * 8 + 8], xtok[0:NS, 4, j * 128:(j + 1) * 128],
                                  ident[0:NS, 0:NS])
            mm.then_inc(misc_full, 1)
            pe.wait_ge(x_scaled, 5)
            pe.wait_ge(misc_free, 2)
            for j in range(DC):
                mm = pe.transpose(mb[:, j * 8:j * 8 + 8], xsc[0:NS, 4, j * 128:(j + 1) * 128],
                                  ident[0:NS, 0:NS])
            mm.then_inc(misc_full, 1)
            for n in range(2 * DC):
                j, src = n % DC, xsc if n < DC else xtok
                pe.wait_ge(lv_free[n % 2], n // 2)
                for i in range(NCH):
                    mm = pe.transpose(level(n)[:, i * 128:(i + 1) * 128],
                                      src[:, i, j * 128:(j + 1) * 128], ident)
                mm.then_inc(lv_full, 1)
            pe.wait_ge(xa_lo, 1)

            pe.sem_inc(v_full, 1)
            with pe.Fori(0, 2) as it:
                for k in range(4):
                    product("A", k, it, k % 2, k, C8, 0, xah, xal)
            with pe.Fori(0, 2) as it:
                for k in range(4):
                    product("V", k, it, k % 2, k, C8, 0, xah, xal)
                    if k % 2:
                        pe.wait_ge(acc_free[0], tidx("V", k - 1, it) + 1)
                        wait_misc(M_A, k - 1, it, 4)
                        for i in range(NCH):
                            mm = pe.transpose(mb[:, i * 128:(i + 1) * 128], hiT[:, i * 128:(i + 1) * 128], ident)
                        mm.then_inc(misc_full, 1)
                        wait_misc(M_A, k, it, 4)
                        pe.transpose(mb[0:NS, 0:128], hiT[:, NT:TT], ident).then_inc(misc_full, 1)

            def head(t, h, cols=slice(None)):
                return t[64 * (h % 2):64 * (h % 2) + 64, h // 2, cols]

            def scores(use, it):
                levels = [l for l in (2 * use, 2 * use + 1) if l < LV]
                pe.wait_ge(prep, it * 8 + levels[-1] + 1)
                pe.wait_ge(merged, it * MERGES + (4 * use + 1))
                taken()
                if use == 3:
                    for c in range(4):
                        pe.matmul(lvb[:, 0, 256 + 2 * c:258 + 2 * c], qk[:, c, :], headsel,
                                  start=True, stop=True)
                for l in levels:
                    hb = 1 << l
                    for h in range(8):
                        q2 = head(lq[l % 4], h).rearrange("k (b two h) -> k b two h", two=2, h=hb)[:, :, 1, :]
                        c0 = 256 * (l % 2) + 64 * (h // 2)
                        out = lvb[:, h % 2, c0:c0 + 64].rearrange("s (b h) -> s b h", h=hb)
                        mm = pe.matmul(out, head(lk[l % 4], h), q2, start=True, stop=True)
                mm.then_inc(sc_full, 1)

            def halves(k, it, between):
                product("B", k, it, k % 2, k, range(4), 0, xah, xal, last=False)
                between()
                product("B", k, it, k % 2, k, range(4, 8), 4, xah, xal, first=False, wait_unit=False)

            with pe.Fori(0, 4) as it:
                step.loop(it, 1)
                pe.wait_ge(v_taken, it * 2 + 1)
                halves(0, it, lambda: scores(0, it))
                scores(1, it)
                pe.wait_ge(smp_staged, it + 1)
                wait_misc(M_B, 0, it, 6)
                pe.transpose(mb[0:NS, 0:128], ks8[:], ident).then_inc(misc_full, 1)

                halves(1, it, lambda: scores(2, it))
                scores(3, it)
                pe.wait_ge(prep, it * 8 + 8)
                wait_misc(M_B, 1, it, 6)
                for c in range(4):
                    mm = pe.transpose(mb[:, c * 128:(c + 1) * 128], lk[3][:, c, :], ident)
                mm.then_inc(misc_full, 1)

                def sample_outer():
                    pe.wait_ge(outer_ready, it + 1)
                    wait_misc(M_B, 2, it, 6)
                    taken()
                    for h2 in range(2):
                        mm = pe.matmul(mb[64 * h2:64 * h2 + 64, :], k8[:, 64 * h2:64 * h2 + 64],
                                       vblk[:, 512 * h2:512 * h2 + 512], start=True, stop=True)
                    mm.then_inc(misc_full, 1)

                halves(2, it, sample_outer)
                pe.wait_ge(merged, it * MERGES + (MERGES + 1))
                pe.wait_ge(vst_ready, it + 1)
                pe.wait_ge(o_free, it + 1)
                wait_misc(M_B, 3, it, 6)
                for h in range(8):
                    out = ob[64 * (h % 2):64 * (h % 2) + 64, (h // 2) * 128:(h // 2 + 1) * 128]
                    pe.matmul(out, vst[:, h * 64:(h + 1) * 64], sfull[:, h, :], start=True, stop=False)
                    mm = pe.matmul(out, head(sst, h), head(lq[3], h), start=False, stop=True)
                mm.then_inc(o_ready, 1)
                for h in range(8):
                    mm = pe.matmul(mb[64 * (h % 2):64 * (h % 2) + 64, (h // 2) * 64:(h // 2 + 1) * 64],
                                   khat[:, h * 64:(h + 1) * 64], vst[:, h * 64:(h + 1) * 64],
                                   start=True, stop=True)
                mm.then_inc(misc_full, 1)

                def head_squares():
                    pe.wait_ge(sq_ready, it + 1)
                    wait_misc(M_B, 4, it, 6)
                    pe.matmul(mb[:], blk64, sq[:], start=True, stop=True).then_inc(misc_full, 1)

                halves(3, it, head_squares)
                wait_misc(M_B, 5, it, 6)
                taken()
                for h2 in range(2):
                    for b in range(NS):
                        mm = pe.matmul(mb[64 * h2:64 * h2 + 64, b:b + 1], ss[64 * h2:64 * h2 + 64, b, :],
                                       qs8[64 * h2:64 * h2 + 64, b:b + 1], start=True, stop=True)
                    if h2 == 0:
                        step(mm)
                mm.then_inc(misc_full, 1)
                pe.wait_ge(acc_free[0], tidx("B", 2, it) + 1)
                for i in range(NCH):
                    mm = pe.transpose(lvb[:, 0, i * 128:(i + 1) * 128], hiT[:, i * 128:(i + 1) * 128], ident)
                mm.then_inc(v_full, 1)
                pe.transpose(lvb[0:NS, 1, 0:128], hiT[:, NT:TT], ident).then_inc(v_full, 1)
            step.end(4)
            pe.wait_ge(v_taken, 9)

            with pe.Fori(0, 4) as it:
                product("C", 0, it, 0, 0, C8, 0, xah, xal)
                pe.wait_ge(staged, it * 2 + 1)
                pe.wait_ge(vst_ready, it + 5)
                wait_level(L_C, 0, it, 4)
                for h in range(4):
                    mm = pe.matmul(level(0)[:, h * 128:(h + 1) * 128], kst[:, h, :], qst[:, h, :],
                                   start=True, stop=True)
                mm.then_inc(lv_full, 1)
                wait_level(L_C, 1, it, 4)
                for h in range(4):
                    mm = pe.transpose(level(1)[:, h * 128:(h + 1) * 128], kst[:, h, :], ident)
                mm.then_inc(lv_full, 1)
                pe.wait_ge(smp_staged, it + 5)
                wait_misc(M_C, 0, it, 4)
                pe.transpose(mb[0:NS, 0:128], ks8[:], ident).then_inc(misc_full, 1)

                product("C", 1, it, 1, 1, C8, 0, xah, xal)
                for b in range(2):
                    pe.wait_ge(lv_free[b], it * 2 + L_C // 2 + 1)
                pe.wait_ge(o_free, it + 5)
                pe.wait_ge(staged, it * 2 + 2)
                for h in range(4):
                    out = ob[:, h * 128:(h + 1) * 128]
                    pe.matmul(out, vst[:, h * 128:(h + 1) * 128], prb[:, h, :], start=True, stop=False)
                    mm = pe.matmul(out, rst[:, h, :], qd[:, h, :], start=False, stop=True)
                mm.then_inc(ret_o, 1)
                wait_misc(M_C, 1, it, 4)
                for h in range(4):
                    mm = pe.matmul(mb[:, h * 128:(h + 1) * 128], ktk[:, h * 128:(h + 1) * 128],
                                   vst[:, h * 128:(h + 1) * 128], start=True, stop=True)
                mm.then_inc(misc_full, 1)
                pe.wait_ge(outer_ready, it + 5)
                for b in range(2):
                    wait_level(L_C, 2 + b, it, 4)
                    pe.matmul(level(b), k8[:], vblk[:, 512 * b:512 * b + 512],
                              start=True, stop=True).then_inc(lv_full, 1)

                product("C", 2, it, 0, 2, range(4), 0, xah, xal, last=False)
                pe.wait_ge(sq_ready, it + 5)
                wait_misc(M_C, 2, it, 4)
                pe.matmul(mb[:], ones128[:], sq[:], start=True, stop=True).then_inc(misc_full, 1)
                product("C", 2, it, 0, 2, range(4, 8), 4, xah, xal, first=False, wait_unit=False)
                wait_misc(M_C, 3, it, 4)
                for b in range(2):
                    pe.wait_ge(lv_free[b], it * 2 + L_C // 2 + 2)
                for b in range(NS):
                    mm = pe.matmul(mb[:, b:b + 1], rsm[:, b, :], qs8[:, b:b + 1], start=True, stop=True)
                mm.then_inc(misc_full, 1)

                product("C", 3, it, 1, 3, C8, 0, xah, xal)

            pe.wait_ge(smp_sq, 2)
            wait_misc(M_R, 0, 0, 0)
            pe.matmul(mb[:, 0:32], blk64, sqs[:, 0:32], start=True, stop=True)
            pe.matmul(mb[:, 32:64], ones128[:], sqs[:, 32:64], start=True, stop=True).then_inc(misc_full, 1)
            pe.wait_ge(ah_lo, 11)
            with pe.Fori(0, 2) as it:
                for k in range(4):
                    product("D", k, it, k % 2, 2 * k, range(4), 0, ahh, ahl, tper=8)
                    product("D", k, it, k % 2, 2 * k + 1, range(4), 4, arh, arl, tper=8, wait_unit=False)

            with pe.Fori(0, 2) as it:
                for k in range(4):
                    product("E", k, it, k % 2, k, C8, 0, xah, xal,
                            chunk_wait=(lambda c: pe.wait_ge(mix_lo, c + 2)) if k == 0 else None)

            def mean_square(n):
                pe.wait_ge(ssq_ready, 8 * (n + 1) + 1)
                for b in range(2):
                    pe.wait_ge(lv_free[b], L_F // 2 + n)
                    pe.matmul(lvb[:, b, 0:HT], ones1024[:], ssq[:, b * HT:(b + 1) * HT],
                              start=True, stop=True).then_inc(lv_full, 1)

            pe.wait_ge(st_loaded, 16)
            wait_misc(M_F, 0, 0, 0)
            for j in range(FC):
                mm = pe.transpose(mb[:, j * 16:(j + 1) * 16], strow[:, j * 128:(j + 1) * 128],
                                  ident[0:16, 0:16])
            mm.then_inc(misc_full, 1)
            mean_square(0)
            pe.wait_ge(xb_lo, 8)
            with pe.Fori(0, 11) as it:
                for k in range(4):
                    product("F", k, it, k % 2, k, C8, 0, xbh, xbl)

            pe.wait_ge(cs_ready, FC)
            for n in range(6):
                wait_misc(M_G, n, 0, 0)
                for j in range(4 * n, min(4 * n + 4, FC)):
                    mm = pe.transpose(mb[0:10, (j % 4) * 128:(j % 4 + 1) * 128], cs[:, j, :], ident)
                mm.then_inc(misc_full, 1)
            pe.wait_ge(ac_lo, FC + 1)
            with pe.Fori(0, 4) as it:
                for k in range(4):
                    product("G", k, it, k % 2, k // 2, range(11 * (k % 2), 11 * (k % 2) + 11), 0, ach, acl,
                            first=k % 2 == 0, last=k % 2 == 1, tper=2)
            pe.wait_ge(p_loaded, 32)
            for j in range(2):
                wait_misc(M_G + 6, 2 * j, 0, 0)
                for i in range(NCH):
                    mm = pe.transpose(mb[:, i * 128:(i + 1) * 128], ptok[:, i, j * 128:(j + 1) * 128], ident)
                mm.then_inc(misc_full, 1)
                wait_misc(M_G + 6, 2 * j + 1, 0, 0)
                pe.transpose(mb[:, 0:NS], ptok[0:NS, 4, j * 128:(j + 1) * 128],
                             ident[0:NS, 0:NS]).then_inc(misc_full, 1)
            mean_square(1)
            pe.wait_ge(xb_lo, 16)
            pe.wait_ge(misc_free, M_G + 10)
            with pe.Fori(0, 2) as it:
                for k in range(4):
                    product("H", k, it, k % 2, 2 * k, C8, 0, xbh, xbl, tper=8)
                    product("H", k, it, k % 2, 2 * k + 1, range(2), 8, pxh, pxl, tper=8, wait_unit=False)

            pe.wait_ge(ssq_ready, 25)
            wait_misc(M_G + 10, 0, 0, 0)
            for i in range(5):
                n = 128 if i < 4 else NS
                mm = pe.matmul(mb[0:n, i:i + 1], ssq[:, i * 128:i * 128 + n], ones1024[:, 0:1],
                               start=True, stop=True)
            mm.then_inc(misc_full, 1)
            pe.wait_ge(y_ready, 8)
            for i in range(5):
                n = 128 if i < 4 else NS
                for half in range(2):
                    u = 2 * i + half
                    pe.wait_ge(lv_free[u % 2], L_F // 2 + 2 + u // 2)
                    for j in range(4 * half, 4 * half + 4):
                        mm = pe.transpose(lvb[0:n, u % 2, (j % 4) * 128:(j % 4 + 1) * 128],
                                          yT[:, j, i * 128:i * 128 + n], ident)
                    mm.then_inc(lv_full, 1)

        @block.scalar
        def _(act):
            step = Steps(act, act_s)
            act.sem_inc(ss_stored, 16)
            act.sem_inc(rsm_stored, 16)

            def taken():
                act.sem_inc(act_passed, 1)

            def hi(sec, k, it, size=None):
                act.wait_ge(raw_loaded[k % 2], it * 64 + 32 * ((SEC[sec][0] + k) // 2 + 1))
                n = size or SIZE[sec]
                act.activation(whi[k % 2][:, 0:n], raw[k % 2][:, 0:n], ACT.Copy).then_inc(hi_ready, 1)

            def done(sec, k, it, per=4):
                act.wait_ge(part_done, parts(sec, k, it, per) + 1)

            def ahead(sec, k, it, nxt=None):
                if k < 2:
                    hi(sec, k + 2, it)
                elif nxt is None:
                    hi(sec, k - 2, it + 1)
                else:
                    hi(nxt, k - 2, 0)

            for src, row in ((lb_logits[0], 0), (lb_logits[1], 4)):
                act.dma_start(vrow[row:row + 4, 0, :], src.rearrange("(c p) -> c p", p=128)).then_inc(vec_loaded, 16)
            for src, row in ((g_mix[0], 8), (g_ffn[0], 16), (g_ple[0], 24), (g_final, 32),
                             (g_hg_out[0], 40), (g_ret_out[0], 44)):
                n = src.shape[0] // 128
                act.dma_start(vrow[row:row + n, 0, :], src.rearrange("(c p) -> c p", p=128)).then_inc(vec_loaded, 16)
            act.dma_start(cst[:], consts).then_inc(const_loaded, 16)
            for i in range(3):
                act.dma_start(vrow[22 * i:22 * i + 22, 1, :],
                              conv_w[0, i].rearrange("(c p) -> c p", p=128)).then_inc(vec_loaded, 16)
            act.dma_start(vrow[66:88, 1, :], conv_b[0].rearrange("(c p) -> c p", p=128)).then_inc(vec_loaded, 16)
            act.dma_start(msk[:], masks).then_inc(const_loaded, 16)
            act.wait_ge(x_loaded, 80)
            act.wait_ge(set_up, 6)
            for i in range(5):
                n = 128 if i < 4 else NS
                act.activation(xsc[0:n, i, :], xtok[0:n, i, :], ACT.Square,
                               accum_out=ssx[0:n, i:i + 1]).then_inc(x_sq, 1)
            act.wait_ge(x_sq, 5)
            step(act.activation(ssx[:, 0:5], ssx[:, 0:5], ACT.Sqrt, bias=eps[:], scale=1.0 / DM))
            hi("A", 0, 0)
            hi("A", 1, 0)
            act.wait_ge(vec_ready, 1)
            act.activation(lbt[:, 1:3, :], lbt[:, 1:3, :], ACT.Exp).then_inc(lb_exp, 1)
            act.wait_ge(misc_full, 2)
            act.activation(xstg[:, :, NT:TT], mb[:, 0:64].rearrange("p (a b) -> p a b", b=NS),
                           ACT.Copy).then_inc(misc_free, 1)
            act.wait_ge(misc_free, 2)
            act.sem_inc(xt_copied, 1)
            for j in range(DC):
                act.wait_ge(lv_full, j + 1)
                act.activation(xah[:, j, 0:NT], lvb[:, j % 2, :], ACT.Copy,
                               scale=vc[:, 8 + j:9 + j]).then_inc(xa_hi, 1)
            act.wait_ge(misc_free, 3)
            act.activation(xah[:, :, NT:TT], xsm[:], ACT.Copy).then_inc(xa_hi, 1)
            for j in range(DC):
                act.wait_ge(lv_full, DC + j + 1)
                act.activation(xstg[:, j, 0:NT], lvb[:, j % 2, :], ACT.Copy).then_inc(lv_free[j % 2], 1)
            act.wait_ge(lv_free[0], 8)
            act.wait_ge(lv_free[1], 8)
            act.sem_inc(xt_copied, 8)

            act.sem_inc(v_taken, 1)
            with act.Fori(0, 2) as it:
                for k in range(4):
                    done("A", k, it)
                    ahead("A", k, it)
                    if k % 2 == 0:
                        act.activation(two(sg[k // 2][:]), ps2(0), ACT.Sigmoid).then_inc(sig_ready, 1)
                    else:
                        act.wait_ge(f_done, it * 2 + (k // 2 + 1))
                        act.activation(two(sgf[:]), ps2(1), ACT.Sigmoid).then_inc(acc_free[1], 1)
            with act.Fori(0, 2) as it:
                for k in range(4):
                    done("V", k, it)
                    ahead("V", k, it)
                    if k % 2 == 0:
                        act.wait_ge(misc_full, it * 4 + (M_A + k))
                        act.activation(two(hiT[:]), ps2(0), ACT.Copy).then_inc(acc_free[0], 1)
                    else:
                        act.activation(two(sg[k // 2][:]), ps2(1), ACT.Sigmoid).then_inc(sig_ready, 1)
                        act.wait_ge(misc_full, it * 4 + (M_A + k))
                        taken()
                        cols = bass.ds(it * 256 + 128 * (k // 2), 128)
                        act.activation(vhg[:, :, cols], m4(mb[:]), ACT.Copy).then_inc(misc_free, 1)
                        act.wait_ge(misc_full, it * 4 + (M_A + k + 1))
                        taken()
                        act.activation(v8h[:, cols], mb[0:NS, 0:128], ACT.Copy).then_inc(misc_free, 1)

            def chunk(t, c):
                return t[:, :, bass.ds(c * CH, CH)]

            def branch_hi(t, it, n):
                act.wait_ge(a_done, it + (n + 1))
                taken()
                act.activation(chunk(t, it), m4(ot[:]), ACT.Copy).then_inc(ah_hi, 1)

            act.wait_ge(misc_free, M_B)
            with act.Fori(0, 4) as it:
                act.wait_ge(misc_full, it * 6 + (M_B - 2))
                taken()
                act.activation(vst[:], vhg[:, it, :], ACT.Copy).then_inc(vst_ready, 1)
                act.wait_ge(ss_stored, it * 16 + 16)
                act.wait_ge(misc_full, it * 6 + M_B)
                taken()
                act.dma_start(ss[:], state_hgrn[0].rearrange("b (c two) k v -> (two k) c b v", two=2)[:, it])\
                    .then_inc(ss_loaded, 16)
                for k, scale in ((0, 1.0), (1, KSCALE)):
                    done("B", k, it)
                    ahead("B", k, it)
                    act.wait_ge(rot_done, it * 2 + (k + 1))
                    for a, b in ((0, 64), (64, 0)):
                        act.activation(two(xs[k][a:a + 64, :]), ps2(k, b, b + 64), ACT.Copy,
                                       scale=scale).then_inc(swapped, 1)
                    if k == 0:
                        act.wait_ge(misc_full, it * 6 + (M_B + 1))
                        act.activation(k8[:], mb[0:NS, 0:128], ACT.Copy).then_inc(misc_free, 1)
                    else:
                        act.wait_ge(misc_full, it * 6 + (M_B + 2))
                        act.activation(khat[:], mb[:], ACT.Copy).then_inc(misc_free, 1)
                done("B", 2, it)
                ahead("B", 2, it)
                act.wait_ge(v_full, it * 2 + 1)
                act.activation(two(hiT[:]), ps2(2), ACT.Copy).then_inc(acc_free[0], 1)
                act.wait_ge(misc_free, it * 6 + (M_B + 3))
                taken()
                act.dma_start(hg_sample[0].rearrange("b (c two) k v -> (two k) c b v", two=2)[:, it], ss[:])\
                    .then_inc(ss_stored, 16)
                act.wait_ge(o_ready, it + 1)
                act.activation(sq[:], ob[:], ACT.Square).then_inc(sq_ready, 1)
                act.wait_ge(misc_full, it * 6 + (M_B + 5))
                act.activation(rs[:], mb[:], ACT.Sqrt, bias=eps[:]).then_inc(misc_free, 1)
                done("B", 3, it)
                ahead("B", 3, it)
                act.activation(two(sg[1][:]), ps2(3), ACT.Sigmoid).then_inc(sig_ready, 1)
                act.wait_ge(v_full, it * 2 + 2)
                taken()
                act.activation(vr[:, :, bass.ds(it * 128, 128)], m4(lvb[:, 0, :]), ACT.Copy).then_inc(v_taken, 1)
                act.wait_ge(v_full, it * 2 + 3)
                taken()
                act.activation(v8r[:, bass.ds(it * 128, 128)], lvb[0:NS, 1, 0:128], ACT.Copy).then_inc(v_taken, 1)
                branch_hi(ahh, it, 0)

            act.wait_ge(rot_done, 9)
            act.wait_ge(v_taken, 9)
            with act.Fori(0, 4) as it:
                act.wait_ge(misc_full, it * 4 + (M_C - 2))
                taken()
                act.activation(kst[:], chunk(kr, it), ACT.Copy)
                act.activation(vst[:], vr[:, it, :], ACT.Copy).then_inc(vst_ready, 1)
                act.wait_ge(rsm_stored, it * 16 + 16)
                act.wait_ge(misc_full, it * 4 + M_C)
                taken()
                act.dma_start(rsm[:], state_ret[0].rearrange("b h d v -> h d b v")[it]).then_inc(rsm_loaded, 16)
                for k in range(4):
                    done("C", k, it)
                    ahead("C", k, it)
                    act.activation(two(gab[:, it * 2 + (k // 2 + DC * (k % 2)), :]), ps2(k),
                                   ACT.Sigmoid).then_inc(acc_free[k % 2], 1)
                    if k == 0:
                        act.wait_ge(misc_full, it * 4 + (M_C + 1))
                        act.activation(k8[:], mb[0:NS, 0:128], ACT.Copy).then_inc(misc_free, 1)
                    if k == 1:
                        act.wait_ge(ret_o, it + 1)
                        act.activation(sq[:], ob[:], ACT.Square).then_inc(sq_ready, 1)
                        act.wait_ge(misc_full, it * 4 + (M_C + 3))
                        act.activation(rs[:], mb[:], ACT.Sqrt, bias=eps[:]).then_inc(misc_free, 1)
                        act.wait_ge(lv_free[1], it * 2 + (L_C // 2 + 2))
                        taken()
                        act.dma_start(ret_sample[0].rearrange("b h d v -> h d b v")[it], rsm[:])\
                            .then_inc(rsm_stored, 16)
                branch_hi(arh, it, 4)

            act.wait_ge(misc_full, M_R + 1)
            act.activation(rss[:], mb[:, 0:64], ACT.Sqrt, bias=eps[:]).then_inc(misc_free, 1)
            act.wait_ge(smp_done, 1)
            for i, t in enumerate((ahh, arh)):
                act.activation(t[:, :, NT:TT], smp[:, i], ACT.Copy).then_inc(ah_hi, 1)
            for h2 in range(2):
                act.dma_start(hg_prompt[0, 0].rearrange("(c two) k v -> two k c v", two=2)[h2],
                              sst[64 * h2:64 * h2 + 64]).then_inc(stored, 16)
            act.dma_start(ret_prompt[0, 0].rearrange("h d v -> d h v"), rst[:]).then_inc(stored, 16)
            act.wait_ge(stored, 48)
            act.wait_ge(rsm_stored, 80)
            act.wait_ge(xt_stored, 16)
            act.wait_ge(ah_lo, 11)
            act.dma_start(hT[:], xt_dram).then_inc(h_loaded, 16)

            with act.Fori(0, 2) as it:
                for k in range(4):
                    done("D", 2 * k + 1, it, 8)
                    ahead("D", k, it)
                    act.wait_ge(mix_sum, it * 4 + (k + 1))
                    taken()
                    act.activation(xah[:, it * 4 + k, :], m1[:], ACT.Copy).then_inc(mix_hi, 1)

            act.dma_start(strow[:], state_conv[0].rearrange("b w n -> (b w) n")).then_inc(st_loaded, 16)

            def residual(sec, tile, it, per, gain):
                j = it * per + tile
                act.wait_ge(acc_free[tile % 2], tidx(sec, tile, it, per) + 1)
                taken()
                act.activation(xbh[:, j, :], hT[:, j, :], ACT.Copy,
                               scale=vc[:, bass.ds(j + gain, 1)]).then_inc(xb_hi, 1)

            def inverse_rms(n):
                act.wait_ge(lv_full, L_TOTAL + 2 * n + 2)
                for b in range(2):
                    act.activation(rstd[:, b * HT:(b + 1) * HT], lvb[:, b, 0:HT], ACT.Sqrt,
                                   bias=eps[:]).then_inc(lv_free[b], 1)

            with act.Fori(0, 2) as it:
                for k in range(4):
                    done("E", k, it)
                    ahead("E", k, it)
                    residual("E", k, it, 4, 16)

            act.wait_ge(misc_full, M_F + 1)
            act.activation(stT[:].rearrange("p a b -> p (a b)"), mb[:, 0:FC * 16], ACT.Copy).then_inc(misc_free, 1)
            inverse_rms(0)

            def ffn(it, nxt=None):
                for k in range(4):
                    done("F", k, it)
                    ahead("F", k, it, nxt)
                    if k % 2 == 0:
                        act.wait_ge(acc_free[0], tidx("F", k, it) + 1)
                        act.wait_ge(act_ready, it * 2 + (k // 2 + 1))
                        taken()
                        act.activation(cv[:, 0:NT], ab[k // 2][:, 0:NT], ACT.Identity,
                                       scale=vc[:, bass.ds(it * 2 + (48 + k // 2), 1)],
                                       bias=vc[:, bass.ds(it * 2 + (48 + 3 * FC + k // 2), 1)]).then_inc(c_first, 1)
                        act.wait_ge(c_ready, it * 2 + (k // 2 + 1))
                        act.activation(cv[:], cv[:], ACT.Gelu_apprx_tanh).then_inc(gelu_ready, 1)
                    else:
                        act.wait_ge(act_ready, it * 2 + (k // 2 + 2))
                        taken()
                        act.activation(ach[:, it * 2 + k // 2, :], gg[:], ACT.Copy).then_inc(ac_hi, 1)

            with act.Fori(0, 10) as it:
                ffn(it)
            ffn(10, "G")
            act.wait_ge(ac_lo, FC + 1)
            for n in range(6):
                w = 512 if n < 5 else 256
                act.wait_ge(misc_full, M_G + n + 1)
                act.activation(csr[:, n * 512:n * 512 + w], mb[0:10, 0:w], ACT.Copy).then_inc(misc_free, 1)

            def down(it, nxt=None):
                for k in range(4):
                    done("G", k, it)
                    ahead("G", k, it, nxt)
                    if k % 2:
                        residual("G", k // 2, it, 2, 24)

            with act.Fori(0, 3) as it:
                down(it)
            down(3, "H")
            for j in range(2):
                act.wait_ge(misc_full, M_G + 6 + 2 * j + 1)
                act.activation(pxh[:, j, 0:NT], mb[:], ACT.Copy).then_inc(p_hi, 1)
                act.wait_ge(misc_full, M_G + 6 + 2 * j + 2)
                act.activation(pxh[:, j, NT:TT], mb[:, 0:NS], ACT.Copy).then_inc(p_hi, 1)
            inverse_rms(1)

            def embed(it, last=False):
                for k in range(4):
                    done("H", 2 * k, it, 8)
                    act.wait_ge(acc_free[0], tidx("H", 2 * k, it, 8) + 1)
                    act.activation(sgg[:], tg[:], ACT.Sigmoid).then_inc(sig_ready, 1)
                    done("H", 2 * k + 1, it, 8)
                    if k < 2 or not last:
                        ahead("H", k, it)
                    act.wait_ge(h_new, it * 4 + (k + 2))
                    taken()
                    act.activation(yT[:, it * 4 + k, :], hT[:, it * 4 + k, :], ACT.Copy,
                                   scale=vc[:, bass.ds(it * 4 + (32 + k), 1)]).then_inc(y_ready, 1)

            embed(0)
            embed(1, last=True)
            act.wait_ge(misc_full, M_G + 11)
            act.activation(rt[:, 0:4], mb[:, 0:4], ACT.Sqrt, bias=eps[:])
            act.activation(rt[0:NS, 4:5], mb[0:NS, 4:5], ACT.Sqrt, bias=eps[0:NS]).then_inc(misc_free, 1)
            act.wait_ge(rt_ready, 1)
            for u in range(0, 10, 2):
                n = 128 if u < 8 else NS
                act.wait_ge(lv_full, L_TOTAL + 4 + u + 1)
                act.activation(ytok[0:n, u // 2, 0:512], lvb[0:n, 0, :], ACT.Copy,
                               scale=rt[0:n, u // 2:u // 2 + 1]).then_inc(lv_free[0], 1)

        @block.vector
        def _(dve):
            def taken():
                dve.sem_inc(dve_passed, 1)

            step = Steps(dve, dve_s)
            dve.sem_inc(lo_ready, 2)
            for first in (*acc_free, rot_done, f_done, merged, o_free, ah_lo, mix_lo, ac_lo, h_new):
                dve.sem_inc(first, 1)

            def lo(sec, k, it):
                dve.wait_ge(hi_ready, unit(sec, k, it) + 1)
                n = SIZE[sec]
                dve.tensor_tensor(wlo[k % 2][:, 0:n], raw[k % 2][:, 0:n], whi[k % 2][:, 0:n].bitcast(fp),
                                  SUB).then_inc(lo_ready, 1)

            def done(sec, k, it, per=4):
                dve.wait_ge(part_done, parts(sec, k, it, per) + 1)

            def ahead(sec, k, it, nxt=None):
                if k < 2:
                    lo(sec, k + 2, it)
                elif nxt is None:
                    lo(sec, k - 2, it + 1)
                else:
                    lo(nxt, k - 2, 0)

            dve.wait_ge(misc_full, 1)
            dve.tensor_copy(vc[:], mb[:, 0:136]).then_inc(misc_free, 1)
            dve.wait_ge(misc_free, 1)
            step(dve.tensor_tensor(lbt[:, 0, :], vc[:, 0:4], vc[:, 4:8], ALU.max))
            step(dve.tensor_tensor(lbt[:, 1, :], vc[:, 0:4], lbt[:, 0, :], SUB))
            dve.tensor_tensor(lbt[:, 2, :], vc[:, 4:8], lbt[:, 0, :], SUB).then_inc(vec_ready, 1)
            dve.wait_ge(act_s, 1)
            step(dve.reciprocal(ssx[:, 0:5], ssx[:, 0:5]))
            for i in range(5):
                n = 128 if i < 4 else NS
                dve.tensor_scalar(xsc[0:n, i, :], xtok[0:n, i, :], ssx[0:n, i:i + 1], None,
                                  MUL).then_inc(x_scaled, 1)
            lo("A", 0, 0)
            lo("A", 1, 0)
            dve.wait_ge(lb_exp, 1)
            step(dve.tensor_tensor(lbt[:, 5, :], lbt[:, 1, :], lbt[:, 2, :], ADD))
            step(dve.reciprocal(lbt[:, 5, :], lbt[:, 5, :]))
            step(dve.tensor_tensor(lbt[:, 3, :], lbt[:, 1, :], lbt[:, 5, :], MUL))
            step(dve.tensor_scalar(lbt[:, 4, :], lbt[:, 3, :], -1.0, 1.0, MUL, ADD))
            dve.wait_ge(misc_full, 3)
            dve.tensor_tensor(xsm[:], mb[:, 0:64].rearrange("p (a b) -> p a b", b=NS),
                              vc[:, 8:16].unsqueeze(2).broadcast_to([128, DC, NS]), MUL).then_inc(misc_free, 1)
            for j in range(DC):
                dve.wait_ge(xa_hi, j + 1)
                dve.scalar_tensor_tensor(xal[:, j, 0:NT], lvb[:, j % 2, :], vc[:, 8 + j:9 + j],
                                         xah[:, j, 0:NT].bitcast(fp), MUL, SUB).then_inc(lv_free[j % 2], 1)
            dve.wait_ge(xa_hi, 9)
            dve.tensor_tensor(xal[:, :, NT:TT], xsm[:], xah[:, :, NT:TT].bitcast(fp), SUB).then_inc(xa_lo, 1)

            with dve.Fori(0, 2) as it:
                for k in range(4):
                    done("A", k, it)
                    ahead("A", k, it)
                    j = it * 2 + k // 2
                    if k % 2 == 0:
                        dve.wait_ge(sig_ready, it * 2 + (k // 2 + 1))
                        dve.tensor_tensor(two(qT[:, j, :]), ps2(0), two(sg[k // 2][:]), MUL).then_inc(acc_free[0], 1)
                    else:
                        dve.wait_ge(acc_free[1], tidx("A", k, it) + 1)
                        dve.tensor_scalar(fT[:, j, :], sgf[:], lbt[:, 4, bass.ds(it * 2 + k // 2, 1)],
                                          lbt[:, 3, bass.ds(it * 2 + k // 2, 1)], MUL, ADD).then_inc(f_done, 1)
            with dve.Fori(0, 2) as it:
                for k in range(4):
                    done("V", k, it)
                    ahead("V", k, it)
                    if k % 2:
                        dve.wait_ge(sig_ready, it * 2 + (k // 2 + 5))
                        dve.scalar_tensor_tensor(two(ghg[:, it * 2 + k // 2, :]), ps2(1),
                                                 vc[:, bass.ds(it * 2 + (40 + k // 2), 1)],
                                                 two(sg[k // 2][:]), MUL, MUL).then_inc(acc_free[1], 1)

            dve.wait_ge(xt_stored, 16)
            dve.wait_ge(set_up, 8)

            def merge(use, it):
                dve.wait_ge(sc_full, it * 4 + (use + 1))
                n = 4 * use
                for l in (2 * use, 2 * use + 1):
                    for b in range(2):
                        dve.wait_ge(merged, it * MERGES + (n + 1))
                        taken()
                        n += 1
                        if l == LV:
                            if b == 0:
                                dve.copy_predicated(
                                    sfull[:], ident.bitcast(u32).unsqueeze(1).broadcast_to([128, 8, CH]),
                                    lvb[:, 0, 256:264].unsqueeze(2).broadcast_to([128, 8, CH])).then_inc(merged, 1)
                            continue
                        hb = 1 << l
                        dst = sfull[:].rearrange("s (e par) (b two h) -> s par e b two h", par=2, two=2, h=hb)
                        on = msk[:, l * 64:(l + 1) * 64].rearrange("s (b h) -> s b h", h=hb).unsqueeze(1)\
                            .broadcast_to([128, 4, 64 // hb, hb])
                        c0 = 256 * (l % 2)
                        src = lvb[:, b, c0:c0 + 256].rearrange("s (e b h) -> s e b h", e=4, h=hb)
                        dve.copy_predicated(dst[:, b, :, :, 1, :], on, src).then_inc(merged, 1)

            def rotate(dst, k, it):
                step(dve.tensor_tensor(xs[k][:], xs[k][:], sinT, MUL))
                dve.wait_ge(acc_free[k], tidx("B", k, it) + 1)
                dve.tensor_tensor(dst, dst, xs[k][:], ADD).then_inc(rot_done, 1)

            def chunk(t, c):
                return t[:, :, bass.ds(c * CH, CH)]

            def stage_samples(k, q, it, f):
                if f:
                    step(dve.tensor_copy(fs8[:], fT[:, it, NT:TT]))
                    dve.tensor_scalar(ks8[:], fs8[:], -1.0, 1.0, MUL, ADD)
                else:
                    dve.tensor_copy(ks8[:], k[:, it, NT:TT])
                dve.tensor_copy(qs8[:], q[:, it, NT:TT]).then_inc(smp_staged, 1)

            def gate_outputs(gate, it, n):
                step(dve.reciprocal(rs[:], rs[:]))
                dve.wait_ge(ah_lo, it + (n + 1))
                dve.tensor_tensor(ot[:], ob[:], rs[:], MUL).then_inc(o_free, 1)
                dve.wait_ge(o_free, it + (n + 2))
                dve.tensor_tensor(m4(ot[:]), m4(ot[:]), chunk(gate, it), MUL).then_inc(a_done, 1)

            def branch_lo(t_lo, t_hi, it, n):
                dve.wait_ge(ah_hi, it + (n + 1))
                dve.tensor_tensor(chunk(t_lo, it), m4(ot[:]), chunk(t_hi, it).bitcast(fp), SUB).then_inc(ah_lo, 1)

            with dve.Fori(0, 4) as it:
                step.loop(it, 6)
                dve.wait_ge(misc_free, it * 6 + M_B)
                stage_samples(None, qT, it, True)
                merge(0, it)
                merge(1, it)
                done("B", 0, it)
                ahead("B", 0, it)
                dve.wait_ge(swapped, it * 4 + 2)
                dve.tensor_tensor(two(qr[:, it, :]), ps2(0), two(cosT), MUL).then_inc(acc_free[0], 1)
                rotate(qr[:, it, :], 0, it)
                merge(2, it)

                done("B", 1, it)
                ahead("B", 1, it)
                dve.wait_ge(swapped, it * 4 + 4)
                dve.scalar_tensor_tensor(two(kr[:, it, :]), ps2(1), KSCALE, two(cosT), MUL,
                                         MUL).then_inc(acc_free[1], 1)
                merge(3, it)
                rotate(kr[:, it, :], 1, it)
                dve.wait_ge(ss_loaded, it * 16 + 16)
                step(dve.tensor_tensor(ss[:], ss[:], fs8[:].unsqueeze(2).broadcast_to([128, NS, 64]), MUL))
                dve.wait_ge(misc_full, it * 6 + (M_B + 3))
                dve.tensor_tensor(ss[:], ss[:], mb[:].rearrange("p (b v) -> p b v", b=NS),
                                  ADD).then_inc(misc_free, 1)

                done("B", 2, it)
                ahead("B", 2, it)
                dve.wait_ge(o_ready, it + 1)
                dve.wait_ge(prep, it * 8 + 8)
                step(dve.tensor_tensor(sst[:], sst[:], tl[LV][:].broadcast_to([128, 4, 64]), MUL))
                dve.wait_ge(misc_full, it * 6 + (M_B + 4))
                dve.tensor_tensor(sst[:], sst[:], mb[:, 0:256].rearrange("p (c v) -> p c v", c=4),
                                  ADD).then_inc(misc_free, 1)
                dve.wait_ge(misc_free, it * 6 + (M_B + 5))
                gate_outputs(ghg, it, 0)

                done("B", 3, it)
                ahead("B", 3, it)
                dve.wait_ge(sig_ready, it + 9)
                dve.scalar_tensor_tensor(two(grt[:, it, :]), ps2(3), vc[:, bass.ds(it + 44, 1)],
                                         two(sg[1][:]), MUL, MUL).then_inc(acc_free[1], 1)
                dve.wait_ge(misc_full, it * 6 + (M_B + 6))
                taken()
                dve.tensor_copy(qT[:, it, NT:TT], mb[:, 0:NS]).then_inc(misc_free, 1)
                branch_lo(ahl, ahh, it, 0)
            step.end(4)

            def square_samples(t, i):
                cols = t[:, :, NT:TT]
                dve.tensor_tensor(sqs[:, 32 * i:32 * i + 32].rearrange("p (a b) -> p a b", a=4), cols, cols,
                                  MUL).then_inc(smp_sq, 1)

            dve.wait_ge(misc_free, M_C)
            square_samples(qT, 0)

            with dve.Fori(0, 4) as it:
                step.loop(it, 2)
                dve.wait_ge(misc_free, it * 4 + M_C)
                stage_samples(kr, qr, it, False)
                done("C", 0, it)
                dve.wait_ge(lv_full, it * 4 + (L_C + 1))
                dve.tensor_tensor(prb[:].rearrange("s h t -> s (h t)"), lvb[:, 0, :], decay,
                                  MUL).then_inc(lv_free[0], 1)
                dve.wait_ge(lv_full, it * 4 + (L_C + 2))
                dve.tensor_tensor(m4(ktk[:]), m4(lvb[:, 1, :]), kdec.unsqueeze(2).broadcast_to([128, 4, 128]),
                                  MUL).then_inc(lv_free[1], 1)
                ahead("C", 0, it)
                done("C", 1, it)
                ahead("C", 1, it)
                dve.wait_ge(ret_o, it + 1)
                step(dve.tensor_tensor(rst[:], rst[:], g128.unsqueeze(2).broadcast_to([128, 4, 128]), MUL))
                dve.wait_ge(misc_full, it * 4 + (M_C + 2))
                dve.tensor_tensor(rst[:], rst[:], m4(mb[:]), ADD).then_inc(misc_free, 1)
                dve.wait_ge(rsm_loaded, it * 16 + 16)
                for b in range(2):
                    dve.wait_ge(lv_full, it * 4 + (L_C + 3 + b))
                    part4 = rsm[:, 4 * b:4 * b + 4, :].rearrange("p b v -> p (b v)")
                    dve.scalar_tensor_tensor(part4, part4, gam[:, bass.ds(it, 1)], lvb[:, b, :], MUL,
                                             ADD).then_inc(lv_free[b], 1)
                dve.wait_ge(misc_free, it * 4 + (M_C + 3))
                gate_outputs(grt, it, 4)
                done("C", 2, it)
                ahead("C", 2, it)
                dve.wait_ge(misc_full, it * 4 + (M_C + 4))
                taken()
                dve.tensor_copy(qr[:, it, NT:TT], mb[:, 0:NS]).then_inc(misc_free, 1)
                branch_lo(arl, arh, it, 4)
                done("C", 3, it)
                ahead("C", 3, it)
            step.end(4)

            dve.wait_ge(misc_free, M_R)
            square_samples(qr, 1)
            dve.wait_ge(misc_free, M_R + 1)
            step(dve.reciprocal(rss[:], rss[:]))
            for i, (t, gate) in enumerate(((qT, ghg), (qr, grt))):
                rt4 = rss[:, 32 * i:32 * i + 32].rearrange("p (a b) -> p a b", a=4)
                step(dve.tensor_tensor(rt4, rt4, gate[:, :, NT:TT], MUL))
                ins = dve.tensor_tensor(smp[:, i], t[:, :, NT:TT], rt4, MUL)
            ins.then_inc(smp_done, 1)
            for i, (t_lo, t_hi) in enumerate(((ahl, ahh), (arl, arh))):
                dve.wait_ge(ah_hi, 8 + i + 1)
                dve.tensor_tensor(t_lo[:, :, NT:TT], smp[:, i], t_hi[:, :, NT:TT].bitcast(fp),
                                  SUB).then_inc(ah_lo, 1)

            with dve.Fori(0, 2) as it:
                for k in range(4):
                    done("D", 2 * k, it, 8)
                    dve.wait_ge(mix_lo, it * 4 + (k + 1))
                    dve.tensor_tensor(two(m1[:]), ps2(0), two(gab[:, it * 4 + k, :]), MUL).then_inc(acc_free[0], 1)
                    done("D", 2 * k + 1, it, 8)
                    dve.tensor_tensor(two(m2[:]), ps2(1), two(gab[:, it * 4 + (DC + k), :]),
                                      MUL).then_inc(acc_free[1], 1)
                    for b in range(2):
                        dve.wait_ge(acc_free[b], tidx("D", 2 * k + b, it, 8) + 1)
                    dve.tensor_tensor(m1[:], m1[:], m2[:], ADD).then_inc(mix_sum, 1)
                    ahead("D", k, it)
                    dve.wait_ge(mix_hi, it * 4 + (k + 1))
                    dve.tensor_tensor(xal[:, it * 4 + k, :], m1[:], xah[:, it * 4 + k, :].bitcast(fp),
                                      SUB).then_inc(mix_lo, 1)

            def residual(sec, tile, it, per, gain, n):
                j = it * per + tile
                dve.tensor_tensor(two(hT[:, j, :]), ps2(tile), two(hT[:, j, :]), ADD).then_inc(acc_free[tile % 2], 1)

                def low():
                    dve.wait_ge(xb_hi, it * per + (n + tile + 1))
                    dve.scalar_tensor_tensor(xbl[:, j, :], hT[:, j, :], vc[:, bass.ds(j + gain, 1)],
                                             xbh[:, j, :].bitcast(fp), MUL, SUB).then_inc(xb_lo, 1)
                return low

            dve.wait_ge(h_loaded, 16)
            with dve.Fori(0, 2) as it:
                for k in range(4):
                    done("E", k, it)
                    low = residual("E", k, it, 4, 16, 0)
                    ahead("E", k, it)
                    low()

            def inverse_rms(n):
                for b in range(2):
                    dve.wait_ge(lv_free[b], L_F // 2 + n + 1)
                step(dve.reciprocal(rstd[:], rstd[:]))

            dve.wait_ge(misc_free, M_F + 1)
            old = stT[:].rearrange("p j (b w) -> p j b w", w=2)

            def tap(i):
                return vc[:, 48 + FC * i:48 + FC * (i + 1)].unsqueeze(2).broadcast_to([128, FC, NS])

            tmp = gg[:, 0:FC * NS].rearrange("p (j b) -> p j b", b=NS)
            step(dve.tensor_tensor(part[:], old[:, :, :, 0], tap(0), MUL))
            step(dve.tensor_tensor(tmp, old[:, :, :, 1], tap(1), MUL))
            step(dve.tensor_tensor(part[:], part[:], tmp, ADD))
            step(dve.tensor_tensor(part[:], part[:], tap(3), ADD))
            for b in range(2):
                step(dve.memset(ab[b][:, 0:2], 0.0))
            inverse_rms(0)

            def ffn(it, nxt=None):
                for k in range(4):
                    done("F", k, it)
                    j = it * 2 + k // 2
                    if k % 2 == 0:
                        a = ab[k // 2]
                        dve.tensor_tensor(two(a[:, 2:TT + 2]), ps2(k), two(rstd[:]), MUL).then_inc(acc_free[0], 1)
                        ahead("F", k, it, nxt)
                        dve.wait_ge(c_first, it * 2 + (k // 2 + 1))
                        w1 = vc[:, bass.ds(it * 2 + (48 + FC + k // 2), 1)]
                        w2 = vc[:, bass.ds(it * 2 + (48 + 2 * FC + k // 2), 1)]
                        step(dve.scalar_tensor_tensor(cv[:, NT:TT], a[:, TT - 6:TT + 2], w2, part[:, j, :], MUL, ADD))
                        step(dve.scalar_tensor_tensor(cv[:, 0:NT], a[:, 1:NT + 1], w1, cv[:, 0:NT], MUL, ADD))
                        dve.scalar_tensor_tensor(cv[:, 0:NT], a[:, 2:NT + 2], w2, cv[:, 0:NT], MUL,
                                                 ADD).then_inc(c_ready, 1)
                    else:
                        dve.wait_ge(ac_lo, it * 2 + (k // 2 + 1))
                        dve.tensor_tensor(two(gg[:]), ps2(k), two(rstd[:]), MUL).then_inc(acc_free[1], 1)
                        ahead("F", k, it, nxt)
                        dve.wait_ge(ac_hi, it * 2 + (k // 2 + 1))
                        dve.tensor_tensor(acl[:, j, :], gg[:], ach[:, j, :].bitcast(fp), SUB).then_inc(ac_lo, 1)

            with dve.Fori(0, 10) as it:
                step.loop(it, 4)
                ffn(it)
            step.end(10)
            ffn(10, "G")

            def down(it, nxt=None):
                for k in range(4):
                    done("G", k, it)
                    if k % 2:
                        low = residual("G", k // 2, it, 2, 24, 8)
                    ahead("G", k, it, nxt)
                    if k % 2:
                        low()

            with dve.Fori(0, 3) as it:
                down(it)
            down(3, "H")
            for j in range(2):
                dve.wait_ge(p_hi, 2 * j + 1)
                dve.tensor_tensor(pxl[:, j, 0:NT], mb[:], pxh[:, j, 0:NT].bitcast(fp), SUB).then_inc(misc_free, 1)
                dve.wait_ge(p_hi, 2 * j + 2)
                dve.tensor_tensor(pxl[:, j, NT:TT], mb[:, 0:NS], pxh[:, j, NT:TT].bitcast(fp),
                                  SUB).then_inc(misc_free, 1)
            inverse_rms(1)

            def embed(it, last=False):
                for k in range(4):
                    done("H", 2 * k, it, 8)
                    dve.tensor_tensor(two(tg[:]), ps2(0), two(rstd[:]), MUL).then_inc(acc_free[0], 1)
                    done("H", 2 * k + 1, it, 8)
                    dve.wait_ge(sig_ready, it * 4 + (12 + k + 1))
                    dve.wait_ge(h_new, it * 4 + (k + 1))
                    dve.tensor_tensor(two(tp[:]), ps2(1), two(sgg[:]), MUL).then_inc(acc_free[1], 1)
                    dve.wait_ge(acc_free[1], tidx("H", 2 * k + 1, it, 8) + 1)
                    dve.tensor_tensor(hT[:, it * 4 + k, :], hT[:, it * 4 + k, :], tp[:], ADD).then_inc(h_new, 1)
                    if k < 2 or not last:
                        ahead("H", k, it)

            embed(0)
            embed(1, last=True)
            dve.wait_ge(misc_free, M_G + 11)
            dve.reciprocal(rt[:, 0:4], rt[:, 0:4])
            dve.reciprocal(rt[0:NS, 4:5], rt[0:NS, 4:5]).then_inc(rt_ready, 1)
            dve.wait_ge(rt_ready, 1)
            for u in range(1, 10, 2):
                n = 128 if u < 8 else NS
                dve.wait_ge(lv_full, L_TOTAL + 4 + u + 1)
                dve.tensor_scalar(ytok[0:n, u // 2, 512:1024], lvb[0:n, 1, :], rt[0:n, u // 2:u // 2 + 1], None,
                                  MUL).then_inc(lv_free[1], 1)

        @block.gpsimd
        def _(pool):
            def taken():
                pool.sem_inc(pool_passed, 1)

            step = Steps(pool, pool_s, taken)
            for first in (act_ready, ssq_ready):
                pool.sem_inc(first, 1)
            for t, v in ((ones128, 1.0 / 128), (ones1024, 1.0 / DM), (eps, EPS), (ssx, 1.0), (sst, 0.0), (rst, 0.0), (one, 1.0)):
                pool.memset(t[:], v).then_inc(set_up, 1)
            pool.wait_ge(const_loaded, 32)

            def chunk(t, c):
                return t[:, :, bass.ds(c * CH, CH)]

            def first_level(c):
                step(pool.tensor_tensor(lk[0][:], one[:].unsqueeze(2).broadcast_to([128, 4, CH]), chunk(fT, c), SUB))
                pool.tensor_tensor(lq[0][:], chunk(qT, c), chunk(fT, c), MUL)
                pool.tensor_tensor(qk[:], chunk(qT, c), lk[0][:], MUL).then_inc(prep, 1)

            def next_level(l, c=None):
                hb = 1 << (l - 1)

                def halves(t):
                    return t[:].rearrange("p c (b two h) -> p c b two h", two=2, h=hb)
                q0, q1, k0, k1 = (halves(t[i % 4]) for t in (lq, lk) for i in (l - 1, l))
                t0 = (chunk(fT, c) if l == 1 else tl[l - 1][:]).rearrange("p c (b two) -> p c b two", two=2)

                def pick(t, i):
                    t = t[:, :, :, i, :]
                    return t[:, :, :, 0] if hb == 1 else t.rearrange("p c b h -> p (c b) h")

                def decays(i):
                    if hb == 1:
                        return t0[:, :, :, i]
                    return t0.rearrange("p c b two -> p (c b) two")[:, :, i:i + 1]\
                        .broadcast_to([128, 4 * (CH // (2 * hb)), hb])
                pool.tensor_copy(pick(q1, 0), pick(q0, 0))
                pool.tensor_copy(pick(k1, 1), pick(k0, 1))
                pool.tensor_tensor(pick(q1, 1), pick(q0, 1), decays(0), MUL)
                pool.tensor_tensor(pick(k1, 0), pick(k0, 0), decays(1), MUL)
                pool.tensor_tensor(tl[l][:], t0[:, :, :, 0], t0[:, :, :, 1], MUL).then_inc(prep, 1)

            def outer_values(src, it, groups):
                g, w = groups, 128 // groups
                out = vblk[:].rearrange("p (g b v) -> p g b v", g=g, b=NS)
                v = src[:, bass.ds(it * 128, 128)].rearrange("p (g v) -> p g v", g=g).unsqueeze(2)\
                    .broadcast_to([NS, g, NS, w])
                d = ident[0:NS, 0:NS].unsqueeze(1).unsqueeze(3).broadcast_to([NS, g, NS, w])
                return pool.tensor_tensor(out, v, d, MUL)

            pool.wait_ge(acc_free[0], 5)
            pool.wait_ge(f_done, 5)
            pool.wait_ge(set_up, 7)
            pool.memset(sfull[:], 0.0).then_inc(set_up, 1)
            first_level(0)
            for l in range(1, 4):
                pool.wait_ge(prep, l)
                next_level(l, 0)

            def hgrn(it, last=False):
                pool.wait_ge(misc_free, it * 6 + M_B)
                taken()
                outer_values(v8h, it, 2).then_inc(outer_ready, 1)
                for l in range(4, LV + 1):
                    pool.wait_ge(prep, it * 8 + l)
                    pool.wait_ge(sc_full, it * 4 + ((l - 4) // 2 + 1))
                    taken()
                    next_level(l)
                if not last:
                    pool.wait_ge(sc_full, it * 4 + 4)
                    taken()
                    first_level(it + 1)
                    for l in range(1, 4):
                        pool.wait_ge(prep, it * 8 + (8 + l))
                        if l == 3:
                            pool.wait_ge(o_ready, it + 1)
                        taken()
                        next_level(l, it + 1)

            with pool.Fori(0, 3) as it:
                step.loop(it, 1)
                hgrn(it)
            step.end(3)
            hgrn(3, last=True)

            pool.wait_ge(rot_done, 9)
            pool.wait_ge(v_taken, 9)
            with pool.Fori(0, 4) as it:
                pool.wait_ge(misc_free, it * 4 + M_C)
                taken()
                pool.tensor_copy(qst[:], chunk(qr, it)).then_inc(staged, 1)
                pool.wait_ge(staged, it * 2 + 1)
                taken()
                pool.tensor_tensor(qd[:], qst[:], m4(qdec), MUL).then_inc(staged, 1)
                outer_values(v8r, it, 1).then_inc(outer_ready, 1)

            def squares(j, n):
                pool.wait_ge(ssq_ready, j + (n + 1))
                taken()
                step(pool.tensor_tensor(sqt[:], hT[:, j, :], hT[:, j, :], MUL))
                pool.tensor_tensor(ssq[:], ssq[:], sqt[:], ADD).then_inc(ssq_ready, 1)

            pool.wait_ge(acc_free[0], tidx("E", 0, 0) + 1)
            step(pool.memset(ssq[:], 0.0))
            with pool.Fori(0, 2) as it:
                step.loop(it, 4)
                for k in range(4):
                    pool.wait_ge(acc_free[k % 2], tidx("E", k, it) + 1)
                    taken()
                    squares(it * 4 + k, 0)
            step.end(2)

            with pool.Fori(0, 11) as it:
                for k in range(2):
                    pool.wait_ge(acc_free[0], tidx("F", 2 * k, it) + 1)
                    taken()
                    pool.tensor_copy(cs[:, it * 2 + k, :], ab[k][:, NT:TT + 2]).then_inc(cs_ready, 1)
                    pool.wait_ge(acc_free[1], tidx("F", 2 * k + 1, it) + 1)
                    pool.wait_ge(gelu_ready, it * 2 + (k + 1))
                    pool.tensor_tensor(gg[:], gg[:], cv[:], MUL).then_inc(act_ready, 1)

            pool.wait_ge(acc_free[0], tidx("G", 0, 0, 2) + 1)
            step(pool.memset(ssq[:], 0.0))
            with pool.Fori(0, 4) as it:
                step.loop(it, 2)
                for k in range(2):
                    pool.wait_ge(acc_free[k], tidx("G", k, it, 2) + 1)
                    taken()
                    squares(it * 2 + k, 8)
            step.end(4)
            pool.wait_ge(h_new, 2)
            step(pool.memset(ssq[:], 0.0))
            with pool.Fori(0, 2) as it:
                step.loop(it, 4)
                for k in range(4):
                    pool.wait_ge(h_new, it * 4 + (k + 2))
                    taken()
                    squares(it * 4 + k, 16)
            step.end(2)


def shape_tables():
    import numpy as np
    f32 = np.float32
    gamma = 1.0 - 2.0 ** (-5.0 - np.arange(4))
    inv = (f32(10000.0) ** (-np.arange(0, 128, 2, dtype=f32) / f32(128))).astype(f32)
    pos = np.concatenate([np.arange(512, dtype=f32), np.full(8, 4096.0, f32)])
    ang = (pos[None, :] * inv[:, None]).astype(f32).astype(np.float64)
    t = np.arange(128)
    s_, t_ = t[:, None], t[None, :]
    tables = {
        "ident": np.eye(128),
        "blk64": (s_ // 64 == t_ // 64) / 64.0,
        "headsel": (s_ // 64 == np.arange(2)[None, :]) * 1.0,
        "cos": np.concatenate([np.cos(ang), np.cos(ang)]),
        "sin": np.concatenate([-np.sin(ang), np.sin(ang)]),
        "decay": np.concatenate([np.where(t_ >= s_, g ** np.maximum(t_ - s_, 0), 0.0) for g in gamma], 1),
        "qdec": np.concatenate([np.broadcast_to(g ** (t_ + 1.0), (128, 128)) for g in gamma], 1),
        "kdec": gamma[None, :] ** (127.0 - s_),
        "g128": np.broadcast_to(gamma ** 128.0, (128, 4)),
        "gam": np.broadcast_to(gamma, (128, 4)),
    }
    offs, at = {}, 0
    for n, a in tables.items():
        offs[n] = at
        at += a.shape[1]
    masks = []
    for l in range(7):
        h = 1 << l
        second = t[(t // h) % 2 == 1]
        masks.append(((s_ // (2 * h) == second[None, :] // (2 * h)) & ((s_ // h) % 2 == 0)).astype(np.uint32))
    return (np.ascontiguousarray(np.concatenate(list(tables.values()), 1), dtype=f32), offs,
            np.ascontiguousarray(np.concatenate(masks, 1)))


_INS = ["x_prompt", "x_sample", "state_hgrn", "state_ret", "state_conv", "p_prompt", "p_sample", "lb_logits",
        "w_in", "g_mix", "g_hg_out", "g_ret_out", "w_br_hg", "w_br_ret", "w_out", "g_ffn", "w_up", "conv_w",
        "conv_b", "w_down", "g_ple", "w_ple", "w_ple_gate", "g_final"]
_OUTS = [(1, 512, 1024), (8, 1, 1024), (1, 1, 8, 64, 64), (1, 1, 4, 128, 128), (1, 1, 2, 2816),
         (1, 8, 8, 64, 64), (1, 8, 4, 128, 128), (1, 8, 2, 2816)]


def kernel(**inputs):
    import numpy as _np
    import concourse.bacc as _bacc
    from concourse import mybir as _mybir
    from concourse.bass_utils import run_bass_kernel_spmd as _run

    nc = _bacc.Bacc("TRN2", target_bir_lowering=False, num_devices=1)
    consts, offs, masks = shape_tables()
    arrays, args = {}, []
    for name in _INS:
        arrays[f"in_{name}"] = _np.ascontiguousarray(inputs[name])
    arrays["consts"], arrays["masks"] = consts, masks
    for name, a in arrays.items():
        args.append(nc.dram_tensor(name, a.shape, _mybir.dt.from_np(a.dtype), kind="ExternalInput").ap())
    for i, shape in enumerate(_OUTS):
        args.append(nc.dram_tensor(f"out_{i}", shape, _mybir.dt.float32, kind="ExternalOutput").ap())
    hybrid_layer(nc, *args, offs=offs)
    r = _run(nc, [arrays], core_ids=[0])
    return tuple(r.results[0][f"out_{i}"] for i in range(len(_OUTS)))
```

```python
import concourse.bass as bass
from concourse import mybir
from contextlib import ExitStack

NT = 512
NS = 8
TT = NT + NS
HT = TT // 2
DM = 1024
DC = DM // 128
CH = 128
NCH = NT // CH
LV = 7
FF = 2816
FC = FF // 128
PD = 256
EPS = 1e-6
WMAX = FC // 2 * 128
YSPLIT = 384

SEC = dict(A=(0, 0, 2), V=(8, 8, 10), B=(16, 16, 18), C=(32, 32, 34), D=(48, 48, 50), E=(56, 64, 66),
           F=(64, 72, 74), G=(108, 116, 118), H=(124, 132, 126))
SIZE = dict(A=1024, V=1024, B=1024, C=1024, D=1024, E=1024, F=1024, G=WMAX, H=1280)
M_B, M_C, M_F, M_G = 3, 27, 47, 48
L_C, L_F, L_Y = 8, 24, 28
MERGES = LV + 1


class Steps:

    def __init__(self, eng, sem, after=None):
        self.eng, self.sem, self.base, self.k, self.it, self.per = eng, sem, 0, 0, 0, 0
        self.after = after

    def loop(self, it, per):
        self.base, self.k, self.it, self.per = self.base + self.k, 0, it, per

    def end(self, rounds):
        assert self.k == self.per, (self.k, self.per)
        self.base, self.k, self.it, self.per = self.base + rounds * self.per, 0, 0, 0

    def __call__(self, ins):
        ins.then_inc(self.sem, 1)
        self.k += 1
        self.eng.wait_ge(self.sem, self.it * self.per + (self.base + self.k))
        if self.after:
            self.after()


def hybrid_layer(nc, x_prompt, x_sample, state_hgrn, state_ret, state_conv, p_prompt, p_sample,
                 lb_logits, w_in, g_mix, g_hg_out, g_ret_out, w_br_hg, w_br_ret, w_out, g_ffn, w_up,
                 conv_w, conv_b, w_down, g_ple, w_ple, w_ple_gate, g_final, consts, masks,
                 y_prompt, y_sample, hg_prompt, ret_prompt, conv_prompt, hg_sample, ret_sample,
                 conv_sample, offs):
    fp, fr, u32 = mybir.dt.float32, mybir.dt.float32r, mybir.dt.uint32
    ALU, ACT = mybir.AluOpType, mybir.ActivationFunctionType
    MUL, ADD, SUB = ALU.mult, ALU.add, ALU.subtract
    KSCALE = float(128 ** -0.5)

    def tiles(w):
        return w[0].rearrange("(c p) (t n) -> p c t n", p=128, n=128)

    win_v, wbh_v, wbr_v, wout_v = tiles(w_in), tiles(w_br_hg), tiles(w_br_ret), tiles(w_out)
    wup_v, wdn_v, wpl_v, wpg_v = tiles(w_up), tiles(w_down), tiles(w_ple), tiles(w_ple_gate)
    COL = {n: i for n, i in zip(("hq", "hf", "hi", "hg", "rq", "rk", "rv", "rg"), range(0, 32, 4))}
    COL.update(ga=32, gb=40)
    xt_dram = nc.dram_tensor("x_transposed", [128, DC, TT], fp).ap()

    base = (nc.sbuf_base + 31) // 32 * 32

    def at(name, shape, off, dt=fp):
        size = 4
        for n in shape[1:]:
            size *= n
        assert off + size <= 212832, (name, off + size)
        return nc.alloc_sbuf_tensor_at(name, shape, dt, offset=base + off)

    class Region:
        def __init__(self, start, stop):
            self.at, self.stop = start, stop

        def __call__(self, name, shape, dt=fp):
            size = 4
            for n in shape[1:]:
                size *= n
            t = at(name, shape, self.at, dt)
            self.at += (size + 31) // 32 * 32
            assert self.at <= self.stop, (name, self.at, self.stop)
            return t

    r = Region(0, 33792)
    raw = [r(f"raw{i}", [128, WMAX]) for i in range(2)]
    whi = [r(f"whi{i}", [128, WMAX], fr) for i in range(2)]
    wlo = [r(f"wlo{i}", [128, WMAX], fr) for i in range(2)]
    r = Region(33792, 49152)
    NCST = consts.shape[1]
    CST0 = r.at
    cst = r("cst", [128, NCST])
    msk = r("msk", [128, LV * 64], u32)
    ones128 = r("ones128", [128, 128])
    ones1024 = r("ones1024", [128, 128])
    vc = r("vc", [128, 136])
    lbt = r("lbt", [128, 6, 4])
    eps = r("eps", [128, 1])
    ssx = r("ssx", [128, 8])
    ot = r("ot", [128, 512])
    ident = cst[:, offs["ident"]:offs["ident"] + 128]
    blk64 = cst[:, offs["blk64"]:offs["blk64"] + 128]
    headsel = cst[:, offs["headsel"]:offs["headsel"] + 2]
    cosT = cst[:, offs["cos"]:offs["cos"] + TT]
    sinT = cst[:, offs["sin"]:offs["sin"] + TT]
    decay = cst[:, offs["decay"]:offs["decay"] + 512]
    qdec = cst[:, offs["qdec"]:offs["qdec"] + 512]
    kdec = cst[:, offs["kdec"]:offs["kdec"] + 4]
    g128 = cst[:, offs["g128"]:offs["g128"] + 4]
    gam = cst[:, offs["gam"]:offs["gam"] + 4]
    r = Region(49152, 49152 + 33280)
    xah = r("xah", [128, DC, TT], fr)
    xal = r("xal", [128, DC, TT], fr)
    XA_END = 82432
    r = Region(XA_END, 212832)
    G0 = r.at
    fT = r("fT", [128, 4, TT])
    qT = r("qT", [128, 4, TT])
    qr = r("qr", [128, 4, TT])
    G1 = r.at
    lq = [r(f"lq{i}", [128, 4, CH]) for i in range(4)]
    lk = [r(f"lk{i}", [128, 4, CH]) for i in range(4)]
    qk = r("qk", [128, 4, CH])
    sfull = r("sfull", [128, 8, CH])
    khat = r("khat", [128, 512])
    vhg = r("vhg", [128, NCH, 512])
    v8h = r("v8h", [NS, 512])
    AG0 = r.at
    ghg = r("ghg", [128, 4, TT])
    AR0 = r.at
    kr = r("kr", [128, 4, TT])
    vr = r("vr", [128, NCH, 512])
    v8r = r("v8r", [NS, 512])
    grt = r("grt", [128, 4, TT])
    vst = r("vst", [128, 512])
    tl = [None] + [r(f"tl{i}", [128, 4, CH >> i]) for i in range(1, LV + 1)]
    sst = r("sst", [128, 4, 64])
    sq = r("sq", [128, 512])
    rs = r("rs", [128, 512])
    vblk = r("vblk", [NS, 1024])
    k8 = r("k8", [NS, 128])
    fs8 = r("fs8", [128, 8])
    ks8 = r("ks8", [128, 8])
    qs8 = r("qs8", [128, 8])
    sqs = r("sqs", [128, 16])
    rss = r("rss", [128, 16])
    smp = r("smp", [128, 2, NS])
    one = r("one", [128, 1])
    T0 = r.at
    xs = [r(f"xs{i}", [128, TT]) for i in range(2)]
    hiT = r("hiT", [128, TT])
    sg = [r(f"sg{i}", [128, TT]) for i in range(2)]
    r = Region(T0, r.at)
    kst = r("kst", [128, 4, CH])
    qst = r("qst", [128, 4, CH])
    qd = r("qd", [128, 4, CH])
    prb = r("prb", [128, 4, CH])
    r = Region(T0 + 10400, 212832)
    ktk = at("ktk", [128, 512], r.at)
    sgf = r("sgf", [128, TT])
    rst = r("rst", [128, 4, 128])
    ss = at("ss", [128, 8, 64], r.at)
    zq = [at(f"zq{i}", [128, 4, 2, CH // 2], o)
          for i, o in enumerate((T0 + 10400, r.at + 2048, r.at + 4096, T0 + 3 * TT * 4))]
    rsm = r("rsm", [128, 8, 128])
    r = Region(G0, 212832)
    xtok = r("xtok", [128, 5, DM])
    xsq = r("xsq", [128, 5, DM])
    dg = r("dg", [128, 5, 128])
    vrow = r("vrow", [128, 2, 128])
    xstg = at("xstg", [128, DC, TT], AR0)
    xsm = at("xsm", [128, DC, NS], AR0 + 16640 + 2048)
    gab = at("gab", [128, 2 * DC, TT], G1)
    assert G1 + 16 * TT * 4 <= AG0
    ahh = at("ahh", [128, 4, TT], G0 + 4 * TT * 4, fr)
    ahl = at("ahl", [128, 4, TT], G0, fr)
    arh = at("arh", [128, 4, TT], G0 + 8 * TT * 4, fr)
    arl = at("arl", [128, 4, TT], AG0, fr)
    A0, B0, H0 = 49152, 49152 + 91520, 49152 + 91520 + 33280
    r = Region(A0, B0)
    ach = r("ach", [128, FC, TT], fr)
    acl = r("acl", [128, FC, TT], fr)
    r = Region(B0, H0)
    xbh = r("xbh", [128, DC, TT], fr)
    xbl = r("xbl", [128, DC, TT], fr)
    r = Region(H0, 212832)
    hT = r("hT", [128, DC, TT])
    m1 = r("m1", [128, TT])
    m2 = r("m2", [128, TT])
    sqt = r("sqt", [128, TT])
    ssq = r("ssq", [128, TT])
    rstd = r("rstd", [128, TT])
    F0 = r.at
    ab = [r(f"ab{i}", [128, TT + 2]) for i in range(2)]
    cv = r("cv", [128, TT])
    gg = r("gg", [128, TT])
    part = r("part", [128, FC, NS])
    cs = at("cs", [128, FC, 10], H0 + 16640)
    stT = at("stT", [128, FC, 16], A0 + 40000)
    strow = at("strow", [16, FF], A0 + 48000)
    csr = at("csr", [10, FF], F0)
    r = Region((CST0 + 4 * offs["cos"] + 31) // 32 * 32, CST0 + 4 * NCST + 4 * LV * 64)
    pxh = r("pxh", [128, 2, TT], fr)
    pxl = r("pxl", [128, 2, TT], fr)
    r = Region(A0, B0)
    ptok = at("ptok", [128, 5, PD], F0)
    tg = r("tg", [128, TT])
    sgg = r("sgg", [128, TT])
    tp = r("tp", [128, TT])
    yT = r("yT", [128, DC, TT])
    ytok = r("ytok", [128, 5, DM])
    rt = r("rt", [128, 5])

    ctx = ExitStack()
    with ctx:
        def sem(name):
            return ctx.enter_context(nc.semaphore(name))

        acc = [ctx.enter_context(nc.psum_tensor(f"acc{i}", [128, 2, 512], fp)) for i in range(2)]
        lvb = ctx.enter_context(nc.psum_tensor("lvb", [128, 2, 512], fp))
        ob = ctx.enter_context(nc.psum_tensor("ob", [128, 512], fp))
        mb = ctx.enter_context(nc.psum_tensor("mb", [128, 512], fp))

        raw_loaded = [sem(f"raw_loaded{i}") for i in range(2)]
        hi_ready = sem("hi_ready")
        lo_ready = sem("lo_ready")
        part_done = sem("part_done")
        acc_free = [sem(f"acc_free{i}") for i in range(2)]
        lv_full = sem("lv_full")
        zq_ready = sem("zq_ready")
        sc_full = sem("sc_full")
        merged = sem("merged")
        lv_free = [sem(f"lv_free{i}") for i in range(2)]
        misc_full = sem("misc_full")
        misc_free = sem("misc_free")
        ident_loaded = sem("ident_loaded")
        const_loaded = sem("const_loaded")
        vec_loaded = sem("vec_loaded")
        x_loaded = [sem(f"x_loaded{i}") for i in range(5)]
        set_up = sem("set_up")
        x_sq = sem("x_sq")
        x_diag = sem("x_diag")
        x_tile = sem("x_tile")
        xa_hi = sem("xa_hi")
        xa_lo = sem("xa_lo")
        vec_ready = sem("vec_ready")
        lb_exp = sem("lb_exp")
        xt_stored = sem("xt_stored")
        sig_ready = sem("sig_ready")
        f_done = sem("f_done")
        swapped = sem("swapped")
        rot_done = sem("rot_done")
        prep = sem("prep")
        o_ready = sem("o_ready")
        v_full = sem("v_full")
        v_taken = sem("v_taken")
        smp_staged = sem("smp_staged")
        staged = sem("staged")
        outer_ready = sem("outer_ready")
        vst_ready = sem("vst_ready")
        sq_ready = sem("sq_ready")
        o_free = sem("o_free")
        a_done = sem("a_done")
        ss_loaded = sem("ss_loaded")
        ss_stored = sem("ss_stored")
        rsm_loaded = sem("rsm_loaded")
        rsm_stored = sem("rsm_stored")
        ret_o = sem("ret_o")
        smp_sq = sem("smp_sq")
        smp_done = sem("smp_done")
        ah_hi = sem("ah_hi")
        ah_lo = sem("ah_lo")
        smp_hi = sem("smp_hi")
        h_loaded = sem("h_loaded")
        mix_sum = sem("mix_sum")
        mix_hi = sem("mix_hi")
        mix_lo = sem("mix_lo")
        h_new = sem("h_new")
        xb_hi = sem("xb_hi")
        xb_lo = sem("xb_lo")
        ssq_ready = sem("ssq_ready")
        st_loaded = sem("st_loaded")
        c_first = sem("c_first")
        c_ready = sem("c_ready")
        gelu_ready = sem("gelu_ready")
        act_ready = sem("act_ready")
        ac_hi = sem("ac_hi")
        ac_lo = sem("ac_lo")
        cs_ready = sem("cs_ready")
        p_loaded = sem("p_loaded")
        p_full = sem("p_full")
        p_hi = sem("p_hi")
        p_lo = sem("p_lo")
        y_ready = sem("y_ready")
        ys_taken = sem("ys_taken")
        y_scaled = [sem(f"y_scaled{i}") for i in range(2)]
        rt_ready = sem("rt_ready")
        stored = sem("stored")
        pe_s, act_s, dve_s, pool_s = (sem(n) for n in ("pe_step", "act_step", "dve_step", "pool_step"))
        pe_passed, act_passed, dve_passed, pool_passed = (
            sem(n) for n in ("pe_passed", "act_passed", "dve_passed", "pool_passed"))

        def unit(sec, k, it):
            return it * 4 + (SEC[sec][0] + k)

        def parts(sec, k, it, per=4):
            return it * per + (SEC[sec][1] + k)

        def tidx(sec, k, it, per=4):
            return it * (per // 2) + (SEC[sec][2] + k) // 2

        def two(ap):
            return ap.rearrange("p (a b) -> p a b", a=2)

        def ps2(t, lo=0, hi=128):
            return acc[t % 2][lo:hi, :, 0:HT]

        def m4(ap):
            return ap.rearrange("p (a b) -> p a b", a=4)

        def x_bank(j):
            return (lvb[:, 0, :], lvb[:, 1, :], ob[:], acc[1][:, 0, :], acc[1][:, 1, :])[j % 5]

        block = ctx.enter_context(nc.Block())


        @block.sync
        def _(sp):
            xp = x_prompt[0].rearrange("(i p) n -> p i n", p=128)
            sp.dma_start(xtok[0:NS, 4, :], x_sample[:, 0, :]).then_inc(x_loaded[4], 16)
            for i in range(NCH):
                sp.dma_start(xtok[:, i, :], xp[:, i, :]).then_inc(x_loaded[i], 16)
            for src, b, row in ((g_mix[0], 0, 8), (lb_logits, 0, 0), (g_ffn[0], 0, 16), (g_ple[0], 0, 24),
                                (g_final, 0, 32), (g_hg_out[0], 0, 40), (g_ret_out[0], 0, 44),
                                (conv_w[0], 1, 0), (conv_b[0], 1, 66)):
                rows = src.rearrange("(c p) -> c p", p=128) if len(src.shape) == 1 \
                    else src.rearrange("i (c p) -> (i c) p", p=128)
                sp.dma_start(vrow[row:row + rows.shape[0], b, :], rows).then_inc(vec_loaded, 16)

            def load(sec, k, it, srcs):
                u = unit(sec, k, it)
                sp.wait_ge(lo_ready, u + 1)
                if len(srcs) == 1:
                    n = (srcs[0].shape[1] + 1) // 2
                    srcs = [srcs[0][:, 0:n], srcs[0][:, n:]]
                at0 = 0
                for src in srcs:
                    n = src.shape[1]
                    dst = raw[k % 2][:, at0 * 128:(at0 + n) * 128].rearrange("p (c n) -> p c n", n=128)
                    sp.dma_start(dst, src).then_inc(raw_loaded[k % 2], 16)
                    at0 += n

            for sec, names in (("A", ("hq", "hf")), ("V", ("hi", "hg"))):
                with sp.Fori(0, 2) as it:
                    for k in range(4):
                        load(sec, k, it, [win_v[:, :, it * 2 + (COL[names[k % 2]] + k // 2), :]])
            for b in range(2):
                sp.wait_ge(lv_free[b], 4)
            sp.wait_ge(misc_free, 1)
            sp.dma_start(xt_dram, xstg[:]).then_inc(xt_stored, 16)
            with sp.Fori(0, 4) as it:
                for k, n in enumerate(("rq", "rk", "rv", "rg")):
                    load("B", k, it, [win_v[:, :, it + COL[n], :]])
            with sp.Fori(0, 4) as it:
                for k in range(4):
                    load("C", k, it, [win_v[:, :, it * 2 + (COL["ga" if k % 2 == 0 else "gb"] + k // 2), :]])
            with sp.Fori(0, 2) as it:
                for k in range(4):
                    load("D", k, it, [wbh_v[:, :, it * 4 + k, :], wbr_v[:, :, it * 4 + k, :]])
            sp.wait_ge(h_loaded, 16)
            sp.dma_start(ptok[:, 0:NCH, :], p_prompt[0, 0].rearrange("(i p) n -> p i n", p=128)).then_inc(p_loaded, 16)
            sp.dma_start(ptok[0:NS, 4, :], p_sample[0, :, 0, :]).then_inc(p_loaded, 16)
            sp.dma_start(conv_sample[0, :, 0, :], state_conv[0, :, 1, :]).then_inc(stored, 16)
            with sp.Fori(0, 2) as it:
                for k in range(4):
                    load("E", k, it, [wout_v[:, :, it * 4 + k, :]])
            with sp.Fori(0, 11) as it:
                for k in range(4):
                    load("F", k, it, [wup_v[:, :, it * 2 + (k // 2 + (0 if k % 2 == 0 else FC)), :]])
            with sp.Fori(0, 4) as it:
                for k in range(4):
                    load("G", k, it, [wdn_v[:, FC // 2 * (k % 2):FC // 2 * (k % 2 + 1), it * 2 + k // 2, :]])
            with sp.Fori(0, 2) as it:
                for k in range(4):
                    load("H", k, it, [wpg_v[:, :, it * 4 + k, :], wpl_v[:, :, it * 4 + k, :]])
            yp = y_prompt[0].rearrange("(i p) n -> p i n", p=128)
            for b in range(2):
                sp.wait_ge(lv_free[b], L_Y // 2 + 7 - b)
            sp.dma_start(conv_prompt[0, 0], csr[0:2, :]).then_inc(stored, 16)
            sp.dma_start(conv_sample[0, :, 1, :], csr[2:10, :]).then_inc(stored, 16)
            for i in range(5):
                for b in range(2):
                    sp.wait_ge(y_scaled[b], i + 1)
                if i < NCH:
                    sp.dma_start(yp[:, i, :], ytok[:, i, :]).then_inc(stored, 16)
                else:
                    sp.dma_start(y_sample[:, 0, :], ytok[0:NS, 4, :]).then_inc(stored, 16)
            sp.wait_ge(xt_stored, 16)
            sp.wait_ge(ss_stored, 80)
            sp.wait_ge(rsm_stored, 80)
            sp.wait_ge(stored, 16 * 11)

        @block.tensor
        def _(pe):
            def taken():
                pe.sem_inc(pe_passed, 1)

            step = Steps(pe, pe_s, taken)

            def level(n):
                return lvb[:, n % 2, :]

            def wait_level(base, k, it, per):
                pe.wait_ge(lv_free[k % 2], it * (per // 2) + (base + k) // 2)

            def wait_misc(base, k, it, per):
                pe.wait_ge(misc_free, it * per + (base + k))

            def product(sec, k, it, slot, tile, chunks, w0, xh, xl, first=True, last=True, tper=4,
                        wait_unit=True, chunk_wait=None):
                if wait_unit:
                    pe.wait_ge(hi_ready, unit(sec, k, it) + 1)
                    pe.wait_ge(lo_ready, unit(sec, k, it) + 3)
                if first:
                    pe.wait_ge(acc_free[tile % 2], tidx(sec, tile, it, tper))
                n = len(chunks)
                for i, c in enumerate(chunks):
                    if chunk_wait:
                        chunk_wait(c)
                    w = slice((w0 + i) * 128, (w0 + i + 1) * 128)
                    for q, (wt, xx) in enumerate(((whi, xh), (whi, xl), (wlo, xh))):
                        for b in range(2):
                            mm = pe.matmul(acc[tile % 2][:, b, 0:HT], wt[slot][:, w],
                                           xx[:, c, b * HT:(b + 1) * HT],
                                           start=first and i == 0 and q == 0,
                                           stop=last and i == n - 1 and q == 2)
                if last or len(chunks) == FC // 2:
                    mm.then_inc(part_done, 1)

            C8 = range(DC)
            pe.wait_ge(ident_loaded, 16)
            pe.wait_ge(x_loaded[4], 16)
            for j in range(DC):
                mm = pe.transpose(mb[:, j * 8:j * 8 + 8], xtok[0:NS, 4, j * 128:(j + 1) * 128],
                                  ident[0:NS, 0:NS])
            mm.then_inc(misc_full, 1)
            for n in range(2 * NCH):
                i = n // 2
                pe.wait_ge(x_loaded[i], 16)
                pe.wait_ge(lv_free[n % 2], n // 2)
                for q in range(4):
                    j = 4 * (n % 2) + q
                    mm = pe.transpose(level(n)[:, q * 128:(q + 1) * 128], xtok[:, i, j * 128:(j + 1) * 128], ident)
                mm.then_inc(lv_full, 1)
            pe.wait_ge(vec_loaded, 16 * 9)
            pe.wait_ge(misc_free, 1)
            pe.transpose(mb[:, 0:48], vrow[0:48, 0, :], ident[0:48, 0:48])
            pe.transpose(mb[:, 48:136], vrow[0:88, 1, :], ident[0:88, 0:88]).then_inc(misc_full, 1)
            pe.wait_ge(x_diag, 5)
            for b in range(2):
                pe.wait_ge(lv_free[b], 4)
            for j in range(DC):
                if j == 5:
                    pe.wait_ge(misc_free, 2)
                    for q in range(DC):
                        mm = pe.matmul(mb[:, q * 8:q * 8 + 8], xtok[0:NS, 4, q * 128:(q + 1) * 128],
                                       dg[0:NS, 4, 0:NS], start=True, stop=True)
                    mm.then_inc(misc_full, 1)
                if j >= 5:
                    pe.wait_ge(xa_lo, j - 5 + 1)
                for i in range(NCH):
                    mm = pe.matmul(x_bank(j)[:, i * 128:(i + 1) * 128], xtok[:, i, j * 128:(j + 1) * 128],
                                   dg[:, i, :], start=True, stop=True)
                mm.then_inc(x_tile, 1)

            pe.sem_inc(v_full, 1)
            def v_transposes():
                for i in range(NCH):
                    mm = pe.transpose(lvb[:, 0, i * 128:(i + 1) * 128], hiT[:, i * 128:(i + 1) * 128], ident)
                mm.then_inc(v_full, 1)
                pe.transpose(lvb[0:NS, 1, 0:128], hiT[:, NT:TT], ident).then_inc(v_full, 1)

            with pe.Fori(0, 2) as it:
                for k in range(4):
                    product("A", k, it, k % 2, k, C8, 0, xah, xal,
                            chunk_wait=(lambda c: pe.wait_ge(xa_lo, max(c + 2, 6))) if k == 0 else None)
            with pe.Fori(0, 2) as it:
                for k in range(4):
                    product("V", k, it, k % 2, k, C8, 0, xah, xal)
                    if k % 2:
                        pe.wait_ge(acc_free[0], tidx("V", k - 1, it) + 1)
                        pe.wait_ge(v_taken, it * 4 + k)
                        v_transposes()

            def head(t, h, cols=slice(None)):
                return t[64 * (h % 2):64 * (h % 2) + 64, h // 2, cols]

            def scores(use, it):
                levels = [l for l in (2 * use, 2 * use + 1) if l < LV]
                pe.wait_ge(zq_ready, it * LV + (levels[-1] + 1))
                pe.wait_ge(merged, it * MERGES + (2 * use + 1))
                taken()
                if use == 3:
                    for c in range(4):
                        pe.matmul(lvb[:, 1, 2 * c:2 + 2 * c], qk[:, c, :], headsel, start=True, stop=True)
                for l in levels:
                    for c in range(4):
                        mm = pe.matmul(lvb[:, l % 2, c * 128:(c + 1) * 128], lk[l % 4][:, c, :],
                                       zq[l % 4][:, c].rearrange("k two t -> k (two t)"), start=True, stop=True)
                    mm.then_inc(sc_full, 1)

            def halves(k, it, between):
                product("B", k, it, k % 2, k, range(4), 0, xah, xal, last=False)
                between()
                product("B", k, it, k % 2, k, range(4, 8), 4, xah, xal, first=False, wait_unit=False)

            with pe.Fori(0, 4) as it:
                step.loop(it, 1)

                def first_scores():
                    pe.wait_ge(v_taken, it * 2 + 9)
                    scores(0, it)

                halves(0, it, first_scores)
                scores(1, it)
                pe.wait_ge(smp_staged, it + 1)
                wait_misc(M_B, 0, it, 6)
                pe.transpose(mb[0:NS, 0:128], ks8[:], ident).then_inc(misc_full, 1)

                halves(1, it, lambda: scores(2, it))
                scores(3, it)
                pe.wait_ge(prep, it * 8 + 8)
                wait_misc(M_B, 1, it, 6)
                for c in range(4):
                    mm = pe.transpose(mb[:, c * 128:(c + 1) * 128], lk[3][:, c, :], ident)
                mm.then_inc(misc_full, 1)

                def sample_outer():
                    pe.wait_ge(outer_ready, it + 1)
                    wait_misc(M_B, 2, it, 6)
                    taken()
                    for h2 in range(2):
                        mm = pe.matmul(mb[64 * h2:64 * h2 + 64, :], k8[:, 64 * h2:64 * h2 + 64],
                                       vblk[:, 512 * h2:512 * h2 + 512], start=True, stop=True)
                    mm.then_inc(misc_full, 1)

                halves(2, it, sample_outer)
                pe.wait_ge(merged, it * MERGES + (MERGES + 1))
                pe.wait_ge(vst_ready, it + 1)
                pe.wait_ge(o_free, it + 1)
                wait_misc(M_B, 3, it, 6)
                for h in range(8):
                    out = ob[64 * (h % 2):64 * (h % 2) + 64, (h // 2) * 128:(h // 2 + 1) * 128]
                    pe.matmul(out, vst[:, h * 64:(h + 1) * 64], sfull[:, h, :], start=True, stop=False)
                    mm = pe.matmul(out, head(sst, h), head(lq[3], h), start=False, stop=True)
                mm.then_inc(o_ready, 1)
                for h in range(8):
                    mm = pe.matmul(mb[64 * (h % 2):64 * (h % 2) + 64, (h // 2) * 64:(h // 2 + 1) * 64],
                                   khat[:, h * 64:(h + 1) * 64], vst[:, h * 64:(h + 1) * 64],
                                   start=True, stop=True)
                mm.then_inc(misc_full, 1)

                def head_squares():
                    pe.wait_ge(sq_ready, it + 1)
                    wait_misc(M_B, 4, it, 6)
                    pe.matmul(mb[:], blk64, sq[:], start=True, stop=True).then_inc(misc_full, 1)
                    pe.wait_ge(acc_free[0], tidx("B", 2, it) + 1)
                    v_transposes()

                halves(3, it, head_squares)
                wait_misc(M_B, 5, it, 6)
                taken()
                for h2 in range(2):
                    for b in range(NS):
                        mm = pe.matmul(mb[64 * h2:64 * h2 + 64, b:b + 1], ss[64 * h2:64 * h2 + 64, b, :],
                                       qs8[64 * h2:64 * h2 + 64, b:b + 1], start=True, stop=True)
                    if h2 == 0:
                        step(mm)
                mm.then_inc(misc_full, 1)
            step.end(4)
            pe.wait_ge(v_taken, 17)

            with pe.Fori(0, 4) as it:
                product("C", 0, it, 0, 0, C8, 0, xah, xal)
                pe.wait_ge(staged, it * 2 + 1)
                pe.wait_ge(vst_ready, it + 5)
                wait_level(L_C, 0, it, 4)
                for h in range(4):
                    mm = pe.matmul(level(0)[:, h * 128:(h + 1) * 128], kst[:, h, :], qst[:, h, :],
                                   start=True, stop=True)
                mm.then_inc(lv_full, 1)
                wait_level(L_C, 1, it, 4)
                for h in range(4):
                    mm = pe.transpose(level(1)[:, h * 128:(h + 1) * 128], kst[:, h, :], ident)
                mm.then_inc(lv_full, 1)
                pe.wait_ge(smp_staged, it + 5)
                wait_misc(M_C, 0, it, 5)
                pe.transpose(mb[0:NS, 0:128], ks8[:], ident).then_inc(misc_full, 1)

                product("C", 1, it, 1, 1, C8, 0, xah, xal)
                for b in range(2):
                    pe.wait_ge(lv_free[b], it * 2 + L_C // 2 + 1)
                pe.wait_ge(o_free, it + 5)
                pe.wait_ge(staged, it * 2 + 2)
                for h in range(4):
                    out = ob[:, h * 128:(h + 1) * 128]
                    pe.matmul(out, vst[:, h * 128:(h + 1) * 128], prb[:, h, :], start=True, stop=False)
                    mm = pe.matmul(out, rst[:, h, :], qd[:, h, :], start=False, stop=True)
                mm.then_inc(ret_o, 1)
                wait_misc(M_C, 1, it, 5)
                for h in range(4):
                    mm = pe.matmul(mb[:, h * 128:(h + 1) * 128], ktk[:, h * 128:(h + 1) * 128],
                                   vst[:, h * 128:(h + 1) * 128], start=True, stop=True)
                mm.then_inc(misc_full, 1)
                pe.wait_ge(outer_ready, it + 5)
                for b in range(2):
                    wait_level(L_C, 2 + b, it, 4)
                    pe.matmul(level(b), k8[:], vblk[:, 512 * b:512 * b + 512],
                              start=True, stop=True).then_inc(lv_full, 1)

                product("C", 2, it, 0, 2, range(4), 0, xah, xal, last=False)
                pe.wait_ge(sq_ready, it + 5)
                wait_misc(M_C, 2, it, 5)
                pe.matmul(mb[:], ones128[:], sq[:], start=True, stop=True).then_inc(misc_full, 1)
                product("C", 2, it, 0, 2, range(4, 8), 4, xah, xal, first=False, wait_unit=False)
                wait_misc(M_C, 3, it, 5)
                for b in range(2):
                    pe.wait_ge(lv_free[b], it * 2 + L_C // 2 + 2)
                for b in range(NS):
                    mm = pe.matmul(mb[:, b:b + 1], rsm[:, b, :], qs8[:, b:b + 1], start=True, stop=True)
                mm.then_inc(misc_full, 1)

                product("C", 3, it, 1, 3, range(5), 0, xah, xal, last=False)
                pe.wait_ge(smp_sq, it + 1)
                wait_misc(M_C, 4, it, 5)
                pe.matmul(mb[:, 0:8], blk64, sqs[:, 0:8], start=True, stop=True)
                pe.matmul(mb[:, 8:16], ones128[:], sqs[:, 8:16], start=True, stop=True).then_inc(misc_full, 1)
                product("C", 3, it, 1, 3, range(5, 8), 5, xah, xal, first=False, wait_unit=False)

            pe.wait_ge(ah_lo, 17)
            with pe.Fori(0, 2) as it:
                for k in range(4):
                    product("D", k, it, k % 2, 2 * k, range(4), 0, ahh, ahl, tper=8)
                    product("D", k, it, k % 2, 2 * k + 1, range(4), 4, arh, arl, tper=8, wait_unit=False)

            pe.wait_ge(p_loaded, 32)
            for j in range(2):
                pe.transpose(ob[:, j * NS:(j + 1) * NS], ptok[0:NS, 4, j * 128:(j + 1) * 128], ident[0:NS, 0:NS])
                for i in range(NCH):
                    mm = pe.transpose(lvb[:, j, i * 128:(i + 1) * 128], ptok[:, i, j * 128:(j + 1) * 128], ident)
                mm.then_inc(p_full, 1)

            with pe.Fori(0, 2) as it:
                for k in range(4):
                    product("E", k, it, k % 2, k, C8, 0, xah, xal,
                            chunk_wait=(lambda c: pe.wait_ge(mix_lo, c + 2)) if k == 0 else None)

            def mean_square(n):
                pe.wait_ge(p_lo, 3)
                pe.wait_ge(ssq_ready, 8 * (n + 1) + 1)
                for b in range(2):
                    pe.wait_ge(lv_free[b], L_F // 2 + n)
                    pe.matmul(lvb[:, b, 0:HT], ones1024[:], ssq[:, b * HT:(b + 1) * HT],
                              start=True, stop=True).then_inc(lv_full, 1)

            pe.wait_ge(st_loaded, 16)
            wait_misc(M_F, 0, 0, 0)
            for j in range(FC):
                mm = pe.transpose(mb[:, j * 16:(j + 1) * 16], strow[:, j * 128:(j + 1) * 128],
                                  ident[0:16, 0:16])
            mm.then_inc(misc_full, 1)
            product("F", 0, 0, 0, 0, C8, 0, xbh, xbl, chunk_wait=lambda c: pe.wait_ge(xb_lo, c + 1))
            mean_square(0)
            for k in range(1, 4):
                product("F", k, 0, k % 2, k, C8, 0, xbh, xbl)
            with pe.Fori(1, 11) as it:
                for k in range(4):
                    product("F", k, it, k % 2, k, C8, 0, xbh, xbl)

            with pe.Fori(0, 4) as it:
                for k in range(4):
                    if k < 2:
                        pe.wait_ge(ac_lo, FC // (2 - k) + 1)
                    product("G", k, it, k % 2, k // 2, range(11 * (k % 2), 11 * (k % 2) + 11), 0, ach, acl,
                            first=k % 2 == 0, last=k % 2 == 1, tper=2)

            def wait_bank(n):
                pe.wait_ge(lv_free[n % 2], L_Y // 2 + n // 2)

            def y_tile(j, n):
                pe.wait_ge(y_ready, j + 1)
                pe.wait_ge(ys_taken, j // 4)
                pe.transpose(ob[0:NS, (j % 4) * 128:(j % 4 + 1) * 128], yT[:, j, NT:TT], ident)
                wait_bank(n)
                for i in range(NCH):
                    mm = pe.transpose(lvb[:, n % 2, i * 128:(i + 1) * 128], yT[:, j, i * 128:(i + 1) * 128], ident)
                mm.then_inc(lv_full, 1)

            for j in range(DC):
                it, k = j // 4, j % 4
                if j == 0:
                    def wait_tile(c):
                        if c == 6:
                            mean_square(1)
                        pe.wait_ge(xb_lo, 8 + c + 1)
                product("H", k, it, k % 2, 2 * k, C8, 0, xbh, xbl, tper=8,
                        chunk_wait=wait_tile if j == 0 else None)
                product("H", k, it, k % 2, 2 * k + 1, range(2), 8, pxh, pxl, tper=8, wait_unit=False)
                if j:
                    y_tile(j - 1, j - 1)
            pe.wait_ge(cs_ready, FC)
            for n in range(6):
                wait_bank(7 + n)
                for j in range(4 * n, min(4 * n + 4, FC)):
                    mm = pe.transpose(lvb[0:10, (7 + n) % 2, (j % 4) * 128:(j % 4 + 1) * 128], cs[:, j, :], ident)
                mm.then_inc(lv_full, 1)
            y_tile(7, 13)
            pe.wait_ge(ssq_ready, 25)
            wait_misc(M_G, 0, 0, 0)
            for i in range(5):
                n = 128 if i < 4 else NS
                mm = pe.matmul(mb[0:n, i:i + 1], ssq[:, i * 128:i * 128 + n], ones1024[:, 0:1],
                               start=True, stop=True)
            mm.then_inc(misc_full, 1)

        @block.scalar
        def _(act):
            step = Steps(act, act_s)
            act.sem_inc(ss_stored, 16)
            act.sem_inc(rsm_stored, 16)

            def taken():
                act.sem_inc(act_passed, 1)

            def hi(sec, k, it, size=None):
                act.wait_ge(raw_loaded[k % 2], it * 64 + 32 * ((SEC[sec][0] + k) // 2 + 1))
                n = size or SIZE[sec]
                act.activation(whi[k % 2][:, 0:n], raw[k % 2][:, 0:n], ACT.Copy).then_inc(hi_ready, 1)

            def done(sec, k, it, per=4):
                act.wait_ge(part_done, parts(sec, k, it, per) + 1)

            def ahead(sec, k, it, nxt=None):
                if k < 2:
                    hi(sec, k + 2, it)
                elif nxt is None:
                    hi(sec, k - 2, it + 1)
                else:
                    hi(nxt, k - 2, 0)

            act.dma_start(cst[:, 0:offs["cos"]], consts[:, 0:offs["cos"]]).then_inc(ident_loaded, 16)
            act.wait_ge(set_up, 4)
            for i in (4, 0, 1, 2, 3):
                n = 128 if i < 4 else NS
                act.wait_ge(x_loaded[i], 16)
                act.activation(xsq[0:n, i, :], xtok[0:n, i, :], ACT.Square,
                               accum_out=ssx[0:n, i:i + 1]).then_inc(x_sq, 1)
            act.wait_ge(x_sq, 5)
            step(act.activation(ssx[:, 0:5], ssx[:, 0:5], ACT.Sqrt, bias=eps[:], scale=1.0 / DM))
            act.dma_start(cst[:, offs["cos"]:], consts[:, offs["cos"]:]).then_inc(const_loaded, 16)
            act.dma_start(msk[:], masks).then_inc(const_loaded, 16)
            hi("A", 0, 0)
            hi("A", 1, 0)
            act.wait_ge(misc_free, 2)
            for j in range(DC):
                if j == 5:
                    act.wait_ge(misc_free, 3)
                    act.activation(xah[:, :, NT:TT], xsm[:], ACT.Copy).then_inc(xa_hi, 1)
                act.wait_ge(x_tile, j + 1)
                act.activation(xah[:, j, 0:NT], x_bank(j), ACT.Copy,
                               scale=vc[:, 8 + j:9 + j]).then_inc(xa_hi, 1)
            act.wait_ge(vec_ready, 1)
            act.activation(lbt[:, 1:3, :], lbt[:, 1:3, :], ACT.Exp).then_inc(lb_exp, 1)

            act.sem_inc(v_taken, 1)
            with act.Fori(0, 2) as it:
                for k in range(4):
                    done("A", k, it)
                    ahead("A", k, it)
                    if k % 2 == 0:
                        act.activation(two(sg[k // 2][:]), ps2(0), ACT.Sigmoid).then_inc(sig_ready, 1)
                    else:
                        act.wait_ge(f_done, it * 2 + (k // 2 + 1))
                        act.activation(two(sgf[:]), ps2(1), ACT.Sigmoid).then_inc(acc_free[1], 1)
            with act.Fori(0, 2) as it:
                for k in range(4):
                    done("V", k, it)
                    ahead("V", k, it)
                    if k % 2 == 0:
                        act.wait_ge(v_full, it * 4 + (k + 1))
                        act.activation(two(hiT[:]), ps2(0), ACT.Copy).then_inc(acc_free[0], 1)
                    else:
                        act.activation(two(sg[1][:]), ps2(1), ACT.Sigmoid).then_inc(sig_ready, 1)
                        act.wait_ge(v_full, it * 4 + (k + 1))
                        taken()
                        cols = bass.ds(it * 256 + 128 * (k // 2), 128)
                        act.activation(vhg[:, :, cols], m4(lvb[:, 0, :]), ACT.Copy).then_inc(v_taken, 1)
                        act.wait_ge(v_full, it * 4 + (k + 2))
                        taken()
                        act.activation(v8h[:, cols], lvb[0:NS, 1, 0:128], ACT.Copy).then_inc(v_taken, 1)

            def chunk(t, c):
                return t[:, :, bass.ds(c * CH, CH)]

            def branch_hi(t, it, n):
                act.wait_ge(a_done, it + (n + 1))
                taken()
                act.activation(chunk(t, it), m4(ot[:]), ACT.Copy).then_inc(ah_hi, 1)

            def pad_queries(l, it):
                act.wait_ge(prep, it * 8 + (l + 1))
                if l >= 4:
                    act.wait_ge(sc_full, it * LV + (l - 3))
                taken()
                hb = 1 << l
                for p in range(2):
                    rows = slice(64 * p, 64 * p + 64)
                    src = lq[l % 4][rows].rearrange("k c (b two h) -> k c b two h", two=2, h=hb)[:, :, :, 1, :]
                    dst = zq[l % 4][rows, :, p, :].rearrange("k c (b h) -> k c b h", h=hb)
                    ins = act.activation(dst, src, ACT.Copy)
                ins.then_inc(zq_ready, 1)

            act.wait_ge(v_taken, 9)
            act.wait_ge(set_up, 8)
            with act.Fori(0, 4) as it:
                for l in range(4):
                    pad_queries(l, it)
                act.wait_ge(misc_full, it * 6 + (M_B - 2))
                taken()
                act.activation(vst[:], vhg[:, it, :], ACT.Copy).then_inc(vst_ready, 1)
                act.wait_ge(ss_stored, it * 16 + 16)
                act.wait_ge(misc_full, it * 6 + M_B)
                taken()
                act.dma_start(ss[:], state_hgrn[0].rearrange("b (c two) k v -> (two k) c b v", two=2)[:, it])\
                    .then_inc(ss_loaded, 16)
                for k, scale in ((0, 1.0), (1, KSCALE)):
                    done("B", k, it)
                    ahead("B", k, it)
                    act.wait_ge(rot_done, it * 2 + (k + 1))
                    for a, b in ((0, 64), (64, 0)):
                        act.activation(two(xs[k][a:a + 64, :]), ps2(k, b, b + 64), ACT.Copy,
                                       scale=scale).then_inc(swapped, 1)
                    if k == 0:
                        act.wait_ge(misc_full, it * 6 + (M_B + 1))
                        act.activation(k8[:], mb[0:NS, 0:128], ACT.Copy).then_inc(misc_free, 1)
                        for l in range(4, LV):
                            pad_queries(l, it)
                    else:
                        act.wait_ge(misc_full, it * 6 + (M_B + 2))
                        act.activation(khat[:], mb[:], ACT.Copy).then_inc(misc_free, 1)
                done("B", 2, it)
                ahead("B", 2, it)
                act.wait_ge(v_full, it * 2 + 9)
                act.activation(two(hiT[:]), ps2(2), ACT.Copy).then_inc(acc_free[0], 1)
                act.wait_ge(misc_free, it * 6 + (M_B + 3))
                taken()
                act.dma_start(hg_sample[0].rearrange("b (c two) k v -> (two k) c b v", two=2)[:, it], ss[:])\
                    .then_inc(ss_stored, 16)
                act.wait_ge(o_ready, it + 1)
                act.activation(sq[:], ob[:], ACT.Square).then_inc(sq_ready, 1)
                act.wait_ge(misc_full, it * 6 + (M_B + 5))
                act.activation(rs[:], mb[:], ACT.Sqrt, bias=eps[:]).then_inc(misc_free, 1)
                act.wait_ge(v_full, it * 2 + 10)
                taken()
                act.activation(vr[:, :, bass.ds(it * 128, 128)], m4(lvb[:, 0, :]), ACT.Copy).then_inc(v_taken, 1)
                act.wait_ge(v_full, it * 2 + 11)
                taken()
                act.activation(v8r[:, bass.ds(it * 128, 128)], lvb[0:NS, 1, 0:128], ACT.Copy).then_inc(v_taken, 1)
                done("B", 3, it)
                ahead("B", 3, it)
                act.activation(two(sg[1][:]), ps2(3), ACT.Sigmoid).then_inc(sig_ready, 1)
                branch_hi(ahh, it, 0)

            act.wait_ge(rot_done, 9)
            act.wait_ge(v_taken, 17)
            with act.Fori(0, 4) as it:
                act.wait_ge(misc_full, it * 5 + (M_C - 3))
                taken()
                act.activation(kst[:], chunk(kr, it), ACT.Copy)
                act.activation(vst[:], vr[:, it, :], ACT.Copy).then_inc(vst_ready, 1)
                act.wait_ge(rsm_stored, it * 16 + 16)
                act.wait_ge(misc_full, it * 5 + M_C)
                taken()
                act.dma_start(rsm[:], state_ret[0].rearrange("b h d v -> h d b v")[it]).then_inc(rsm_loaded, 16)
                for k in range(4):
                    if k == 3:
                        branch_hi(arh, it, 4)
                        act.wait_ge(misc_full, it * 5 + (M_C + 5))
                        act.activation(rss[:], mb[:, 0:16], ACT.Sqrt, bias=eps[:]).then_inc(misc_free, 1)
                        act.wait_ge(smp_done, it + 1)
                        taken()
                        for i, t in enumerate((ahh, arh)):
                            act.activation(t[:, it, NT:TT], smp[:, i], ACT.Copy).then_inc(smp_hi, 1)
                    done("C", k, it)
                    ahead("C", k, it)
                    act.activation(two(gab[:, it * 2 + (k // 2 + DC * (k % 2)), :]), ps2(k),
                                   ACT.Sigmoid).then_inc(acc_free[k % 2], 1)
                    if k == 0:
                        act.wait_ge(misc_full, it * 5 + (M_C + 1))
                        act.activation(k8[:], mb[0:NS, 0:128], ACT.Copy).then_inc(misc_free, 1)
                    if k == 1:
                        act.wait_ge(ret_o, it + 1)
                        act.activation(sq[:], ob[:], ACT.Square).then_inc(sq_ready, 1)
                        act.wait_ge(misc_full, it * 5 + (M_C + 3))
                        act.activation(rs[:], mb[:], ACT.Sqrt, bias=eps[:]).then_inc(misc_free, 1)
                        act.wait_ge(lv_free[1], it * 2 + (L_C // 2 + 2))
                        taken()
                        act.dma_start(ret_sample[0].rearrange("b h d v -> h d b v")[it], rsm[:])\
                            .then_inc(rsm_stored, 16)

            for h2 in range(2):
                act.dma_start(hg_prompt[0, 0].rearrange("(c two) k v -> two k c v", two=2)[h2],
                              sst[64 * h2:64 * h2 + 64]).then_inc(stored, 16)
            act.dma_start(ret_prompt[0, 0].rearrange("h d v -> d h v"), rst[:]).then_inc(stored, 16)
            act.wait_ge(stored, 48)
            act.wait_ge(rsm_stored, 80)
            act.wait_ge(xt_stored, 16)
            act.wait_ge(ah_lo, 17)
            act.dma_start(hT[:], xt_dram).then_inc(h_loaded, 16)

            with act.Fori(0, 2) as it:
                for k in range(4):
                    done("D", 2 * k + 1, it, 8)
                    ahead("D", k, it)
                    act.wait_ge(mix_sum, it * 4 + (k + 1))
                    taken()
                    act.activation(xah[:, it * 4 + k, :], m1[:], ACT.Copy).then_inc(mix_hi, 1)

            for j in range(2):
                act.wait_ge(p_full, j + 1)
                act.activation(pxh[:, j, 0:NT], lvb[:, j, :], ACT.Copy).then_inc(p_hi, 1)
            act.activation(pxh[:, :, NT:TT], ob[:, 0:2 * NS].rearrange("p (a b) -> p a b", a=2),
                           ACT.Copy).then_inc(p_hi, 1)

            act.dma_start(strow[:], state_conv[0].rearrange("b w n -> (b w) n")).then_inc(st_loaded, 16)

            def residual(sec, tile, it, per, gain):
                j = it * per + tile
                act.wait_ge(acc_free[tile % 2], tidx(sec, tile, it, per) + 1)
                taken()
                act.activation(xbh[:, j, :], hT[:, j, :], ACT.Copy,
                               scale=vc[:, bass.ds(j + gain, 1)]).then_inc(xb_hi, 1)

            def inverse_rms(n):
                act.wait_ge(lv_full, L_F + 2 * n + 2)
                for b in range(2):
                    act.activation(rstd[:, b * HT:(b + 1) * HT], lvb[:, b, 0:HT], ACT.Sqrt,
                                   bias=eps[:]).then_inc(lv_free[b], 1)

            with act.Fori(0, 2) as it:
                for k in range(4):
                    done("E", k, it)
                    ahead("E", k, it)
                    residual("E", k, it, 4, 16)

            act.wait_ge(misc_full, M_F + 1)
            act.activation(stT[:].rearrange("p a b -> p (a b)"), mb[:, 0:FC * 16], ACT.Copy).then_inc(misc_free, 1)
            inverse_rms(0)

            def ffn(it, nxt=None):
                for k in range(4):
                    done("F", k, it)
                    ahead("F", k, it, nxt)
                    if k % 2 == 0:
                        act.wait_ge(acc_free[0], tidx("F", k, it) + 1)
                        act.wait_ge(act_ready, it * 2 + (k // 2 + 1))
                        taken()
                        act.activation(cv[:, 0:NT], ab[k // 2][:, 0:NT], ACT.Identity,
                                       scale=vc[:, bass.ds(it * 2 + (48 + k // 2), 1)],
                                       bias=vc[:, bass.ds(it * 2 + (48 + 3 * FC + k // 2), 1)]).then_inc(c_first, 1)
                        act.wait_ge(c_ready, it * 2 + (k // 2 + 1))
                        act.activation(cv[:], cv[:], ACT.Gelu_apprx_tanh).then_inc(gelu_ready, 1)
                    else:
                        act.wait_ge(act_ready, it * 2 + (k // 2 + 2))
                        taken()
                        act.activation(ach[:, it * 2 + k // 2, :], gg[:], ACT.Copy).then_inc(ac_hi, 1)

            with act.Fori(0, 10) as it:
                ffn(it)
            ffn(10, "G")
            def down(it, nxt=None):
                for k in range(4):
                    done("G", k, it)
                    ahead("G", k, it, nxt)
                    if k % 2:
                        residual("G", k // 2, it, 2, 24)

            with act.Fori(0, 3) as it:
                down(it)
            down(3, "H")
            inverse_rms(1)

            def y_copy(j, n):
                act.wait_ge(lv_full, L_Y + n + 1)
                act.activation(ytok[:, 0:NCH, j * 128:(j + 1) * 128], m4(lvb[:, 0, :]), ACT.Copy)\
                    .then_inc(lv_free[0], 1)

            for j in range(DC):
                it, k = j // 4, j % 4
                done("H", 2 * k, it, 8)
                act.wait_ge(acc_free[0], tidx("H", 2 * k, it, 8) + 1)
                act.activation(sgg[:], tg[:], ACT.Sigmoid).then_inc(sig_ready, 1)
                done("H", 2 * k + 1, it, 8)
                if j < DC - 2:
                    ahead("H", k, it)
                act.wait_ge(h_new, j + 2)
                act.activation(yT[:, j, :], hT[:, j, :], ACT.Copy, scale=vc[:, 32 + j:33 + j]).then_inc(y_ready, 1)
                if j % 2:
                    y_copy(j - 1, j - 1)
            for n in range(1, 6, 2):
                w = 512 if n < 5 else 256
                act.wait_ge(lv_full, L_Y + 7 + n + 1)
                act.activation(csr[:, n * 512:n * 512 + w], lvb[0:10, 0, 0:w], ACT.Copy).then_inc(lv_free[0], 1)
            act.wait_ge(misc_full, M_G + 1)
            act.activation(rt[:, 0:4], mb[:, 0:4], ACT.Sqrt, bias=eps[:])
            act.activation(rt[0:NS, 4:5], mb[0:NS, 4:5], ACT.Sqrt, bias=eps[0:NS]).then_inc(misc_free, 1)
            act.wait_ge(rt_ready, 1)
            act.wait_ge(lv_free[0], L_Y // 2 + 7)
            act.wait_ge(lv_free[1], L_Y // 2 + 7)
            act.wait_ge(ys_taken, 2)
            for i in range(5):
                n = 128 if i < 4 else NS
                act.activation(ytok[0:n, i, 0:YSPLIT], ytok[0:n, i, 0:YSPLIT], ACT.Copy,
                               scale=rt[0:n, i:i + 1]).then_inc(y_scaled[0], 1)

        @block.vector
        def _(dve):
            def taken():
                dve.sem_inc(dve_passed, 1)

            step = Steps(dve, dve_s)
            dve.sem_inc(lo_ready, 2)
            for first in (*acc_free, rot_done, f_done, merged, o_free, ah_lo, mix_lo, ac_lo, h_new):
                dve.sem_inc(first, 1)

            def lo(sec, k, it):
                dve.wait_ge(hi_ready, unit(sec, k, it) + 1)
                n = SIZE[sec]
                dve.tensor_tensor(wlo[k % 2][:, 0:n], raw[k % 2][:, 0:n], whi[k % 2][:, 0:n].bitcast(fp),
                                  SUB).then_inc(lo_ready, 1)

            def done(sec, k, it, per=4):
                dve.wait_ge(part_done, parts(sec, k, it, per) + 1)

            def ahead(sec, k, it, nxt=None):
                if k < 2:
                    lo(sec, k + 2, it)
                elif nxt is None:
                    lo(sec, k - 2, it + 1)
                else:
                    lo(nxt, k - 2, 0)

            dve.wait_ge(misc_full, 1)
            dve.tensor_copy(xstg[:, :, NT:TT], mb[:, 0:64].rearrange("p (a b) -> p a b", b=NS)).then_inc(misc_free, 1)

            def x_copy(n):
                dve.wait_ge(lv_full, n + 1)
                h, i = n % 2, n // 2
                dve.tensor_copy(xstg[:, 4 * h:4 * h + 4, i * 128:(i + 1) * 128], m4(lvb[:, h, :])).then_inc(lv_free[h], 1)

            for n in range(6):
                x_copy(n)
            dve.wait_ge(act_s, 1)
            step(dve.reciprocal(ssx[:, 0:5], ssx[:, 0:5]))
            for i in (4, 0, 1, 2, 3):
                n = 128 if i < 4 else NS
                dve.tensor_scalar(dg[0:n, i, 0:n], ident[0:n, 0:n], ssx[0:n, i:i + 1], None, MUL).then_inc(x_diag, 1)
            x_copy(6)
            x_copy(7)
            dve.wait_ge(misc_full, 2)
            dve.tensor_copy(vc[:], mb[:, 0:136]).then_inc(misc_free, 1)
            dve.wait_ge(misc_free, 2)
            step(dve.tensor_tensor(lbt[:, 0, :], vc[:, 0:4], vc[:, 4:8], ALU.max))
            step(dve.tensor_tensor(lbt[:, 1, :], vc[:, 0:4], lbt[:, 0, :], SUB))
            dve.tensor_tensor(lbt[:, 2, :], vc[:, 4:8], lbt[:, 0, :], SUB).then_inc(vec_ready, 1)
            lo("A", 0, 0)
            lo("A", 1, 0)
            for j in range(DC):
                if j == 5:
                    dve.wait_ge(misc_full, 3)
                    dve.tensor_tensor(xsm[:], mb[:, 0:64].rearrange("p (a b) -> p a b", b=NS),
                                      vc[:, 8:16].unsqueeze(2).broadcast_to([128, DC, NS]), MUL).then_inc(misc_free, 1)
                    dve.wait_ge(xa_hi, 6)
                    dve.tensor_tensor(xal[:, :, NT:TT], xsm[:], xah[:, :, NT:TT].bitcast(fp), SUB).then_inc(xa_lo, 1)
                dve.wait_ge(xa_hi, j + (1 if j < 5 else 2))
                dve.scalar_tensor_tensor(xal[:, j, 0:NT], x_bank(j), vc[:, 8 + j:9 + j],
                                         xah[:, j, 0:NT].bitcast(fp), MUL, SUB).then_inc(xa_lo, 1)
            dve.wait_ge(lb_exp, 1)
            step(dve.tensor_tensor(lbt[:, 5, :], lbt[:, 1, :], lbt[:, 2, :], ADD))
            step(dve.reciprocal(lbt[:, 5, :], lbt[:, 5, :]))
            step(dve.tensor_tensor(lbt[:, 3, :], lbt[:, 1, :], lbt[:, 5, :], MUL))
            step(dve.tensor_scalar(lbt[:, 4, :], lbt[:, 3, :], -1.0, 1.0, MUL, ADD))

            with dve.Fori(0, 2) as it:
                for k in range(4):
                    done("A", k, it)
                    ahead("A", k, it)
                    j = it * 2 + k // 2
                    if k % 2 == 0:
                        dve.wait_ge(sig_ready, it * 2 + (k // 2 + 1))
                        dve.tensor_tensor(two(qT[:, j, :]), ps2(0), two(sg[k // 2][:]), MUL).then_inc(acc_free[0], 1)
                    else:
                        dve.wait_ge(acc_free[1], tidx("A", k, it) + 1)
                        dve.tensor_scalar(fT[:, j, :], sgf[:], lbt[:, 4, bass.ds(it * 2 + k // 2, 1)],
                                          lbt[:, 3, bass.ds(it * 2 + k // 2, 1)], MUL, ADD).then_inc(f_done, 1)
            with dve.Fori(0, 2) as it:
                for k in range(4):
                    done("V", k, it)
                    ahead("V", k, it)
                    if k % 2:
                        dve.wait_ge(sig_ready, it * 2 + (k // 2 + 5))
                        dve.scalar_tensor_tensor(two(ghg[:, it * 2 + k // 2, :]), ps2(1),
                                                 vc[:, bass.ds(it * 2 + (40 + k // 2), 1)],
                                                 two(sg[1][:]), MUL, MUL).then_inc(acc_free[1], 1)

            dve.wait_ge(const_loaded, 32)
            dve.wait_ge(xt_stored, 16)
            dve.wait_ge(set_up, 8)

            def merge(use, it):
                for n in (2 * use, 2 * use + 1):
                    dve.wait_ge(sc_full, it * LV + min(n + 1, LV))
                    dve.wait_ge(merged, it * MERGES + (n + 1))
                    taken()
                    if n == LV:
                        dve.copy_predicated(
                            sfull[:], ident.bitcast(u32).unsqueeze(1).broadcast_to([128, 8, CH]),
                            lvb[:, 1, 0:8].unsqueeze(2).broadcast_to([128, 8, CH])).then_inc(merged, 1)
                        continue
                    hb = 1 << n
                    dst = sfull[:].rearrange("s e (b two h) -> s e b two h", two=2, h=hb)
                    on = msk[:, n * 64:(n + 1) * 64].rearrange("s (b h) -> s b h", h=hb).unsqueeze(1)\
                        .broadcast_to([128, 8, 64 // hb, hb])
                    src = lvb[:, n % 2, :].rearrange("s (e b h) -> s e b h", e=8, h=hb)
                    dve.copy_predicated(dst[:, :, :, 1, :], on, src).then_inc(merged, 1)

            def rotate(dst, k, it):
                step(dve.tensor_tensor(xs[k][:], xs[k][:], sinT, MUL))
                dve.wait_ge(acc_free[k], tidx("B", k, it) + 1)
                dve.tensor_tensor(dst, dst, xs[k][:], ADD).then_inc(rot_done, 1)

            def chunk(t, c):
                return t[:, :, bass.ds(c * CH, CH)]

            def stage_samples(k, q, it, f):
                if f:
                    step(dve.tensor_copy(fs8[:], fT[:, it, NT:TT]))
                    dve.tensor_scalar(ks8[:], fs8[:], -1.0, 1.0, MUL, ADD)
                else:
                    dve.tensor_copy(ks8[:], k[:, it, NT:TT])
                dve.tensor_copy(qs8[:], q[:, it, NT:TT]).then_inc(smp_staged, 1)

            def gate_outputs(gate, it, n, per=1):
                step(dve.reciprocal(rs[:], rs[:]))
                dve.wait_ge(ah_lo, it * per + (n + 1))
                dve.tensor_tensor(ot[:], ob[:], rs[:], MUL).then_inc(o_free, 1)
                dve.wait_ge(o_free, it + (n + 2))
                dve.tensor_tensor(m4(ot[:]), m4(ot[:]), chunk(gate, it), MUL).then_inc(a_done, 1)

            def branch_lo(t_lo, t_hi, it, n):
                dve.wait_ge(ah_hi, it + (n + 1))
                dve.tensor_tensor(chunk(t_lo, it), m4(ot[:]), chunk(t_hi, it).bitcast(fp), SUB).then_inc(ah_lo, 1)

            with dve.Fori(0, 4) as it:
                step.loop(it, 6)
                dve.wait_ge(misc_free, it * 6 + M_B)
                stage_samples(None, qT, it, True)
                merge(0, it)
                merge(1, it)
                done("B", 0, it)
                ahead("B", 0, it)
                dve.wait_ge(swapped, it * 4 + 2)
                dve.tensor_tensor(two(qr[:, it, :]), ps2(0), two(cosT), MUL).then_inc(acc_free[0], 1)
                rotate(qr[:, it, :], 0, it)
                merge(2, it)

                done("B", 1, it)
                ahead("B", 1, it)
                dve.wait_ge(swapped, it * 4 + 4)
                dve.scalar_tensor_tensor(two(kr[:, it, :]), ps2(1), KSCALE, two(cosT), MUL,
                                         MUL).then_inc(acc_free[1], 1)
                merge(3, it)
                rotate(kr[:, it, :], 1, it)
                dve.wait_ge(ss_loaded, it * 16 + 16)
                step(dve.tensor_tensor(ss[:], ss[:], fs8[:].unsqueeze(2).broadcast_to([128, NS, 64]), MUL))
                dve.wait_ge(misc_full, it * 6 + (M_B + 3))
                dve.tensor_tensor(ss[:], ss[:], mb[:].rearrange("p (b v) -> p b v", b=NS),
                                  ADD).then_inc(misc_free, 1)

                done("B", 2, it)
                ahead("B", 2, it)
                dve.wait_ge(o_ready, it + 1)
                dve.wait_ge(prep, it * 8 + 8)
                step(dve.tensor_tensor(sst[:], sst[:], tl[LV][:].broadcast_to([128, 4, 64]), MUL))
                dve.wait_ge(misc_full, it * 6 + (M_B + 4))
                dve.tensor_tensor(sst[:], sst[:], mb[:, 0:256].rearrange("p (c v) -> p c v", c=4),
                                  ADD).then_inc(misc_free, 1)
                dve.wait_ge(misc_free, it * 6 + (M_B + 5))
                gate_outputs(ghg, it, 0)

                done("B", 3, it)
                ahead("B", 3, it)
                dve.wait_ge(sig_ready, it + 9)
                dve.scalar_tensor_tensor(two(grt[:, it, :]), ps2(3), vc[:, bass.ds(it + 44, 1)],
                                         two(sg[1][:]), MUL, MUL).then_inc(acc_free[1], 1)
                dve.wait_ge(misc_full, it * 6 + (M_B + 6))
                taken()
                dve.tensor_copy(qT[:, it, NT:TT], mb[:, 0:NS]).then_inc(misc_free, 1)
                branch_lo(ahl, ahh, it, 0)
            step.end(4)

            dve.wait_ge(misc_free, M_C)
            with dve.Fori(0, 4) as it:
                step.loop(it, 4)
                dve.wait_ge(misc_free, it * 5 + M_C)
                stage_samples(kr, qr, it, False)
                done("C", 0, it)
                dve.wait_ge(lv_full, it * 4 + (L_C + 1))
                dve.tensor_tensor(prb[:].rearrange("s h t -> s (h t)"), lvb[:, 0, :], decay,
                                  MUL).then_inc(lv_free[0], 1)
                dve.wait_ge(lv_full, it * 4 + (L_C + 2))
                dve.tensor_tensor(m4(ktk[:]), m4(lvb[:, 1, :]), kdec.unsqueeze(2).broadcast_to([128, 4, 128]),
                                  MUL).then_inc(lv_free[1], 1)
                ahead("C", 0, it)
                done("C", 1, it)
                ahead("C", 1, it)
                dve.wait_ge(ret_o, it + 1)
                step(dve.tensor_tensor(rst[:], rst[:], g128.unsqueeze(2).broadcast_to([128, 4, 128]), MUL))
                dve.wait_ge(misc_full, it * 5 + (M_C + 2))
                dve.tensor_tensor(rst[:], rst[:], m4(mb[:]), ADD).then_inc(misc_free, 1)
                dve.wait_ge(rsm_loaded, it * 16 + 16)
                for b in range(2):
                    dve.wait_ge(lv_full, it * 4 + (L_C + 3 + b))
                    part4 = rsm[:, 4 * b:4 * b + 4, :].rearrange("p b v -> p (b v)")
                    dve.scalar_tensor_tensor(part4, part4, gam[:, bass.ds(it, 1)], lvb[:, b, :], MUL,
                                             ADD).then_inc(lv_free[b], 1)
                dve.wait_ge(misc_free, it * 5 + (M_C + 3))
                gate_outputs(grt, it, 4, per=3)
                done("C", 2, it)
                ahead("C", 2, it)
                dve.wait_ge(misc_full, it * 5 + (M_C + 4))
                taken()
                dve.tensor_copy(qr[:, it, NT:TT], mb[:, 0:NS]).then_inc(misc_free, 1)
                dve.wait_ge(misc_free, it * 5 + (M_C + 4))
                taken()
                cols = qT[:, it, NT:TT], qr[:, it, NT:TT]
                dve.tensor_tensor(sqs[:, 0:8], cols[0], cols[0], MUL)
                dve.tensor_tensor(sqs[:, 8:16], cols[1], cols[1], MUL).then_inc(smp_sq, 1)
                branch_lo(arl, arh, it, 4)
                dve.wait_ge(misc_free, it * 5 + (M_C + 5))
                step(dve.reciprocal(rss[:], rss[:]))
                dve.tensor_tensor(rss[:, 0:8], rss[:, 0:8], ghg[:, it, NT:TT], MUL)
                step(dve.tensor_tensor(rss[:, 8:16], rss[:, 8:16], grt[:, it, NT:TT], MUL))
                taken()
                dve.tensor_tensor(smp[:, 0], cols[0], rss[:, 0:8], MUL)
                dve.tensor_tensor(smp[:, 1], cols[1], rss[:, 8:16], MUL).then_inc(smp_done, 1)
                for i, (t_lo, t_hi) in enumerate(((ahl, ahh), (arl, arh))):
                    dve.wait_ge(smp_hi, it * 2 + (i + 1))
                    taken()
                    dve.tensor_tensor(t_lo[:, it, NT:TT], smp[:, i], t_hi[:, it, NT:TT].bitcast(fp),
                                      SUB).then_inc(ah_lo, 1)
                done("C", 3, it)
                ahead("C", 3, it)
            step.end(4)

            with dve.Fori(0, 2) as it:
                for k in range(4):
                    done("D", 2 * k, it, 8)
                    dve.wait_ge(mix_lo, it * 4 + (k + 1))
                    dve.tensor_tensor(two(m1[:]), ps2(0), two(gab[:, it * 4 + k, :]), MUL).then_inc(acc_free[0], 1)
                    done("D", 2 * k + 1, it, 8)
                    dve.tensor_tensor(two(m2[:]), ps2(1), two(gab[:, it * 4 + (DC + k), :]),
                                      MUL).then_inc(acc_free[1], 1)
                    for b in range(2):
                        dve.wait_ge(acc_free[b], tidx("D", 2 * k + b, it, 8) + 1)
                    dve.tensor_tensor(m1[:], m1[:], m2[:], ADD).then_inc(mix_sum, 1)
                    ahead("D", k, it)
                    dve.wait_ge(mix_hi, it * 4 + (k + 1))
                    dve.tensor_tensor(xal[:, it * 4 + k, :], m1[:], xah[:, it * 4 + k, :].bitcast(fp),
                                      SUB).then_inc(mix_lo, 1)

            def residual(sec, tile, it, per, gain, n):
                j = it * per + tile
                dve.tensor_tensor(two(hT[:, j, :]), ps2(tile), two(hT[:, j, :]), ADD).then_inc(acc_free[tile % 2], 1)

                def low():
                    dve.wait_ge(xb_hi, it * per + (n + tile + 1))
                    dve.scalar_tensor_tensor(xbl[:, j, :], hT[:, j, :], vc[:, bass.ds(j + gain, 1)],
                                             xbh[:, j, :].bitcast(fp), MUL, SUB).then_inc(xb_lo, 1)
                return low

            for j in range(2):
                dve.wait_ge(p_hi, j + 1)
                dve.tensor_tensor(pxl[:, j, 0:NT], lvb[:, j, :], pxh[:, j, 0:NT].bitcast(fp), SUB).then_inc(p_lo, 1)
            dve.wait_ge(p_hi, 3)
            dve.tensor_tensor(pxl[:, :, NT:TT], ob[:, 0:2 * NS].rearrange("p (a b) -> p a b", a=2),
                              pxh[:, :, NT:TT].bitcast(fp), SUB).then_inc(p_lo, 1)

            dve.wait_ge(h_loaded, 16)
            with dve.Fori(0, 2) as it:
                for k in range(4):
                    done("E", k, it)
                    low = residual("E", k, it, 4, 16, 0)
                    ahead("E", k, it)
                    low()

            def inverse_rms(n):
                for b in range(2):
                    dve.wait_ge(lv_free[b], L_F // 2 + n + 1)
                step(dve.reciprocal(rstd[:], rstd[:]))

            dve.wait_ge(misc_free, M_F + 1)
            old = stT[:].rearrange("p j (b w) -> p j b w", w=2)

            def tap(i):
                return vc[:, 48 + FC * i:48 + FC * (i + 1)].unsqueeze(2).broadcast_to([128, FC, NS])

            tmp = gg[:, 0:FC * NS].rearrange("p (j b) -> p j b", b=NS)
            step(dve.tensor_tensor(part[:], old[:, :, :, 0], tap(0), MUL))
            step(dve.tensor_tensor(tmp, old[:, :, :, 1], tap(1), MUL))
            step(dve.tensor_tensor(part[:], part[:], tmp, ADD))
            step(dve.tensor_tensor(part[:], part[:], tap(3), ADD))
            for b in range(2):
                step(dve.memset(ab[b][:, 0:2], 0.0))
            inverse_rms(0)

            def ffn(it, nxt=None):
                for k in range(4):
                    done("F", k, it)
                    j = it * 2 + k // 2
                    if k % 2 == 0:
                        a = ab[k // 2]
                        dve.tensor_tensor(two(a[:, 2:TT + 2]), ps2(k), two(rstd[:]), MUL).then_inc(acc_free[0], 1)
                        ahead("F", k, it, nxt)
                        dve.wait_ge(c_first, it * 2 + (k // 2 + 1))
                        w1 = vc[:, bass.ds(it * 2 + (48 + FC + k // 2), 1)]
                        w2 = vc[:, bass.ds(it * 2 + (48 + 2 * FC + k // 2), 1)]
                        step(dve.scalar_tensor_tensor(cv[:, NT:TT], a[:, TT - 6:TT + 2], w2, part[:, j, :], MUL, ADD))
                        step(dve.scalar_tensor_tensor(cv[:, 0:NT], a[:, 1:NT + 1], w1, cv[:, 0:NT], MUL, ADD))
                        dve.scalar_tensor_tensor(cv[:, 0:NT], a[:, 2:NT + 2], w2, cv[:, 0:NT], MUL,
                                                 ADD).then_inc(c_ready, 1)
                    else:
                        dve.wait_ge(ac_lo, it * 2 + (k // 2 + 1))
                        dve.tensor_tensor(two(gg[:]), ps2(k), two(rstd[:]), MUL).then_inc(acc_free[1], 1)
                        ahead("F", k, it, nxt)
                        dve.wait_ge(ac_hi, it * 2 + (k // 2 + 1))
                        dve.tensor_tensor(acl[:, j, :], gg[:], ach[:, j, :].bitcast(fp), SUB).then_inc(ac_lo, 1)

            with dve.Fori(0, 10) as it:
                step.loop(it, 4)
                ffn(it)
            step.end(10)
            ffn(10, "G")

            def down(it, nxt=None):
                for k in range(4):
                    done("G", k, it)
                    if k % 2:
                        low = residual("G", k // 2, it, 2, 24, 8)
                    ahead("G", k, it, nxt)
                    if k % 2:
                        low()

            with dve.Fori(0, 3) as it:
                down(it)
            down(3, "H")
            inverse_rms(1)

            def y_copy(j, n):
                dve.wait_ge(lv_full, L_Y + n + 1)
                dve.tensor_copy(ytok[:, 0:NCH, j * 128:(j + 1) * 128], m4(lvb[:, 1, :])).then_inc(lv_free[1], 1)

            for j in range(DC):
                it, k = j // 4, j % 4
                done("H", 2 * k, it, 8)
                dve.tensor_tensor(two(tg[:]), ps2(0), two(rstd[:]), MUL).then_inc(acc_free[0], 1)
                done("H", 2 * k + 1, it, 8)
                dve.wait_ge(sig_ready, 12 + j + 1)
                dve.wait_ge(h_new, j + 1)
                dve.tensor_tensor(two(tp[:]), ps2(1), two(sgg[:]), MUL).then_inc(acc_free[1], 1)
                dve.wait_ge(acc_free[1], tidx("H", 2 * k + 1, it, 8) + 1)
                dve.tensor_tensor(hT[:, j, :], hT[:, j, :], tp[:], ADD).then_inc(h_new, 1)
                if j < DC - 2:
                    ahead("H", k, it)
                if j and j % 2 == 0:
                    y_copy(j - 1, j - 1)
                if j == 4:
                    dve.tensor_copy(ytok[0:NS, 4, 0:512], ob[0:NS, :]).then_inc(ys_taken, 1)
            for n in range(0, 6, 2):
                dve.wait_ge(lv_full, L_Y + 7 + n + 1)
                dve.tensor_copy(csr[:, n * 512:n * 512 + 512], lvb[0:10, 1, :]).then_inc(lv_free[1], 1)
            y_copy(7, 13)
            dve.tensor_copy(ytok[0:NS, 4, 512:1024], ob[0:NS, :]).then_inc(ys_taken, 1)
            dve.wait_ge(misc_free, M_G + 1)
            dve.reciprocal(rt[:, 0:4], rt[:, 0:4])
            dve.reciprocal(rt[0:NS, 4:5], rt[0:NS, 4:5]).then_inc(rt_ready, 1)
            dve.wait_ge(rt_ready, 1)
            dve.wait_ge(lv_free[0], L_Y // 2 + 7)
            dve.wait_ge(lv_free[1], L_Y // 2 + 7)
            dve.wait_ge(ys_taken, 2)
            for i in range(5):
                n = 128 if i < 4 else NS
                dve.tensor_scalar(ytok[0:n, i, YSPLIT:], ytok[0:n, i, YSPLIT:], rt[0:n, i:i + 1], None,
                                  MUL).then_inc(y_scaled[1], 1)

        @block.gpsimd
        def _(pool):
            def taken():
                pool.sem_inc(pool_passed, 1)

            step = Steps(pool, pool_s, taken)
            for first in (act_ready, ssq_ready):
                pool.sem_inc(first, 1)
            for t, v in ((ones128, 1.0 / 128), (ones1024, 1.0 / DM), (eps, EPS), (ssx, 1.0), (sst, 0.0), (rst, 0.0), (one, 1.0)):
                pool.memset(t[:], v).then_inc(set_up, 1)
            pool.wait_ge(const_loaded, 32)

            def chunk(t, c):
                return t[:, :, bass.ds(c * CH, CH)]

            def first_level(c):
                step(pool.tensor_tensor(lk[0][:], one[:].unsqueeze(2).broadcast_to([128, 4, CH]), chunk(fT, c), SUB))
                pool.tensor_tensor(lq[0][:], chunk(qT, c), chunk(fT, c), MUL)
                pool.tensor_tensor(qk[:], chunk(qT, c), lk[0][:], MUL).then_inc(prep, 1)

            def next_level(l, c=None):
                hb = 1 << (l - 1)

                def halves(t):
                    return t[:].rearrange("p c (b two h) -> p c b two h", two=2, h=hb)
                q0, q1, k0, k1 = (halves(t[i % 4]) for t in (lq, lk) for i in (l - 1, l))
                t0 = (chunk(fT, c) if l == 1 else tl[l - 1][:]).rearrange("p c (b two) -> p c b two", two=2)

                def pick(t, i):
                    t = t[:, :, :, i, :]
                    return t[:, :, :, 0] if hb == 1 else t.rearrange("p c b h -> p (c b) h")

                def decays(i):
                    if hb == 1:
                        return t0[:, :, :, i]
                    return t0.rearrange("p c b two -> p (c b) two")[:, :, i:i + 1]\
                        .broadcast_to([128, 4 * (CH // (2 * hb)), hb])
                pool.tensor_copy(pick(q1, 0), pick(q0, 0))
                pool.tensor_copy(pick(k1, 1), pick(k0, 1))
                pool.tensor_tensor(pick(q1, 1), pick(q0, 1), decays(0), MUL)
                pool.tensor_tensor(pick(k1, 0), pick(k0, 0), decays(1), MUL)
                pool.tensor_tensor(tl[l][:], t0[:, :, :, 0], t0[:, :, :, 1], MUL).then_inc(prep, 1)

            def outer_values(src, it, groups):
                g, w = groups, 128 // groups
                out = vblk[:].rearrange("p (g b v) -> p g b v", g=g, b=NS)
                v = src[:, bass.ds(it * 128, 128)].rearrange("p (g v) -> p g v", g=g).unsqueeze(2)\
                    .broadcast_to([NS, g, NS, w])
                d = ident[0:NS, 0:NS].unsqueeze(1).unsqueeze(3).broadcast_to([NS, g, NS, w])
                return pool.tensor_tensor(out, v, d, MUL)

            pool.wait_ge(acc_free[0], 5)
            pool.wait_ge(f_done, 5)
            pool.wait_ge(set_up, 7)
            for z in zq:
                pool.memset(z[:], 0.0)
            pool.memset(sfull[:], 0.0).then_inc(set_up, 1)
            first_level(0)
            for l in range(1, 4):
                pool.wait_ge(prep, l)
                next_level(l, 0)

            def hgrn(it, last=False):
                pool.wait_ge(v_taken, 9)
                pool.wait_ge(misc_free, it * 6 + M_B)
                taken()
                outer_values(v8h, it, 2).then_inc(outer_ready, 1)
                for l in range(4, LV + 1):
                    pool.wait_ge(prep, it * 8 + l)
                    pool.wait_ge(sc_full, it * LV + (l - 3))
                    taken()
                    next_level(l)
                if not last:
                    pool.wait_ge(sc_full, it * LV + LV)
                    taken()
                    first_level(it + 1)
                    for l in range(1, 4):
                        pool.wait_ge(prep, it * 8 + (8 + l))
                        if l == 3:
                            pool.wait_ge(o_ready, it + 1)
                        taken()
                        next_level(l, it + 1)

            with pool.Fori(0, 3) as it:
                step.loop(it, 1)
                hgrn(it)
            step.end(3)
            hgrn(3, last=True)

            pool.wait_ge(rot_done, 9)
            pool.wait_ge(v_taken, 17)
            with pool.Fori(0, 4) as it:
                pool.wait_ge(misc_free, it * 5 + M_C)
                taken()
                pool.tensor_copy(qst[:], chunk(qr, it)).then_inc(staged, 1)
                pool.wait_ge(staged, it * 2 + 1)
                taken()
                pool.tensor_tensor(qd[:], qst[:], m4(qdec), MUL).then_inc(staged, 1)
                outer_values(v8r, it, 1).then_inc(outer_ready, 1)

            def squares(j, n):
                pool.wait_ge(ssq_ready, j + (n + 1))
                taken()
                step(pool.tensor_tensor(sqt[:], hT[:, j, :], hT[:, j, :], MUL))
                pool.tensor_tensor(ssq[:], ssq[:], sqt[:], ADD).then_inc(ssq_ready, 1)

            pool.wait_ge(acc_free[0], tidx("E", 0, 0) + 1)
            step(pool.memset(ssq[:], 0.0))
            with pool.Fori(0, 2) as it:
                step.loop(it, 4)
                for k in range(4):
                    pool.wait_ge(acc_free[k % 2], tidx("E", k, it) + 1)
                    taken()
                    squares(it * 4 + k, 0)
            step.end(2)

            with pool.Fori(0, 11) as it:
                for k in range(2):
                    pool.wait_ge(acc_free[0], tidx("F", 2 * k, it) + 1)
                    taken()
                    pool.tensor_copy(cs[:, it * 2 + k, :], ab[k][:, NT:TT + 2]).then_inc(cs_ready, 1)
                    pool.wait_ge(acc_free[1], tidx("F", 2 * k + 1, it) + 1)
                    pool.wait_ge(gelu_ready, it * 2 + (k + 1))
                    pool.tensor_tensor(gg[:], gg[:], cv[:], MUL).then_inc(act_ready, 1)

            pool.wait_ge(acc_free[0], tidx("G", 0, 0, 2) + 1)
            step(pool.memset(ssq[:], 0.0))
            with pool.Fori(0, 4) as it:
                step.loop(it, 2)
                for k in range(2):
                    pool.wait_ge(acc_free[k], tidx("G", k, it, 2) + 1)
                    taken()
                    squares(it * 2 + k, 8)
            step.end(4)
            pool.wait_ge(h_new, 2)
            step(pool.memset(ssq[:], 0.0))
            with pool.Fori(0, 2) as it:
                step.loop(it, 4)
                for k in range(4):
                    pool.wait_ge(h_new, it * 4 + (k + 2))
                    taken()
                    squares(it * 4 + k, 16)
            step.end(2)


def shape_tables():
    import numpy as np
    f32 = np.float32
    gamma = 1.0 - 2.0 ** (-5.0 - np.arange(4))
    inv = (f32(10000.0) ** (-np.arange(0, 128, 2, dtype=f32) / f32(128))).astype(f32)
    pos = np.concatenate([np.arange(512, dtype=f32), np.full(8, 4096.0, f32)])
    ang = (pos[None, :] * inv[:, None]).astype(f32).astype(np.float64)
    t = np.arange(128)
    s_, t_ = t[:, None], t[None, :]
    tables = {
        "ident": np.eye(128),
        "blk64": (s_ // 64 == t_ // 64) / 64.0,
        "headsel": (s_ // 64 == np.arange(2)[None, :]) * 1.0,
        "cos": np.concatenate([np.cos(ang), np.cos(ang)]),
        "sin": np.concatenate([-np.sin(ang), np.sin(ang)]),
        "decay": np.concatenate([np.where(t_ >= s_, g ** np.maximum(t_ - s_, 0), 0.0) for g in gamma], 1),
        "qdec": np.concatenate([np.broadcast_to(g ** (t_ + 1.0), (128, 128)) for g in gamma], 1),
        "kdec": gamma[None, :] ** (127.0 - s_),
        "g128": np.broadcast_to(gamma ** 128.0, (128, 4)),
        "gam": np.broadcast_to(gamma, (128, 4)),
    }
    offs, at = {}, 0
    for n, a in tables.items():
        offs[n] = at
        at += a.shape[1]
    masks = []
    for l in range(7):
        h = 1 << l
        second = t[(t // h) % 2 == 1]
        masks.append(((s_ // (2 * h) == second[None, :] // (2 * h)) & ((s_ // h) % 2 == 0)).astype(np.uint32))
    return (np.ascontiguousarray(np.concatenate(list(tables.values()), 1), dtype=f32), offs,
            np.ascontiguousarray(np.concatenate(masks, 1)))


_INS = ["x_prompt", "x_sample", "state_hgrn", "state_ret", "state_conv", "p_prompt", "p_sample", "lb_logits",
        "w_in", "g_mix", "g_hg_out", "g_ret_out", "w_br_hg", "w_br_ret", "w_out", "g_ffn", "w_up", "conv_w",
        "conv_b", "w_down", "g_ple", "w_ple", "w_ple_gate", "g_final"]
_OUTS = [(1, 512, 1024), (8, 1, 1024), (1, 1, 8, 64, 64), (1, 1, 4, 128, 128), (1, 1, 2, 2816),
         (1, 8, 8, 64, 64), (1, 8, 4, 128, 128), (1, 8, 2, 2816)]


def kernel(**inputs):
    import numpy as _np
    import concourse.bacc as _bacc
    from concourse import mybir as _mybir
    from concourse.bass_utils import run_bass_kernel_spmd as _run

    nc = _bacc.Bacc("TRN2", target_bir_lowering=False, num_devices=1)
    consts, offs, masks = shape_tables()
    arrays, args = {}, []
    for name in _INS:
        arrays[f"in_{name}"] = _np.ascontiguousarray(inputs[name])
    arrays["consts"], arrays["masks"] = consts, masks
    for name, a in arrays.items():
        args.append(nc.dram_tensor(name, a.shape, _mybir.dt.from_np(a.dtype), kind="ExternalInput").ap())
    for i, shape in enumerate(_OUTS):
        args.append(nc.dram_tensor(f"out_{i}", shape, _mybir.dt.float32, kind="ExternalOutput").ap())
    hybrid_layer(nc, *args, offs=offs)
    r = _run(nc, [arrays], core_ids=[0])
    return tuple(r.results[0][f"out_{i}"] for i in range(len(_OUTS)))
```
